# Optimizing a Trainium2 kernel written in Bass

```python
import math
import jax
import jax.numpy as jnp
from jax import lax
import numpy as np

D_MODEL = 1024
BATCH = 1
SEQ = 1024
DEPTH = 2
DEC_BATCH = 1
DEC_SEQ = 64
PAST_LEN = 2048

CHUNK = 64
N_EVEN = (DEPTH + 1) // 2
N_ODD = DEPTH // 2
HEAD_DIM = 64
Q_BLOCK = 128
LN_EPS = 1e-5
ALPHA = (2 * DEPTH) ** 0.25
BETA = (8 * DEPTH) ** -0.25
D_FF = 4 * D_MODEL
A_HEADS = 8
A_KV_HEADS = 2
A_GROUP = A_HEADS // A_KV_HEADS
WINDOW = 128
WIN_CHUNKS = WINDOW // CHUNK
B_HEADS = 8
B_WIDTH = B_HEADS * HEAD_DIM
W_LORA = 64
A_LORA = 64
G_LORA = 128
B_COLS = 3 * B_WIDTH + W_LORA + A_LORA + G_LORA
RWKV_GN_EPS = 64e-5
C_HEADS = 4
C_VDIM = 2 * HEAD_DIM
C_WIDTH = C_HEADS * C_VDIM
D_HEADS = 8
D_KV_HEADS = 2
D_GROUP = D_HEADS // D_KV_HEADS
IDX_HEADS = 8
IDX_DIM = 64
TOPK_MAX = 256

EVEN_SPLIT = [A_HEADS * HEAD_DIM, A_KV_HEADS * HEAD_DIM, A_KV_HEADS * HEAD_DIM, B_COLS]
ODD_SPLIT = [C_HEADS * 2 * HEAD_DIM, C_HEADS * 2 * HEAD_DIM, C_WIDTH,
             D_HEADS * HEAD_DIM, D_KV_HEADS * HEAD_DIM, D_KV_HEADS * HEAD_DIM,
             IDX_HEADS * IDX_DIM, IDX_DIM, IDX_HEADS]
COLS_E = sum(EVEN_SPLIT)
COLS_O = sum(ODD_SPLIT)
D_MIX_E = A_HEADS * HEAD_DIM + B_WIDTH
D_MIX_O = C_WIDTH + D_HEADS * HEAD_DIM

kernel_name = 'chunk_streaming_hybrid_encoder_step'

def split_cols(p, sizes):
    offs = [int(o) for o in np.cumsum(sizes)[:-1]]
    return jnp.split(p, offs, axis=-1)

def alibi_slopes(n):
    return jnp.asarray(2.0 ** (-8.0 * np.arange(1, n + 1) / n), dtype=jnp.float32)

def layer_norm(x, g, b):
    xf = x.astype(jnp.float32)
    mu = jnp.mean(xf, -1, keepdims=True)
    var = jnp.mean(jnp.square(xf - mu), -1, keepdims=True)
    return ((xf - mu) * lax.rsqrt(var + LN_EPS) * g + b).astype(x.dtype)

def softmax_with_sink(logits, sink):
    m = jnp.maximum(jnp.max(logits, -1, keepdims=True), sink)
    p = jnp.exp(logits - m)
    return p / (jnp.sum(p, -1, keepdims=True) + jnp.exp(sink - m))

def swa_sink_prompt(q, k, v, sink):
    B, S = q.shape[:2]
    nc = S // CHUNK
    pad = WIN_CHUNKS * CHUNK
    span = (WIN_CHUNKS + 1) * CHUNK

    def band(t):
        tp = jnp.pad(t, ((0, 0), (pad, 0), (0, 0), (0, 0))).reshape(B, nc + WIN_CHUNKS, CHUNK, A_KV_HEADS, HEAD_DIM)
        return jnp.concatenate([tp[:, j:j + nc] for j in range(WIN_CHUNKS + 1)], axis=2)

    kb, vb = band(k), band(v)
    qb = q.reshape(B, nc, CHUNK, A_KV_HEADS, A_GROUP, HEAD_DIM)
    s = jnp.einsum('bnqkgd,bnskd->bnkgqs', qb, kb).astype(jnp.float32) * HEAD_DIM ** -0.5
    qpos = jnp.arange(S).reshape(nc, CHUNK)
    kpos = jnp.arange(nc)[:, None] * CHUNK - pad + jnp.arange(span)[None, :]
    dist = jnp.abs(qpos[:, :, None] - kpos[:, None, :]).astype(jnp.float32)
    slopes = alibi_slopes(A_HEADS).reshape(A_KV_HEADS, A_GROUP)
    logits = s - slopes[None, None, :, :, None, None] * dist[None, :, None, None]
    logits = jnp.where((kpos >= 0)[None, :, None, None, None, :], logits, -jnp.inf)
    sk = sink.astype(jnp.float32).reshape(A_KV_HEADS, A_GROUP)[None, None, :, :, None, None]
    p = softmax_with_sink(logits, sk)
    o = jnp.einsum('bnkgqs,bnskd->bnqkgd', p.astype(v.dtype), vb)
    return o.reshape(B, S, A_HEADS * HEAD_DIM)

def swa_sink_step(q, k_all, v_all, sink):
    B, T = q.shape[:2]
    L = k_all.shape[1]
    qg = q.reshape(B, T, A_KV_HEADS, A_GROUP, HEAD_DIM)
    s = jnp.einsum('bqkgd,bskd->bkgqs', qg, k_all).astype(jnp.float32) * HEAD_DIM ** -0.5
    qpos = PAST_LEN + jnp.arange(T)
    kpos = PAST_LEN - WINDOW + jnp.arange(L)
    dist = jnp.abs(qpos[:, None] - kpos[None, :]).astype(jnp.float32)
    slopes = alibi_slopes(A_HEADS).reshape(A_KV_HEADS, A_GROUP)
    logits = s - slopes[None, :, :, None, None] * dist
    sk = sink.astype(jnp.float32).reshape(A_KV_HEADS, A_GROUP)[None, :, :, None, None]
    p = softmax_with_sink(logits, sk)
    o = jnp.einsum('bkgqs,bskd->bqkgd', p.astype(v_all.dtype), v_all)
    return o.reshape(B, T, A_HEADS * HEAD_DIM)

def rwkv7(pb, shift_prev, S0, mu, w0, w_up, a0, a_up, g_up, k_k, k_a, r_k, lnx_g, lnx_b):
    B, T = pb.shape[:2]
    prev = jnp.concatenate([shift_prev.astype(pb.dtype), pb[:, :-1]], axis=1)
    xm = (pb + (prev - pb) * mu).astype(jnp.float32)
    r, k, v, wl, al, gl = split_cols(xm, [B_WIDTH, B_WIDTH, B_WIDTH, W_LORA, A_LORA, G_LORA])
    w_log = -jax.nn.softplus(-(w0 + jnp.tanh(wl) @ w_up)) - 0.5
    decay = jnp.exp(-jnp.exp(w_log))
    a = jax.nn.sigmoid(a0 + al @ a_up)
    g = jax.nn.sigmoid(gl) @ g_up
    heads = lambda t: t.reshape(B, T, B_HEADS, HEAD_DIM)
    kk = heads(k * k_k)
    kk = kk * lax.rsqrt(jnp.sum(kk * kk, -1, keepdims=True) + 1e-12)
    k = k * (1.0 + (a - 1.0) * k_a)
    r, k, v, decay, a = heads(r), heads(k), heads(v), heads(decay), heads(a)

    def step(S, inp):
        r_t, w_t, k_t, v_t, kk_t, a_t = inp
        sa = jnp.einsum('bhij,bhj->bhi', S, -kk_t)
        S = S * w_t[:, :, None, :] + sa[..., None] * (kk_t * a_t)[:, :, None, :] + v_t[..., None] * k_t[:, :, None, :]
        return S, jnp.einsum('bhij,bhj->bhi', S, r_t)

    seq = tuple(jnp.moveaxis(t, 1, 0) for t in (r, decay, k, v, kk, a))
    S_T, y = lax.scan(step, S0.astype(jnp.float32), seq)
    y = jnp.moveaxis(y, 0, 1)
    ym = jnp.mean(y, -1, keepdims=True)
    yv = jnp.mean(jnp.square(y - ym), -1, keepdims=True)
    y = ((y - ym) * lax.rsqrt(yv + RWKV_GN_EPS)).reshape(B, T, B_WIDTH) * lnx_g + lnx_b
    bonus = jnp.sum(r * k * r_k, -1, keepdims=True) * v
    y = (y + bonus.reshape(B, T, B_WIDTH)) * g
    return y.astype(pb.dtype), pb[:, -1:], S_T

def diff_attention(q, k, v, q_pos, lam, subln_g, lam_init):
    B, T = q.shape[:2]
    L = k.shape[1]
    qbs = min(Q_BLOCK, T)
    nb = T // qbs
    k_pos = jnp.arange(L)
    slopes = alibi_slopes(C_HEADS)

    def block(args):
        qb, pb = args
        s = jnp.einsum('bqhmd,bshmd->bhmqs', qb, k).astype(jnp.float32) * HEAD_DIM ** -0.5
        dist = jnp.abs(pb[:, None] - k_pos[None, :]).astype(jnp.float32)
        s = s - slopes[None, :, None, None, None] * dist
        allowed = (k_pos[None, :] // CHUNK) <= (pb[:, None] // CHUNK)
        p = jax.nn.softmax(jnp.where(allowed, s, -jnp.inf), axis=-1)
        attn = p[:, :, 0] - lam * p[:, :, 1]
        return jnp.einsum('bhqs,bshe->bqhe', attn.astype(v.dtype), v)

    qs = jnp.moveaxis(q.reshape(B, nb, qbs, C_HEADS, 2, HEAD_DIM), 1, 0)
    o = lax.map(block, (qs, q_pos.reshape(nb, qbs)))
    o = jnp.moveaxis(o, 0, 1).reshape(B, T, C_HEADS, C_VDIM).astype(jnp.float32)
    o = o * lax.rsqrt(jnp.mean(o * o, -1, keepdims=True) + LN_EPS) * subln_g * (1.0 - lam_init)
    return o.reshape(B, T, C_WIDTH).astype(q.dtype)

def dsa_attention(q, k, v, q_idx, k_idx, w_idx, q_pos):
    B, T = q.shape[:2]
    L = k.shape[1]
    n_sel = min(TOPK_MAX, L // 4)
    qbs = min(Q_BLOCK, T)
    nb = T // qbs
    k_pos = jnp.arange(L)
    slopes = alibi_slopes(D_HEADS).reshape(D_KV_HEADS, D_GROUP)
    gather = jax.vmap(lambda t, i: t[i])

    def block(args):
        qb, qib, wb, pb = args
        score = jnp.einsum('bqhd,bsd->bqhs', qib, k_idx).astype(jnp.float32) * IDX_DIM ** -0.5
        index = jnp.einsum('bqhs,bqh->bqs', jax.nn.relu(score), wb.astype(jnp.float32)) * IDX_HEADS ** -0.5
        allowed = (k_pos[None, :] // CHUNK) <= (pb[:, None] // CHUNK)
        index = jnp.where(allowed[None], index, -jnp.inf)
        top_val, top_idx = lax.top_k(index, n_sel)
        ks = gather(k, top_idx)
        vs = gather(v, top_idx)
        qg = qb.reshape(B, qbs, D_KV_HEADS, D_GROUP, HEAD_DIM)
        s = jnp.einsum('bqkgd,bqskd->bqkgs', qg, ks).astype(jnp.float32) * HEAD_DIM ** -0.5
        dist = jnp.abs(pb[None, :, None] - top_idx).astype(jnp.float32)
        s = s - slopes[None, None, :, :, None] * dist[:, :, None, None, :]
        s = jnp.where(jnp.isfinite(top_val)[:, :, None, None, :], s, -jnp.inf)
        p = jax.nn.softmax(s, axis=-1)
        o = jnp.einsum('bqkgs,bqskd->bqkgd', p.astype(v.dtype), vs)
        return o.reshape(B, qbs, D_HEADS * HEAD_DIM)

    blk = lambda t: jnp.moveaxis(t.reshape((B, nb, qbs) + t.shape[2:]), 1, 0)
    o = lax.map(block, (blk(q), blk(q_idx), blk(w_idx), q_pos.reshape(nb, qbs)))
    return jnp.moveaxis(o, 0, 1).reshape(B, T, D_HEADS * HEAD_DIM)

def even_mix(x, w_in, w_out, sink, rw, state=None):
    B, T = x.shape[:2]
    p = x @ w_in
    qa, ka, va, pb = split_cols(p, EVEN_SPLIT)
    qa = qa.reshape(B, T, A_HEADS, HEAD_DIM)
    ka = ka.reshape(B, T, A_KV_HEADS, HEAD_DIM)
    va = va.reshape(B, T, A_KV_HEADS, HEAD_DIM)
    if state is None:
        oa = swa_sink_prompt(qa, ka, va, sink)
        k_buf, v_buf = ka, va
        shift = jnp.zeros((B, 1, B_COLS), p.dtype)
        wkv = jnp.zeros((B, B_HEADS, HEAD_DIM, HEAD_DIM), jnp.float32)
    else:
        cache_k, cache_v, shift, wkv = state
        k_buf = jnp.concatenate([cache_k.astype(ka.dtype), ka], axis=1)
        v_buf = jnp.concatenate([cache_v.astype(va.dtype), va], axis=1)
        oa = swa_sink_step(qa, k_buf, v_buf, sink)
    ob, new_shift, new_wkv = rwkv7(pb, shift, wkv, *rw)
    mix = jnp.concatenate([oa, ob], axis=-1) @ w_out
    return mix, (k_buf[:, -WINDOW:], v_buf[:, -WINDOW:], new_shift, new_wkv)

def odd_mix(x, q_pos, w_in, w_out, lam_q1, lam_k1, lam_q2, lam_k2, subln_g, lam_init, state=None):
    B, T = x.shape[:2]
    p = x @ w_in
    qc, kc, vc, qd, kd, vd, qi, ki, wi = split_cols(p, ODD_SPLIT)
    qc = qc.reshape(B, T, C_HEADS, 2, HEAD_DIM)
    kc = kc.reshape(B, T, C_HEADS, 2, HEAD_DIM)
    vc = vc.reshape(B, T, C_HEADS, C_VDIM)
    qd = qd.reshape(B, T, D_HEADS, HEAD_DIM)
    kd = kd.reshape(B, T, D_KV_HEADS, HEAD_DIM)
    vd = vd.reshape(B, T, D_KV_HEADS, HEAD_DIM)
    qi = qi.reshape(B, T, IDX_HEADS, IDX_DIM)
    new_rows = (kc, vc, kd, vd, ki)
    if state is None:
        kc_all, vc_all, kd_all, vd_all, ki_all = new_rows
    else:
        kc_all, vc_all, kd_all, vd_all, ki_all = [
            jnp.concatenate([c.astype(n.dtype), n], axis=1) for c, n in zip(state, new_rows)]
    lam = (jnp.exp(jnp.sum(lam_q1.astype(jnp.float32) * lam_k1.astype(jnp.float32)))
           - jnp.exp(jnp.sum(lam_q2.astype(jnp.float32) * lam_k2.astype(jnp.float32))) + lam_init)
    oc = diff_attention(qc, kc_all, vc_all, q_pos, lam, subln_g, lam_init)
    od = dsa_attention(qd, kd_all, vd_all, qi, ki_all, wi, q_pos)
    mix = jnp.concatenate([oc, od], axis=-1) @ w_out
    return mix, new_rows

def residual_block(x, mix, g1, b1, g2, b2, w_up, w_down):
    x = layer_norm(ALPHA * x + mix, g1, b1)
    h = jnp.square(jax.nn.relu(x @ w_up)) @ w_down
    return layer_norm(ALPHA * x + h, g2, b2)

def stack_states(states):
    return [jnp.stack(z, axis=0) for z in zip(*states)]

def setup_inputs(seed: int = 0) -> dict:
    key = jax.random.key(seed)
    ks = iter(jax.random.split(key, 48))

    def nrm(shape, scale=1.0):
        return jax.random.normal(next(ks), shape, jnp.float32) * scale

    def unif(shape, lo, hi):
        return jax.random.uniform(next(ks), shape, jnp.float32, lo, hi)

    D = D_MODEL
    return {
        'x_prompt': nrm((BATCH, SEQ, D)),
        'x_sample': nrm((DEC_BATCH, DEC_SEQ, D)),
        'cache_a_k': nrm((N_EVEN, DEC_BATCH, WINDOW, A_KV_HEADS, HEAD_DIM)),
        'cache_a_v': nrm((N_EVEN, DEC_BATCH, WINDOW, A_KV_HEADS, HEAD_DIM)),
        'state_b_shift': nrm((N_EVEN, DEC_BATCH, 1, B_COLS)),
        'state_b_wkv': nrm((N_EVEN, DEC_BATCH, B_HEADS, HEAD_DIM, HEAD_DIM), 0.3),
        'cache_c_k': nrm((N_ODD, DEC_BATCH, PAST_LEN, C_HEADS, 2, HEAD_DIM)),
        'cache_c_v': nrm((N_ODD, DEC_BATCH, PAST_LEN, C_HEADS, C_VDIM)),
        'cache_d_k': nrm((N_ODD, DEC_BATCH, PAST_LEN, D_KV_HEADS, HEAD_DIM)),
        'cache_d_v': nrm((N_ODD, DEC_BATCH, PAST_LEN, D_KV_HEADS, HEAD_DIM)),
        'cache_d_kidx': nrm((N_ODD, DEC_BATCH, PAST_LEN, IDX_DIM)),
        'w_in_even': nrm((N_EVEN, D, COLS_E), D ** -0.5),
        'sink_a': nrm((N_EVEN, A_HEADS), 0.5),
        'mu_b': unif((N_EVEN, B_COLS), 0.0, 1.0),
        'w0_b': unif((N_EVEN, B_WIDTH), -4.0, 1.0),
        'w_up_b': nrm((N_EVEN, W_LORA, B_WIDTH), 0.5 * W_LORA ** -0.5),
        'a0_b': nrm((N_EVEN, B_WIDTH), 0.1),
        'a_up_b': nrm((N_EVEN, A_LORA, B_WIDTH), 0.5 * A_LORA ** -0.5),
        'g_up_b': nrm((N_EVEN, G_LORA, B_WIDTH), G_LORA ** -0.5),
        'k_k_b': 0.85 + nrm((N_EVEN, B_WIDTH), 0.05),
        'k_a_b': 1.0 + nrm((N_EVEN, B_WIDTH), 0.05),
        'r_k_b': nrm((N_EVEN, B_HEADS, HEAD_DIM), 0.1),
        'lnx_g_b': 1.0 + nrm((N_EVEN, B_WIDTH), 0.05),
        'lnx_b_b': nrm((N_EVEN, B_WIDTH), 0.02),
        'w_out_even': nrm((N_EVEN, D_MIX_E, D), BETA * D_MIX_E ** -0.5),
        'w_in_odd': nrm((N_ODD, D, COLS_O), D ** -0.5),
        'lam_q1_c': nrm((N_ODD, HEAD_DIM), 0.1),
        'lam_k1_c': nrm((N_ODD, HEAD_DIM), 0.1),
        'lam_q2_c': nrm((N_ODD, HEAD_DIM), 0.1),
        'lam_k2_c': nrm((N_ODD, HEAD_DIM), 0.1),
        'subln_g_c': 1.0 + nrm((N_ODD, C_VDIM), 0.05),
        'w_out_odd': nrm((N_ODD, D_MIX_O, D), BETA * D_MIX_O ** -0.5),
        'ln_mix_g': 1.0 + nrm((DEPTH, D), 0.05),
        'ln_mix_b': nrm((DEPTH, D), 0.02),
        'ln_ffn_g': 1.0 + nrm((DEPTH, D), 0.05),
        'ln_ffn_b': nrm((DEPTH, D), 0.02),
        'w_ff_up': nrm((DEPTH, D, D_FF), D ** -0.5),
        'w_ff_down': nrm((DEPTH, D_FF, D), BETA * D_FF ** -0.5),
    }

def reference(x_prompt, x_sample, cache_a_k, cache_a_v, state_b_shift, state_b_wkv,
              cache_c_k, cache_c_v, cache_d_k, cache_d_v, cache_d_kidx,
              w_in_even, sink_a, mu_b, w0_b, w_up_b, a0_b, a_up_b, g_up_b, k_k_b, k_a_b,
              r_k_b, lnx_g_b, lnx_b_b, w_out_even,
              w_in_odd, lam_q1_c, lam_k1_c, lam_q2_c, lam_k2_c, subln_g_c, w_out_odd,
              ln_mix_g, ln_mix_b, ln_ffn_g, ln_ffn_b, w_ff_up, w_ff_down):
    xp, xs = x_prompt, x_sample
    pos_p = jnp.arange(xp.shape[1])
    pos_s = PAST_LEN + jnp.arange(xs.shape[1])
    even_p, even_s, odd_p, odd_s = [], [], [], []
    for layer in range(DEPTH):
        i = layer // 2
        if layer % 2 == 0:
            rw = (mu_b[i], w0_b[i], w_up_b[i], a0_b[i], a_up_b[i], g_up_b[i],
                  k_k_b[i], k_a_b[i], r_k_b[i], lnx_g_b[i], lnx_b_b[i])
            mp, st_p = even_mix(xp, w_in_even[i], w_out_even[i], sink_a[i], rw)
            ms, st_s = even_mix(xs, w_in_even[i], w_out_even[i], sink_a[i], rw,
                                (cache_a_k[i], cache_a_v[i], state_b_shift[i], state_b_wkv[i]))
            even_p.append(st_p)
            even_s.append(st_s)
        else:
            lam_init = 0.8 - 0.6 * math.exp(-0.3 * layer)
            cp = (w_in_odd[i], w_out_odd[i], lam_q1_c[i], lam_k1_c[i], lam_q2_c[i], lam_k2_c[i],
                  subln_g_c[i], lam_init)
            mp, st_p = odd_mix(xp, pos_p, *cp)
            ms, st_s = odd_mix(xs, pos_s, *cp, state=(cache_c_k[i], cache_c_v[i], cache_d_k[i],
                                                      cache_d_v[i], cache_d_kidx[i]))
            odd_p.append(st_p)
            odd_s.append(st_s)
        ffn = (ln_mix_g[layer], ln_mix_b[layer], ln_ffn_g[layer], ln_ffn_b[layer],
               w_ff_up[layer], w_ff_down[layer])
        xp = residual_block(xp, mp, *ffn)
        xs = residual_block(xs, ms, *ffn)
    a_k_p, a_v_p, b_shift_p, b_wkv_p = stack_states(even_p)
    a_k_s, a_v_s, b_shift_s, b_wkv_s = stack_states(even_s)
    c_k_p, c_v_p, d_k_p, d_v_p, d_kidx_p = stack_states(odd_p)
    c_k_s, c_v_s, d_k_s, d_v_s, d_kidx_s = stack_states(odd_s)
    return (xp, xs, a_k_p, a_v_p, b_shift_p, b_wkv_p, c_k_p, c_v_p, d_k_p, d_v_p, d_kidx_p,
            a_k_s, a_v_s, b_shift_s, b_wkv_s, c_k_s, c_v_s, d_k_s, d_v_s, d_kidx_s)


_drawn_inputs = setup_inputs


def setup_inputs(seed=0):
    import zlib

    import numpy as np

    out = dict(_drawn_inputs(seed))
    spreads = {}
    factors = {'sink_a': 8.0,
     'lnx_g_b': 3.113,
     'lnx_b_b': 5.403,
     'lam_k1_c': 2.691,
     'lam_q2_c': 8.0,
     'subln_g_c': 6.956,
     'cache_d_k': 2.89}
    for name, (base, spread) in spreads.items():
        noise = np.random.default_rng([zlib.crc32(name.encode()), seed]).standard_normal(out[name].shape)
        drawn = base * np.exp(spread * noise) if base else spread * noise
        out[name] = jnp.asarray(drawn.astype(out[name].dtype))
    for name, factor in factors.items():
        out[name] = (out[name] * factor).astype(out[name].dtype)
    return out
```

```python
import math

import numpy as np
import concourse.bass as bass
from concourse import mybir

F32 = mybir.dt.float32
ALU = mybir.AluOpType
ACT = mybir.ActivationFunctionType
AX = mybir.AxisListType

D = 1024
KD = D // 128
TP = 1024
TS = 64
T = TP + TS
TB = T // 4
NQ = TP // 128
PAST = 2048
LS = PAST + TS
NPT = PAST // 128
CH = 64
HD = 64
NCHUNK = TP // CH
FF = 4096
ALPHA = 4 ** 0.25
LN_EPS = 1e-5
GN_EPS = 64e-5
DECAY = math.exp(-0.5)
LAM_INIT = 0.8 - 0.6 * math.exp(-0.3)
TOPK = 256
SCALE = HD ** -0.5
FAR = 1e30
TAKEN = -3e38

ROWS = {}
_at = 0
for _n, _c in (("mu", 14), ("w0", 4), ("a0", 4), ("kk", 4), ("ka", 4), ("rk", 4), ("lnxg", 4), ("lnxb", 4),
               ("mixg", 16), ("mixb", 16), ("ffng", 16), ("ffnb", 16), ("subln", 1), ("shift", 14)):
    ROWS[_n] = _at
    _at += _c
NROWS = _at

CONST = {}
_at = 0
for _n, _c in (("ident", 128), ("mean", 128), ("heads", 128), ("slopeC", 4), ("slopeD", 8), ("eps", 3),
               ("strict", 128), ("upto", 128), ("low1", 128), ("up1", 128), ("low2", 128), ("low4", 128),
               ("low8", 128), ("low16", 128), ("low32", 128), ("reset", T), ("distA", 256),
               ("distP", TP), ("distS", LS)):
    CONST[_n] = (_at, _c)
    _at += _c
NCONST = _at


def constants():
    c = np.zeros((128, NCONST), np.float32)

    def put(name, a):
        o, n = CONST[name]
        c[:, o:o + n] = a

    i = np.arange(128)
    p, q = i[:, None], i[None, :]
    same = (p // 64) == (q // 64)
    put("ident", p == q)
    put("mean", 1.0 / D)
    put("heads", same)
    put("slopeC", -2.0 ** (-8.0 * np.arange(1, 5) / 4)[None, :])
    put("slopeD", -2.0 ** (-8.0 * np.arange(1, 9) / 8)[None, :])
    put("eps", np.array([LN_EPS, 1e-12, GN_EPS])[None, :])
    put("strict", same & (p < q))
    put("upto", same & (p <= q))
    for n in (1, 2, 4, 8, 16, 32):
        low = (p // (2 * n) == q // (2 * n)) & (p // n > q // n)
        put(f"low{n}", low)
        if n == 1:
            put("up1", low.T)
    put("reset", (np.arange(T) % CH != 0)[None, :])
    x = np.arange(256)[None, :]
    dist = np.abs(p + 128 - x).astype(np.float64)
    put("distA", np.where(np.where(p < 64, x < 192, x >= 64), dist, FAR))
    x = np.arange(TP)[None, :]
    dist = np.abs(p + TP - 128 - x).astype(np.float64)
    put("distP", np.where((p < 64) & (x >= TP - 64), FAR, dist))
    x = np.arange(LS)[None, :]
    put("distS", np.abs(p + PAST - x))
    return c


class Steps:

    def __init__(self, nc, name, steps):
        self.sem, self.steps, self.at = nc.alloc_semaphore(name), list(steps), 0

    def step(self, name):
        assert self.steps[self.at % len(self.steps)] == name, (name, self.steps[self.at % len(self.steps)])
        self.at += 1
        return self.sem, 1

    def done(self, t, name):
        return t * len(self.steps) + self.steps.index(name) + 1

    def rounds(self, t):
        return t * len(self.steps)


def ds(start, n):
    return bass.ds(start, n) if not isinstance(start, int) else slice(start, start + n)


def repeat(engine, parts, body):
    for start, end in parts:
        if end - start == 1:
            body(start, start == 0)
        else:
            with engine.Fori(start, end) as i:
                body(i, False)


class Core:
    pass


def blocks4(ap):
    return ap.rearrange("p (b t) -> p b t", b=4)


def bank(m, b):
    return m.ps[:, b * 512:(b + 1) * 512]


def linear_out(m, buf):
    return m.ps[:, buf * 2048:(buf + 1) * 2048].rearrange("p (b t) -> p b t", b=4)[:, :, 0:TB]


def heads4(ap):
    return ap.rearrange("p (h c) -> p h c", h=4)


def linear(m, name, tiles, pieces, loads, ndma, parts, rhs, evacuate, on_vector=False):
    nc = m.nc
    per = 4 if pieces == 1 else 2
    rounds = tiles // per
    each = per * pieces // 4
    ring = m.arena[:, m.ring:m.ring + 4096].rearrange("p (s k c) -> p s k c", s=4, k=8)
    loaded = [nc.alloc_semaphore(f"{name}_loaded{s}") for s in range(4)]
    used = nc.alloc_semaphore(f"{name}_used")
    freed = nc.alloc_semaphore(f"{name}_freed")
    inner = nc.alloc_semaphore(f"{name}_inner")
    with nc.Block() as block:

        @block.sync
        def _(sp):
            def fill(i, first):
                for c in range(per * pieces):
                    if not first or c >= 4:
                        sp.wait_ge(used, i * per * pieces + c - 3)
                    for dst, src in loads(i, c // pieces, c % pieces, ring[:, c % 4]):
                        sp.dma_start(dst, src).then_inc(loaded[c % 4], 16)

            repeat(sp, parts, fill)

        @block.tensor
        def _(pe):
            def multiply(i, first):
                for u in range(per):
                    if not first or u >= 2:
                        pe.wait_ge(freed, i * per + u - 1)
                    for c in range(pieces):
                        g = u * pieces + c
                        pe.wait_ge(loaded[g % 4], (i * each + g // 4 + 1) * 16 * ndma)
                        for b in range(4):
                            at = (u % 2) * 2048 + b * 512
                            for k in range(8):
                                last = nc.tensor.matmul(
                                    m.ps[:, at:at + TB], ring[:, g % 4, k, :],
                                    rhs(c * 8 + k)[:, b * TB:(b + 1) * TB],
                                    start=(c == 0 and k == 0), stop=(c == pieces - 1 and k == 7),
                                    skip_group_check=True)
                        last.then_inc(used, 1)

            repeat(pe, [(0, 1), (1, rounds)], multiply)

        def leave(engine):
            def tile(i, first):
                for u in range(per):
                    engine.wait_ge(used, (i * per + u + 1) * pieces)
                    evacuate(engine, i * per + u, linear_out(m, u % 2), inner).then_inc(freed, 1)

            repeat(engine, [(0, 1), (1, rounds)], tile)

        if on_vector:
            block.vector(leave)
        else:
            block.scalar(leave)


def weight_view(w):
    return w.rearrange("(k p) c -> p k c", p=128)


def halves(slot, src):
    return [(slot[:, 0:4], src[:, 0:4]), (slot[:, 4:8], src[:, 4:8])]


def grouped_columns(slot, w, base, a):
    return [(slot[:, :, 64 * g:64 * g + 64], w[:, :, base + 256 * g + 64 * a:base + 256 * g + 64 * a + 64])
            for g in range(2)]


def project_even(m):
    w = weight_view(m.io["w_in_even"][0])

    def loads(i, u, c, slot):
        if isinstance(i, int) and i == 0:
            return grouped_columns(slot, w, 0, u)
        if isinstance(i, int):
            at = (512, 640, 2304, 2432)[u]
            return halves(slot, w[:, :, at:at + 128])
        return halves(slot, w[:, :, ds(i * 512 + (256 + 128 * u), 128)])

    def evacuate(act, tile, out, inner):
        return m.nc.scalar.activation(blocks4(tile_of(m.p, tile)), out, ACT.Copy)

    linear(m, "in0", 20, 1, loads, 2, [(0, 1), (1, 4), (4, 5)], lambda k: m.x[:, k, :], evacuate)


def tile_of(p, tile):
    if isinstance(tile, int):
        return p[:, tile, :]
    return p[:, ds(tile, 1), :].rearrange("p a t -> p (a t)")


def project_odd(m):
    w = weight_view(m.io["w_in_odd"][0])

    def loads(i, u, c, slot):
        if isinstance(i, int) and i == 3:
            return grouped_columns(slot, w, 1536, u)
        if isinstance(i, int) and i == 5:
            if u == 1:
                return [(slot[:, :, 0:64], w[:, :, 2816:2880]), (slot[:, :, 64:128], w[:, :, 2816:2880])]
            if u == 3:
                return halves(slot[:, :, 0:8], w[:, :, 2880:2888])
            at = {0: 2048, 2: 2176}[u]
            return halves(slot, w[:, :, at:at + 128])
        if isinstance(i, int) and i == 4:
            return halves(slot, w[:, :, 2304 + 128 * u:2304 + 128 * u + 128])
        return halves(slot, w[:, :, ds(i * 512 + 128 * u, 128)])

    def evacuate(act, tile, out, inner):
        return m.nc.scalar.activation(blocks4(tile_of(m.p, tile)), out, ACT.Copy)

    linear(m, "in1", 24, 1, loads, 2, [(0, 1), (1, 3), (3, 4), (4, 5), (5, 6)], lambda k: m.x[:, k, :],
           evacuate)


def add_residual(m):
    def evacuate(dve, tile, out, inner):
        x = blocks4(tile_of(m.x, tile))
        return m.nc.vector.scalar_tensor_tensor(out=x, in0=x, scalar=ALPHA, in1=out, op0=ALU.mult, op1=ALU.add)
    return evacuate


def project_out(m, name, w, mixed, grouped):
    rows = w.rearrange("(k p) c -> p k c", p=128)
    plain = 4 - grouped
    by_group = w[128 * grouped:128 * grouped + 512, :].rearrange("(g a d) c -> g d a c", g=2, a=4)

    def loads(i, u, c, slot):
        cols = ds(i * 512 + 128 * u, 128)
        return [(slot[0:64, grouped:grouped + 4], by_group[0][:, :, cols]),
                (slot[64:128, grouped:grouped + 4], by_group[1][:, :, cols]),
                (slot[:, plain:plain + 4], rows[:, plain:plain + 4, cols])]

    linear(m, name, 8, 1, loads, 3, [(0, 1), (1, 2)], lambda k: mixed[k], add_residual(m), on_vector=True)


def mlp(m, layer):
    up = weight_view(m.io["w_ff_up"][layer])
    down = m.io["w_ff_down"][layer].rearrange("(q k p) c -> q p k c", k=8, p=128)
    hidden = m.arena[:, m.work:m.work + 32 * T].rearrange("p (f t) -> p f t", f=32)

    def square(act, tile, out, inner):
        h = tile_of(hidden, tile)
        m.nc.scalar.activation(blocks4(h), out, ACT.Relu).then_inc(inner, 1)
        act.wait_ge(inner, 1)
        act.wait_ge(inner, tile + 1)
        return m.nc.scalar.activation(h, h, ACT.Square)

    m.ring = m.work + 32 * T
    linear(m, f"up{layer}", 32, 1, lambda i, u, c, slot: halves(slot, up[:, :, ds(i * 512 + 128 * u, 128)]), 2,
           [(0, 1), (1, 8)], lambda k: m.x[:, k, :], square)
    linear(m, f"down{layer}", 8, 4,
           lambda i, u, c, slot: halves(slot, down[c][:, :, ds(i * 256 + 128 * u, 128)]), 2,
           [(0, 1), (1, 4)], lambda k: hidden[:, k, :], add_residual(m), on_vector=True)


def layer_norm(m, name, gain, shift):
    nc = m.nc
    P = Steps(nc, f"{name}_pe", ["mean"] + [f"v{k}" for k in range(8)])
    V = Steps(nc, f"{name}_dve", [f"c{k}" for k in range(8)] + ["rstd"] + [f"n{k}" for k in range(8)])
    A = Steps(nc, f"{name}_act", [f"s{k}" for k in range(8)] + ["std"] + [f"g{k}" for k in range(8)])
    sq = m.arena[:, m.work:m.work + 2 * T].rearrange("p (s t) -> p s t", s=2)
    rstd = m.arena[:, m.work + 2 * T:m.work + 3 * T]
    with nc.Block() as block:

        @block.tensor
        def _(pe):
            for b in range(4):
                for k in range(8):
                    last = nc.tensor.matmul(m.ps[:, b * 512:b * 512 + TB], m.c("mean"),
                                            m.x[:, k, b * TB:(b + 1) * TB], start=(k == 0), stop=(k == 7))
            last.then_inc(*P.step("mean"))
            for k in range(8):
                pe.wait_ge(A.sem, A.done(0, f"s{k}"))
                for b in range(4):
                    at = 2048 + b * 512
                    last = nc.tensor.matmul(m.ps[:, at:at + TB], m.c("mean"), sq[:, k % 2, b * TB:(b + 1) * TB],
                                            start=(k == 0), stop=(k == 7), skip_group_check=True)
                last.then_inc(*P.step(f"v{k}"))

        @block.vector
        def _(dve):
            dve.wait_ge(P.sem, P.done(0, "mean"))
            for k in range(8):
                x = blocks4(m.x[:, k, :])
                nc.vector.tensor_tensor(x, x, linear_out(m, 0), ALU.subtract).then_inc(*V.step(f"c{k}"))
            dve.wait_ge(A.sem, A.done(0, "std"))
            nc.vector.reciprocal(rstd, rstd).then_inc(*V.step("rstd"))
            dve.wait_ge(V.sem, V.done(0, "rstd"))
            for k in range(8):
                nc.vector.tensor_tensor(m.x[:, k, :], m.x[:, k, :], rstd, ALU.mult).then_inc(*V.step(f"n{k}"))

        @block.scalar
        def _(act):
            for k in range(8):
                act.wait_ge(V.sem, V.done(0, f"c{k}"))
                if k >= 2:
                    act.wait_ge(P.sem, P.done(0, f"v{k - 2}"))
                nc.scalar.activation(sq[:, k % 2], m.x[:, k, :], ACT.Square).then_inc(*A.step(f"s{k}"))
            act.wait_ge(P.sem, P.done(0, "v7"))
            nc.scalar.activation(blocks4(rstd), linear_out(m, 1), ACT.Sqrt,
                                 bias=m.eps(0)).then_inc(*A.step("std"))
            for k in range(8):
                act.wait_ge(V.sem, V.done(0, f"n{k}"))
                nc.scalar.activation(m.x[:, k, :], m.x[:, k, :], ACT.Identity, scale=m.col(gain + k),
                                     bias=m.col(shift + k)).then_inc(*A.step(f"g{k}"))


def start(m):
    nc, io = m.nc, m.io
    natural = m.arena[:, m.work:m.work + 9 * D].rearrange("p (t d) -> p t d", t=9)
    rows = m.arena[:, m.work + 9 * D:m.work + 9 * D + 128]
    consts = nc.alloc_semaphore("consts_loaded")
    params = nc.alloc_semaphore("params_loaded")
    prompt = nc.alloc_semaphore("prompt_loaded")
    sample = nc.alloc_semaphore("sample_loaded")
    sinks = m.sinks_loaded = nc.alloc_semaphore("sinks_loaded")
    cleared = nc.alloc_semaphore("rows_cleared")
    turned = nc.alloc_semaphore("turned")
    moved = nc.alloc_semaphore("turned_moved")
    by_rows = [("mu", io["mu_b"], 14), ("w0", io["w0_b"], 4), ("a0", io["a0_b"], 4), ("kk", io["k_k_b"], 4),
               ("ka", io["k_a_b"], 4), ("lnxg", io["lnx_g_b"], 4), ("lnxb", io["lnx_b_b"], 4),
               ("subln", io["subln_g_c"], 1)]
    with nc.Block() as block:

        @block.sync
        def _(sp):
            sp.dma_start(m.const, io["consts"][:, 0:m.nconst]).then_inc(consts, 16)
            sp.dma_start(natural[:, 0:8, :], io["x_prompt"][0].rearrange("(t p) d -> p t d", p=128))\
              .then_inc(prompt, 16)
            sp.dma_start(natural[0:TS, 8, :], io["x_sample"][0]).then_inc(sample, 16)

        @block.scalar
        def _(act):
            act.wait_ge(cleared, 1)
            n = 0
            for name, src, count in by_rows:
                act.dma_start(rows[ROWS[name]:ROWS[name] + count, :],
                              src[0].rearrange("(k p) -> k p", p=128)).then_inc(params, 16)
                n += 1
            act.dma_start(rows[ROWS["rk"]:ROWS["rk"] + 4, :],
                          io["r_k_b"][0].rearrange("(k h) d -> k (h d)", h=2)).then_inc(params, 16)
            act.dma_start(rows[ROWS["shift"]:ROWS["shift"] + 14, :],
                          io["state_b_shift"][0, 0, 0].rearrange("(k p) -> k p", p=128)).then_inc(params, 16)
            for name, src in (("mixg", "ln_mix_g"), ("mixb", "ln_mix_b"), ("ffng", "ln_ffn_g"), ("ffnb", "ln_ffn_b")):
                act.dma_start(rows[ROWS[name]:ROWS[name] + 16, :],
                              io[src].rearrange("l (k p) -> (l k) p", p=128)).then_inc(params, 16)
            act.dma_start(m.sink, io["sink_a"].partition_broadcast(128).rearrange("p a h -> p (a h)"))\
               .then_inc(sinks, 16)
            for v, name in enumerate(("lam_q1_c", "lam_k1_c", "lam_q2_c", "lam_k2_c")):
                act.dma_start(m.lam_in[:, v, :], io[name].partition_broadcast(128).rearrange("p a h -> p (a h)"))\
                   .then_inc(sinks, 16)
            act.wait_ge(sinks, 16 * 5)

        @block.vector
        def _(dve):
            nc.vector.memset(m.om, 0.0)
            nc.vector.memset(rows, 0.0).then_inc(cleared, 1)
            for t in range(9):
                n = 128 if t < 8 else TS
                dve.wait_ge(turned, t + 1)
                nc.vector.tensor_copy(m.x[:, :, t * 128:t * 128 + n],
                                      m.ps[:, (t % 2) * 1024:(t % 2) * 1024 + 1024]
                                      .rearrange("p (k t) -> p k t", k=8)[:, :, 0:n]).then_inc(moved, 1)
            dve.wait_ge(turned, 10)
            nc.vector.tensor_copy(m.cols, bank(m, 4)[:, 0:128]).then_inc(moved, 1)

        @block.tensor
        def _(pe):
            pe.wait_ge(consts, 16)
            pe.wait_ge(prompt, 16)
            for t in range(9):
                n = 128 if t < 8 else TS
                if t == 8:
                    pe.wait_ge(sample, 16)
                if t >= 2:
                    pe.wait_ge(moved, t - 1)
                for k in range(8):
                    at = (t % 2) * 1024 + k * 128
                    last = nc.tensor.transpose(m.ps[:, at:at + n], natural[0:n, t, k * 128:(k + 1) * 128],
                                               m.c("ident")[0:n, 0:n])
                last.then_inc(turned, 1)
            pe.wait_ge(params, 16 * 14)
            nc.tensor.transpose(bank(m, 4)[:, 0:128], rows, m.c("ident")).then_inc(turned, 1)


def window_attention(m):
    nc, io = m.nc, m.io
    w = m.work
    vn = m.arena[:, w:w + 1280].rearrange("p (t c) -> p t c", t=10)
    kcache = m.arena[:, w + 1280:w + 1408]
    kct = m.arena[:, w + 1408:w + 1536]
    out_rows = m.arena[:, w + 1536:w + 2048].rearrange("p (a c) -> p a c", a=4)
    w += 2048
    qz = m.arena[:, w:w + 1024].rearrange("p (h q) -> p h q", h=8)
    idle = m.om[:, 5:6]
    logits = m.arena[:, w + 1024:w + 3072].rearrange("p (h k) -> p h k", h=8)
    pt = m.arena[:, w + 3072:w + 5120].rearrange("p (h j q) -> p h j q", h=8, j=2)
    on = m.arena[:, w + 5120:w + 5632]
    st = m.arena[:, w + 5632:w + 5696]
    top, low, total, sink_e, inv = (st[:, 8 * n:8 * n + 8] for n in range(5))
    q, kT, vT = m.p[:, 0:4, :], m.p[:, 16, :], m.p[:, 17, :]

    cached = nc.alloc_semaphore("a_cache_loaded")
    stored = nc.alloc_semaphore("a_stored")
    pre = Steps(nc, "a_pre_pe", [f"v{t}" for t in range(9)] + ["kc", "k7", "k8"])
    prev = Steps(nc, "a_pre_dve", [f"v{t}" for t in range(9)] + ["kc", "k7", "k8"])
    with nc.Block() as block:

        @block.sync
        def _(sp):
            sp.dma_start(kcache, io["cache_a_k"][0, 0].rearrange("s g d -> s (g d)")).then_inc(cached, 16)
            sp.dma_start(vn[:, 9, :], io["cache_a_v"][0, 0].rearrange("s g d -> s (g d)")).then_inc(cached, 16)
            rows = lambda o: o[0, 0].rearrange("s g d -> s (g d)")
            sp.dma_start(rows(io["a_k_s"])[0:64], io["cache_a_k"][0, 0, 64:128].rearrange("s g d -> s (g d)"))\
              .then_inc(stored, 16)
            sp.dma_start(rows(io["a_v_s"])[0:64], io["cache_a_v"][0, 0, 64:128].rearrange("s g d -> s (g d)"))\
              .then_inc(stored, 16)
            sp.wait_ge(prev.sem, prev.done(0, "k8"))
            sp.dma_start(rows(io["a_v_p"]), vn[:, 7, :]).then_inc(stored, 16)
            sp.dma_start(rows(io["a_v_s"])[64:128], vn[0:64, 8, :]).then_inc(stored, 16)
            sp.dma_start(rows(io["a_k_p"]), out_rows[:, 0, :]).then_inc(stored, 16)
            sp.dma_start(rows(io["a_k_s"])[64:128], out_rows[0:64, 1, :]).then_inc(stored, 16)
            sp.wait_ge(stored, 16 * 6)

        @block.gpsimd
        def _(pool):
            nc.gpsimd.memset(qz, 0.0)

        @block.tensor
        def _(pe):
            def turn(bk, src, n, name):
                nc.tensor.transpose(bank(m, bk)[0:n, 0:128], src, m.c("ident")).then_inc(*pre.step(name))

            for t in range(9):
                n = 128 if t < 8 else TS
                if t >= 4:
                    pe.wait_ge(prev.sem, prev.done(0, f"v{t - 4}"))
                turn(t % 4, vT[:, t * 128:t * 128 + n], n, f"v{t}")
            pe.wait_ge(cached, 32)
            turn(4, kcache, 128, "kc")
            turn(5, kT[:, TP - 128:TP], 128, "k7")
            turn(6, kT[:, TP:T], TS, "k8")

        @block.vector
        def _(dve):
            for t in range(9):
                n = 128 if t < 8 else TS
                dve.wait_ge(pre.sem, pre.done(0, f"v{t}"))
                nc.vector.tensor_copy(vn[0:n, t, :], bank(m, t % 4)[0:n, 0:128]).then_inc(*prev.step(f"v{t}"))
            for name, bk, dst in (("kc", 4, kct), ("k7", 5, out_rows[:, 0, :]), ("k8", 6, out_rows[0:64, 1, :])):
                dve.wait_ge(pre.sem, pre.done(0, name))
                n = dst.shape[0]
                nc.vector.tensor_copy(dst, bank(m, bk)[0:n, 0:128]).then_inc(*prev.step(name))

    P = Steps(nc, "a_pe", ["scores", "pt0", "pt1", "out", "turn"])
    V = Steps(nc, "a_dve", [f"logits{h}" for h in range(8)] + ["max", "top", "low", "pt1", "sum", "inv", "norm"])
    A = Steps(nc, "a_act", ["q0", "q1"] + [f"exp{h}" for h in range(8)] + ["sink", "pt0", "turned"])

    def keys(first, sample):
        return (1, 2, 256) if first else (0, 2, 192) if sample else (0, 2, 256)

    with nc.Block() as block:

        def rounds(engine, body):
            body(0, True, False)
            with engine.Fori(1, NQ) as t:
                body(t, False, False)
            body(NQ, False, True)

        @block.scalar
        def _(act):
            def body(t, first, sample):
                n = TS if sample else 128
                qs = q[:, :, ds(t * 128, n)]
                if not first:
                    act.wait_ge(P.sem, P.done(t - 1, "scores"))
                nc.scalar.activation(qz[0:64, 0:4, 0:n], qs[0:64], ACT.Copy, scale=SCALE).then_inc(*A.step("q0"))
                nc.scalar.activation(qz[64:128, 4:8, 0:n], qs[64:128], ACT.Copy, scale=SCALE)\
                    .then_inc(*A.step("q1"))
                a, _, z = keys(first, sample)
                act.wait_ge(V.sem, V.done(t, "low"))
                for h in range(8):
                    e = logits[:, h, a * 128:z]
                    nc.scalar.activation(e, e, ACT.Exp, bias=low[:, h:h + 1], accum_out=total[:, h:h + 1])\
                        .then_inc(*A.step(f"exp{h}"))
                nc.scalar.activation(sink_e, top, ACT.Exp).then_inc(*A.step("sink"))
                act.wait_ge(P.sem, P.done(t, "pt0"))
                move = m.ps[:, 2048:3072].rearrange("p (h j q) -> p h j q", h=4, j=2)
                if first:
                    nc.scalar.activation(pt[:, 0:4, 1, :], move[:, :, 1, :], ACT.Copy).then_inc(*A.step("pt0"))
                elif sample:
                    nc.scalar.activation(pt[:, 0:4, 0, :], move[:, :, 0, :], ACT.Copy)
                    nc.scalar.activation(pt[0:64, 0:4, 1, :], move[0:64, :, 1, :], ACT.Copy)\
                        .then_inc(*A.step("pt0"))
                else:
                    nc.scalar.activation(pt[:, 0:4], move, ACT.Copy).then_inc(*A.step("pt0"))
                act.wait_ge(P.sem, P.done(t, "turn"))
                nc.scalar.activation(idle, idle, ACT.Copy)
                nc.scalar.activation(q[:, :, ds(t * 128, n)],
                                     bank(m, 6).rearrange("p (a q) -> p a q", a=4)[:, :, 0:n], ACT.Copy)\
                    .then_inc(*A.step("turned"))

            rounds(act, body)

        @block.vector
        def _(dve):
            def body(t, first, sample):
                a, _, z = keys(first, sample)
                dve.wait_ge(P.sem, P.done(t, "scores"))
                for h in range(8):
                    at = h * 256
                    nc.vector.scalar_tensor_tensor(
                        out=logits[:, h, a * 128:z], in0=m.c("distA")[:, a * 128:z],
                        scalar=-2.0 ** (-(h + 1)), in1=m.ps[:, at + a * 128:at + z],
                        op0=ALU.mult, op1=ALU.add).then_inc(*V.step(f"logits{h}"))
                dve.wait_ge(V.sem, V.done(t, "logits7"))
                nc.vector.tensor_reduce(top, logits[:, :, a * 128:z], AX.X, ALU.max).then_inc(*V.step("max"))
                dve.wait_ge(V.sem, V.done(t, "max"))
                nc.vector.tensor_tensor(inv, top, m.sink, ALU.max).then_inc(*V.step("top"))
                dve.wait_ge(V.sem, V.done(t, "top"))
                nc.vector.tensor_tensor(top, m.sink, inv, ALU.subtract)
                nc.vector.tensor_scalar(low, inv, -1.0, None, ALU.mult).then_inc(*V.step("low"))
                dve.wait_ge(P.sem, P.done(t, "pt1"))
                move = m.ps[:, 0:1024].rearrange("p (h j q) -> p h j q", h=4, j=2)
                if first:
                    nc.vector.tensor_copy(pt[:, 4:8, 1, :], move[:, :, 1, :]).then_inc(*V.step("pt1"))
                elif sample:
                    nc.vector.tensor_copy(pt[:, 4:8, 0, :], move[:, :, 0, :])
                    nc.vector.tensor_copy(pt[0:64, 4:8, 1, :], move[0:64, :, 1, :]).then_inc(*V.step("pt1"))
                else:
                    nc.vector.tensor_copy(pt[:, 4:8], move).then_inc(*V.step("pt1"))
                dve.wait_ge(A.sem, A.done(t, "sink"))
                nc.vector.tensor_tensor(total, total, sink_e, ALU.add).then_inc(*V.step("sum"))
                dve.wait_ge(V.sem, V.done(t, "sum"))
                nc.vector.reciprocal(inv, total).then_inc(*V.step("inv"))
                dve.wait_ge(V.sem, V.done(t, "inv"))
                dve.wait_ge(P.sem, P.done(t, "out"))
                nc.vector.tensor_tensor(
                    on.rearrange("p (a g d) -> p g a d", a=4, g=2),
                    bank(m, 7).rearrange("p (g a d) -> p g a d", g=2, a=4),
                    inv.rearrange("p (g a) -> p g a", g=2).unsqueeze(3).to_broadcast([128, 2, 4, 64]),
                    ALU.mult).then_inc(*V.step("norm"))

            rounds(dve, body)

        @block.tensor
        def _(pe):
            def turn_probs(t, first, sample, base, heads, name):
                for n, h in enumerate(heads):
                    for j in (1,) if first else (0, 1):
                        k = TS if sample and j == 1 else 128
                        at = base + n * 256 + j * 128
                        last = nc.tensor.transpose(m.ps[0:k, at:at + 128], logits[:, h, j * 128:j * 128 + k],
                                                   m.c("ident"))
                last.then_inc(*P.step(name))

            def body(t, first, sample):
                pe.wait_ge(A.sem, A.done(t, "q1"))
                for h in range(8):
                    at = h * 256
                    if sample:
                        nc.tensor.matmul(m.ps[:, at:at + 128], qz[:, h, :], kct, start=True, stop=True)
                        last = nc.tensor.matmul(m.ps[:, at + 128:at + 192], qz[:, h, :], kT[:, TP:T],
                                                start=True, stop=True)
                    elif first:
                        last = nc.tensor.matmul(m.ps[:, at + 128:at + 256], qz[:, h, :], kT[:, 0:128],
                                                start=True, stop=True)
                    else:
                        last = nc.tensor.matmul(m.ps[:, at:at + 256], qz[:, h, :], kT[:, ds(t * 128 - 128, 256)],
                                                start=True, stop=True)
                last.then_inc(*P.step("scores"))
                pe.wait_ge(A.sem, A.done(t, "exp3"))
                turn_probs(t, first, sample, 2048, range(4), "pt0")
                pe.wait_ge(A.sem, A.done(t, "exp7"))
                turn_probs(t, first, sample, 0, range(4, 8), "pt1")
                pe.wait_ge(A.sem, A.done(t, "pt0"))
                pe.wait_ge(V.sem, V.done(t, "pt1"))
                for h in range(8):
                    g = h // 4
                    for j in (1,) if first else (0, 1):
                        k = TS if sample and j == 1 else 128
                        if sample or first:
                            v = vn[0:k, (9, 8)[j] if sample else 0, 64 * g:64 * g + 64]
                        else:
                            v = vn[:, ds(t + (j - 1), 1), 64 * g:64 * g + 64].rearrange("p a d -> p (a d)")
                        last = nc.tensor.matmul(bank(m, 7)[:, h * 64:h * 64 + 64], pt[0:k, h, j, :], v,
                                                start=(j == 0 or first), stop=(j == 1))
                last.then_inc(*P.step("out"))
                pe.wait_ge(V.sem, V.done(t, "norm"))
                if not first:
                    pe.wait_ge(A.sem, A.done(t - 1, "turned"))
                for a in range(4):
                    last = nc.tensor.transpose(bank(m, 6)[:, a * 128:a * 128 + 128], on[:, a * 128:a * 128 + 128],
                                               m.c("ident"))
                last.then_inc(*P.step("turn"))

            rounds(pe, body)


def rwkv_prepare(m):
    nc, io = m.nc, m.io
    w = m.work
    m.kk = m.arena[:, w:w + 4 * T].rearrange("p (h t) -> p h t", h=4)
    m.a = m.arena[:, w + 4 * T:w + 8 * T].rearrange("p (h t) -> p h t", h=4)
    m.pc = m.arena[:, w + 8 * T:w + 8 * T + 68].rearrange("p (h c) -> p h c", h=4)
    m.g_up = m.arena[:, w + 8 * T + 68:w + 8 * T + 580]
    w += 8 * T + 580
    m.chunk_at = w
    diff = m.arena[:, w:w + 2 * T].rearrange("p (s t) -> p s t", s=2)
    edge = m.arena[:, w + 2 * T:w + 2 * T + 28].rearrange("p (k e) -> p k e", e=2)
    lastc = m.arena[:, w + 2 * T + 28:w + 2 * T + 56]
    lastr = m.arena[:, w + 2 * T + 64:w + 2 * T + 192]
    wa_up = m.arena[:, w + 2 * T + 192:w + 2 * T + 704]
    w += 2 * T + 704
    sg, cum, before, tmp = (m.arena[:, w + n * T:w + n * T + T] for n in range(4))
    assert w + 4 * T <= m.limit, w + 4 * T
    p = m.p
    r, k, v = p[:, 4:8, :], p[:, 8:12, :], p[:, 12:16, :]
    spots = [(0, 12, 4), (12, 14, 18)]

    loaded = nc.alloc_semaphore("b_weights_loaded")
    stored = nc.alloc_semaphore("b_shift_stored")
    S = Steps(nc, "b_shift_dve", ["edge"] + [f"t{j}" for j in range(3 * 14)] + ["last"])
    S2 = nc.alloc_semaphore("b_shift_turned")
    with nc.Block() as block:

        @block.sync
        def _(sp):
            sp.dma_start(wa_up[0:64], io["w_up_b"][0]).then_inc(loaded, 16)
            sp.dma_start(wa_up[64:128], io["a_up_b"][0]).then_inc(loaded, 16)
            sp.dma_start(m.g_up, io["g_up_b"][0]).then_inc(loaded, 16)
            sp.wait_ge(S.sem, S.done(0, "last"))
            for n, out in enumerate(("b_shift_p", "b_shift_s")):
                sp.dma_start(io[out][0, 0, 0].rearrange("(k p) -> k p", p=128), lastr[14 * n:14 * n + 14, :])                  .then_inc(stored, 16)
            sp.wait_ge(stored, 32)

        @block.vector
        def _(dve):
            for a, b, at in spots:
                nc.vector.tensor_copy(lastc[:, a:b], p[:, at:at + b - a, TP - 1])
                nc.vector.tensor_copy(lastc[:, 14 + a:14 + b], p[:, at:at + b - a, T - 1])
            for a, b, at in spots:
                nc.vector.tensor_scalar(edge[:, a:b, 0], p[:, at:at + b - a, 0], -1.0, None, ALU.mult)
                last = nc.vector.tensor_tensor(edge[:, a:b, 1], m.cols[:, ROWS["shift"] + a:ROWS["shift"] + b],
                                               p[:, at:at + b - a, TP], ALU.subtract)
            last.then_inc(*S.step("edge"))
            dve.wait_ge(S.sem, S.done(0, "edge"))
            for j in range(14):
                x = p[:, 4 + j if j < 12 else 6 + j, :]
                d = diff[:, j % 2]
                nc.vector.tensor_tensor(d[:, 1:T], x[:, 0:T - 1], x[:, 1:T], ALU.subtract)                    .then_inc(*S.step(f"t{3 * j}"))
                dve.wait_ge(S.sem, S.done(0, f"t{3 * j}"))
                nc.vector.tensor_copy(d[:, 0:T:TP], edge[:, j, :]).then_inc(*S.step(f"t{3 * j + 1}"))
                dve.wait_ge(S.sem, S.done(0, f"t{3 * j + 1}"))
                nc.vector.scalar_tensor_tensor(out=x, in0=d, scalar=m.col(ROWS["mu"] + j), in1=x,
                                               op0=ALU.mult, op1=ALU.add).then_inc(*S.step(f"t{3 * j + 2}"))
            dve.wait_ge(S2, 1)
            nc.vector.tensor_copy(lastr[0:28, :], bank(m, 0)[0:28, 0:128]).then_inc(*S.step("last"))

        @block.tensor
        def _(pe):
            pe.wait_ge(S.sem, S.done(0, "edge"))
            nc.tensor.transpose(bank(m, 0)[0:28, 0:128], lastc, m.c("ident")).then_inc(S2, 1)

    bonus = [16, 17, 20, 18]
    m.bonus = bonus
    m.y = r
    P = Steps(nc, "b_pe", ["w", "a", "norm", "bonus"])
    V = Steps(nc, "b_dve", ["kk", "kk2", "cum", "before", "ak", "k", "rk", "rkk", "rnorm", "kkn", "bon", "b",
                            "A", "K", "B", "pc"])
    A = Steps(nc, "b_act", ["sg", "a", "norm", "e1", "e2", "e3"])
    om = m.om
    pre = nc.alloc_semaphore("b_one_minus_ka")
    gates = nc.alloc_semaphore("b_gates")
    e1, e2, e3 = diff[:, 0], diff[:, 1], sg

    with nc.Block() as block:

        @block.tensor
        def _(pe):
            pe.wait_ge(loaded, 48)
            for h in range(4):
                cols = slice(128 * h, 128 * h + 128)

                def product(base, lhsT, src, name):
                    for b in range(4):
                        at = base + 512 * b
                        last = nc.tensor.matmul(m.ps[:, at:at + TB], lhsT, src[:, b * TB:(b + 1) * TB],
                                                start=True, stop=True)
                    last.then_inc(*P.step(name))

                if h:
                    pe.wait_ge(A.sem, A.done(h - 1, "norm"))
                pe.wait_ge(gates, 1)
                product(0, wa_up[0:64, cols], p[0:64, 18, :], "w")
                if h:
                    pe.wait_ge(V.sem, V.done(h - 1, "bon"))
                product(2048, wa_up[64:128, cols], p[64:128, 18, :], "a")
                pe.wait_ge(A.sem, A.done(h, "a"))
                pe.wait_ge(V.sem, V.done(h, "kk2"))
                product(0, m.c("heads"), tmp, "norm")
                pe.wait_ge(V.sem, V.done(h, "rkk"))
                product(2048, m.c("heads"), before, "bonus")

        @block.scalar
        def _(act):
            for h in range(4):
                if h == 0:
                    nc.scalar.activation(p[0:64, 18, :], p[0:64, 18, :], ACT.Tanh).then_inc(gates, 1)
                    nc.scalar.activation(p[:, 19, :], p[:, 19, :], ACT.Sigmoid).then_inc(gates, 1)
                act.wait_ge(P.sem, P.done(h, "w"))
                if h:
                    act.wait_ge(V.sem, V.done(h - 1, "B"))
                nc.scalar.activation(blocks4(sg), linear_out(m, 0), ACT.Sigmoid, bias=m.col(ROWS["w0"] + h))                    .then_inc(*A.step("sg"))
                act.wait_ge(P.sem, P.done(h, "a"))
                nc.scalar.activation(blocks4(m.a[:, h]), linear_out(m, 1), ACT.Sigmoid,
                                     bias=m.col(ROWS["a0"] + h)).then_inc(*A.step("a"))
                act.wait_ge(P.sem, P.done(h, "norm"))
                nc.scalar.activation(blocks4(tmp), linear_out(m, 0), ACT.Sqrt, bias=m.eps(1))                    .then_inc(*A.step("norm"))
                act.wait_ge(V.sem, V.done(h, "k"))
                nc.scalar.activation(e1, cum, ACT.Exp, scale=-DECAY).then_inc(*A.step("e1"))
                nc.scalar.activation(e2, e2, ACT.Exp, scale=-DECAY).then_inc(*A.step("e2"))
                nc.scalar.activation(e3, cum, ACT.Exp, scale=DECAY).then_inc(*A.step("e3"))

        @block.vector
        def _(dve):
            dve.wait_ge(S.sem, S.done(0, "last"))
            nc.vector.tensor_scalar(om[:, 0:4], m.cols[:, ROWS["ka"]:ROWS["ka"] + 4], -1.0, 1.0,
                                    ALU.mult, ALU.add).then_inc(pre, 1)
            dve.wait_ge(pre, 1)
            tt, stt = nc.vector.tensor_tensor, nc.vector.scalar_tensor_tensor

            for h in range(4):
                kk, a = m.kk[:, h], m.a[:, h]

                def after(name, t=h):
                    dve.wait_ge(V.sem, V.done(t, name))

                nc.vector.tensor_scalar(kk, k[:, h], m.col(ROWS["kk"] + h), None, ALU.mult).then_inc(*V.step("kk"))
                after("kk")
                tt(tmp, kk, kk, ALU.mult).then_inc(*V.step("kk2"))
                dve.wait_ge(A.sem, A.done(h, "a"))
                nc.vector.tensor_tensor_scan(cum, m.c("reset"), sg, 0.0, ALU.mult, ALU.add)                    .then_inc(*V.step("cum"))
                after("cum")
                tt(e2, cum, sg, ALU.subtract).then_inc(*V.step("before"))
                nc.vector.tensor_scalar(e1, a, m.col(ROWS["ka"] + h), om[:, h:h + 1], ALU.mult, ALU.add)                    .then_inc(*V.step("ak"))
                after("ak")
                tt(k[:, h], k[:, h], e1, ALU.mult).then_inc(*V.step("k"))
                nc.vector.tensor_scalar(before, r[:, h], m.col(ROWS["rk"] + h), None, ALU.mult)                    .then_inc(*V.step("rk"))
                after("rk")
                tt(before, before, k[:, h], ALU.mult).then_inc(*V.step("rkk"))
                dve.wait_ge(A.sem, A.done(h, "norm"))
                nc.vector.reciprocal(tmp, tmp).then_inc(*V.step("rnorm"))
                after("rnorm")
                stt(out=kk, in0=kk, scalar=-1.0, in1=tmp, op0=ALU.mult, op1=ALU.mult).then_inc(*V.step("kkn"))
                dve.wait_ge(P.sem, P.done(h, "bonus"))
                tt(blocks4(p[:, bonus[h], :]), linear_out(m, 1), blocks4(v[:, h]), ALU.mult)                    .then_inc(*V.step("bon"))
                after("kkn")
                stt(out=a, in0=a, scalar=-1.0, in1=kk, op0=ALU.mult, op1=ALU.mult).then_inc(*V.step("b"))
                dve.wait_ge(A.sem, A.done(h, "e3"))
                after("b")
                tt(r[:, h], r[:, h], e1, ALU.mult)
                tt(kk, kk, e2, ALU.mult).then_inc(*V.step("A"))
                tt(k[:, h], k[:, h], e3, ALU.mult).then_inc(*V.step("K"))
                tt(a, a, e3, ALU.mult).then_inc(*V.step("B"))
                nc.vector.tensor_copy(m.pc[:, h, :], e1[:, CH - 1:T:CH]).then_inc(*V.step("pc"))
                after("pc")


def rwkv_chunks(m):
    nc, io = m.nc, m.io
    w = m.chunk_at
    slot = {}
    for name in ("R", "A", "B", "K", "V", "Vn", "Bn", "Kn", "X0", "XT0", "XT1", "LT", "LkT", "MbT", "MkT", "T1"):
        slot[name] = m.arena[:, w:w + 512]
        w += 512
    slot["U"], slot["SA"], slot["X1"] = slot["B"], slot["K"], slot["V"]
    S = slot["S"] = m.state
    assert w <= m.limit, w
    block4 = {n: heads4(a) for n, a in slot.items()}
    p = m.p
    src = {"R": p[:, 4:8, :], "A": m.kk, "B": m.a, "K": p[:, 8:12, :], "V": p[:, 12:16, :]}
    LEVELS = (2, 4, 8, 16, 32)
    pairs = (("L", "A", "B"), ("LT", "B", "A"), ("LkT", "K", "A"), ("MbT", "B", "R"), ("MkT", "K", "R"))
    pe_steps = [n for n, _, _ in pairs] + ["Vn", "Bn", "Kn", "T2", "X2", "XT2", "T4", "X4", "XT4", "T8", "X8",
                                           "XT8", "T16", "X16", "XT16", "T32", "XT32", "U", "SA", "Y", "S"]
    banks = {n: i % 8 for i, n in enumerate(pe_steps)}
    P = Steps(nc, "w_pe", pe_steps)
    V = Steps(nc, "w_dve", ["copyR", "copyA", "L", "X1", "LT", "XT1m", "XT1", "LkT", "MbT", "MkT"]
              + sum([[f"T{n}"] + ([f"X{n}"] if n < 32 else []) + [f"XT{n}"] for n in LEVELS], [])
              + ["U", "SA", "Sadd", "S"])
    A = Steps(nc, "w_act", ["copyB", "copyK", "copyV", "Vn", "Bn", "Kn", "Y"])
    st_load = nc.alloc_semaphore("w_state_loaded")
    st_turn = nc.alloc_semaphore("w_state_turned")
    st_move = nc.alloc_semaphore("w_state_moved")
    cleared = nc.alloc_semaphore("w_cleared")
    stored = nc.alloc_semaphore("w_stored")
    state_in = slot["U"]
    state_out = slot["SA"]

    with nc.Block() as block:

        @block.gpsimd
        def _(pool):
            for n in ("R", "A", "B", "K", "V", "S"):
                last = nc.gpsimd.memset(slot[n], 0.0)
            last.then_inc(cleared, 1)

    def mask(name):
        return m.c(name).unsqueeze(1).to_broadcast([128, 4, 128])

    def halves_copy(op, name, t):
        cols = ds(t * CH, CH)
        op(block4[name][0:64, :, 0:64], src[name][0:64, :, cols])
        return op(block4[name][64:128, :, 64:128], src[name][64:128, :, cols])

    def chunk_vector(dve, t, first):
        nc_v = nc.vector
        tt = nc_v.tensor_tensor

        def after(name):
            dve.wait_ge(V.sem, V.done(t, name))

        def product(name):
            dve.wait_ge(P.sem, P.done(t, name))
            return heads4(bank(m, banks[name]))

        if not first:
            dve.wait_ge(P.sem, P.rounds(t))
        halves_copy(nc_v.tensor_copy, "R", t).then_inc(*V.step("copyR"))
        halves_copy(nc_v.tensor_copy, "A", t).then_inc(*V.step("copyA"))
        tt(block4["T1"], product("L"), mask("low1"), ALU.mult).then_inc(*V.step("L"))
        after("L")
        tt(block4["X0"], block4["T1"], mask("ident"), ALU.add).then_inc(*V.step("X1"))
        tt(block4["LT"], product("LT"), mask("strict"), ALU.mult).then_inc(*V.step("LT"))
        after("LT")
        tt(block4["T1"], block4["LT"], mask("up1"), ALU.mult).then_inc(*V.step("XT1m"))
        after("XT1m")
        tt(block4["XT0"], block4["T1"], mask("ident"), ALU.add).then_inc(*V.step("XT1"))
        tt(block4["LkT"], product("LkT"), mask("strict"), ALU.mult).then_inc(*V.step("LkT"))
        tt(block4["MbT"], product("MbT"), mask("upto"), ALU.mult).then_inc(*V.step("MbT"))
        tt(block4["MkT"], product("MkT"), mask("upto"), ALU.mult).then_inc(*V.step("MkT"))
        for i, n in enumerate(LEVELS):
            old, new = i % 2, 1 - i % 2
            tt(block4["T1"], product(f"T{n}"), mask(f"low{n}"), ALU.mult).then_inc(*V.step(f"T{n}"))
            if n < 32:
                tt(block4[f"X{new}"], product(f"X{n}"), block4[f"X{old}"], ALU.add).then_inc(*V.step(f"X{n}"))
            tt(block4[f"XT{new}"], product(f"XT{n}"), block4[f"XT{old}"], ALU.add).then_inc(*V.step(f"XT{n}"))
        nc_v.tensor_copy(block4["U"], product("U")).then_inc(*V.step("U"))
        nc_v.tensor_copy(block4["SA"], product("SA")).then_inc(*V.step("SA"))
        tt(block4["T1"], product("S"), block4["S"], ALU.add).then_inc(*V.step("Sadd"))
        after("Sadd")
        tt(block4["S"], block4["T1"], m.pc[:, :, ds(t, 1)].to_broadcast([128, 4, 128]), ALU.mult)\
            .then_inc(*V.step("S"))

    def chunk_scalar(act, t, first):
        def copy(out, in_):
            return nc.scalar.activation(out, in_, ACT.Copy)

        if not first:
            act.wait_ge(P.sem, P.rounds(t))
        for name in ("B", "K", "V"):
            halves_copy(copy, name, t).then_inc(*A.step(f"copy{name}"))
        for name in ("Vn", "Bn", "Kn"):
            act.wait_ge(P.sem, P.done(t, name))
            copy(slot[name], bank(m, banks[name])).then_inc(*A.step(name))
        act.wait_ge(P.sem, P.done(t, "Y"))
        y = heads4(bank(m, banks["Y"]))
        cols = ds(t * CH, CH)
        copy(m.y[0:64, :, cols], y[0:64, :, 0:64])
        copy(m.y[64:128, :, cols], y[64:128, :, 64:128]).then_inc(*A.step("Y"))

    def chunk_tensor(pe, t, first):
        def product(name, *terms):
            for h in range(4):
                out = bank(m, banks[name])[:, h * 128:h * 128 + 128]
                for i, (lhsT, rhs) in enumerate(terms):
                    last = nc.tensor.matmul(out, block4[lhsT][:, h, :], block4[rhs][:, h, :], start=(i == 0),
                                            stop=(i == len(terms) - 1))
            last.then_inc(*P.step(name))

        def turn(name, src_name):
            for h in range(4):
                last = nc.tensor.transpose(bank(m, banks[name])[:, h * 128:h * 128 + 128], block4[src_name][:, h, :],
                                           m.c("ident"))
            last.then_inc(*P.step(name))

        if not first:
            pe.wait_ge(V.sem, V.rounds(t))
            pe.wait_ge(A.sem, A.rounds(t))
        pe.wait_ge(V.sem, V.done(t, "copyA"))
        pe.wait_ge(A.sem, A.done(t, "copyV"))
        for name, lhsT, rhs in pairs:
            product(name, (lhsT, rhs))
        turn("Vn", "V")
        turn("Bn", "B")
        turn("Kn", "K")
        pe.wait_ge(V.sem, V.done(t, "MkT"))
        for i, n in enumerate(LEVELS):
            old = i % 2
            if i:
                pe.wait_ge(V.sem, V.done(t, f"XT{LEVELS[i - 1]}"))
            product(f"T{n}", ("LT", f"X{old}"))
            pe.wait_ge(V.sem, V.done(t, f"T{n}"))
            if n == 2:
                pe.wait_ge(A.sem, A.done(t, "Kn"))
            if n < 32:
                product(f"X{n}", (f"XT{old}", "T1"))
            product(f"XT{n}", ("T1", f"XT{old}"))
        product("U", ("A", "S"), ("LkT", "Vn"))
        pe.wait_ge(V.sem, V.done(t, "U"))
        product("SA", ("XT1", "U"))
        pe.wait_ge(V.sem, V.done(t, "SA"))
        product("Y", ("S", "R"), ("SA", "MbT"), ("Vn", "MkT"))
        product("S", ("Bn", "SA"), ("Kn", "Vn"))

    def over_chunks(engine, body, between):
        body(engine, 0, True)
        with engine.Fori(1, NCHUNK) as t:
            body(engine, t, False)
        between(engine)
        body(engine, NCHUNK, False)

    heads_out = io["b_wkv_p"][0, 0], io["b_wkv_s"][0, 0]

    with nc.Block() as block:

        @block.vector
        def _(dve):
            dve.wait_ge(cleared, 1)

            def save(n):
                dve.wait_ge(st_turn, 2 * n + 1)
                nc.vector.tensor_copy(state_out, bank(m, 0)).then_inc(st_move, 1)

            def between(engine):
                save(0)
                dve.wait_ge(st_turn, 2)
                nc.vector.tensor_copy(S, bank(m, 1)).then_inc(st_move, 1)
                dve.wait_ge(st_move, 2)
                dve.wait_ge(stored, 32 * 4)

            over_chunks(dve, chunk_vector, between)
            save(1)

        @block.scalar
        def _(act):
            def between(engine):
                act.wait_ge(st_turn, 2)
                act.wait_ge(stored, 32 * 4)

            over_chunks(act, chunk_scalar, between)

        @block.tensor
        def _(pe):
            pe.wait_ge(cleared, 1)

            def save():
                for h in range(4):
                    last = nc.tensor.transpose(bank(m, 0)[:, h * 128:h * 128 + 128], block4["S"][:, h, :],
                                               m.c("ident"))
                last.then_inc(st_turn, 1)

            def between(engine):
                pe.wait_ge(V.sem, V.rounds(NCHUNK))
                pe.wait_ge(A.sem, A.rounds(NCHUNK))
                save()
                pe.wait_ge(st_load, 32 * 4)
                for h in range(4):
                    last = nc.tensor.transpose(bank(m, 1)[:, h * 128:h * 128 + 128],
                                               heads4(state_in)[:, h, :], m.c("ident"))
                last.then_inc(st_turn, 1)
                pe.wait_ge(st_move, 2)

            over_chunks(pe, chunk_tensor, between)
            pe.wait_ge(V.sem, V.rounds(NCHUNK + 1))
            pe.wait_ge(A.sem, A.rounds(NCHUNK + 1))
            save()

        @block.sync
        def _(sp):
            sp.wait_ge(V.sem, V.rounds(NCHUNK))
            sp.wait_ge(P.sem, P.rounds(NCHUNK))
            for h in range(8):
                o = 64 * (h % 2)
                sp.dma_start(heads4(state_in)[o:o + 64, h // 2, o:o + 64], io["state_b_wkv"][0, 0, h])\
                  .then_inc(st_load, 16)
            for n in range(2):
                sp.wait_ge(st_move, 2 * n + 1)
                for h in range(8):
                    o = 64 * (h % 2)
                    sp.dma_start(heads_out[n][h], heads4(state_out)[o:o + 64, h // 2, o:o + 64])\
                      .then_inc(stored, 16)
            sp.wait_ge(stored, 32 * 8)


def rwkv_finish(m):
    nc = m.nc
    w = m.chunk_at
    sq, tmp = (m.arena[:, w + n * T:w + n * T + T] for n in range(2))
    P = Steps(nc, "e_pe", ["mean", "gate", "var"])
    V = Steps(nc, "e_dve", ["mean", "centred", "rstd", "normal", "bonus", "gated"])
    A = Steps(nc, "e_act", ["square", "std", "affine"])
    y = m.y
    with nc.Block() as block:

        def sums(base, lhsT, src, name):
            for b in range(4):
                at = base + 512 * b
                last = nc.tensor.matmul(m.ps[:, at:at + TB], lhsT, src[:, b * TB:(b + 1) * TB], start=True, stop=True)
            last.then_inc(*P.step(name))

        @block.tensor
        def _(pe):
            for h in range(4):
                if h:
                    pe.wait_ge(V.sem, V.done(h - 1, "gated"))
                sums(0, m.c("heads"), y[:, h], "mean")
                sums(2048, m.g_up[:, h * 128:h * 128 + 128], m.p[:, 19, :], "gate")
                pe.wait_ge(A.sem, A.done(h, "square"))
                sums(0, m.c("heads"), sq, "var")

        @block.vector
        def _(dve):
            for h in range(4):
                def after(name, t=h):
                    dve.wait_ge(V.sem, V.done(t, name))

                dve.wait_ge(P.sem, P.done(h, "mean"))
                nc.vector.tensor_scalar(blocks4(tmp), linear_out(m, 0), 1.0 / HD, None, ALU.mult)\
                    .then_inc(*V.step("mean"))
                after("mean")
                nc.vector.tensor_tensor(y[:, h], y[:, h], tmp, ALU.subtract).then_inc(*V.step("centred"))
                dve.wait_ge(A.sem, A.done(h, "std"))
                nc.vector.reciprocal(tmp, tmp).then_inc(*V.step("rstd"))
                after("rstd")
                nc.vector.tensor_tensor(y[:, h], y[:, h], tmp, ALU.mult).then_inc(*V.step("normal"))
                dve.wait_ge(A.sem, A.done(h, "affine"))
                nc.vector.tensor_tensor(y[:, h], y[:, h], m.p[:, m.bonus[h], :], ALU.add).then_inc(*V.step("bonus"))
                dve.wait_ge(P.sem, P.done(h, "gate"))
                after("bonus")
                nc.vector.tensor_tensor(blocks4(y[:, h]), blocks4(y[:, h]), linear_out(m, 1), ALU.mult)\
                    .then_inc(*V.step("gated"))

        @block.scalar
        def _(act):
            for h in range(4):
                act.wait_ge(V.sem, V.done(h, "centred"))
                nc.scalar.activation(sq, y[:, h], ACT.Square).then_inc(*A.step("square"))
                act.wait_ge(P.sem, P.done(h, "var"))
                nc.scalar.activation(blocks4(tmp), linear_out(m, 0), ACT.Sqrt, bias=m.eps(2), scale=1.0 / HD)\
                    .then_inc(*A.step("std"))
                act.wait_ge(V.sem, V.done(h, "normal"))
                nc.scalar.activation(y[:, h], y[:, h], ACT.Identity, scale=m.col(ROWS["lnxg"] + h),
                                     bias=m.col(ROWS["lnxb"] + h)).then_inc(*A.step("affine"))


def turn_rows(m):
    nc, io = m.nc, m.io
    w = m.work
    m.vn = m.arena[:, w:w + 9 * 512].rearrange("p (t c) -> p t c", t=9)
    w += 9 * 512
    m.vd = m.arena[:, w:w + 9 * 128].rearrange("p (t c) -> p t c", t=9)
    w += 9 * 128
    m.wn = m.arena[:, w:w + 72].rearrange("p (t h) -> p t h", t=9)
    w += 72
    m.odd_work = w
    rows = m.arena[:, w:w + 2 * 704].rearrange("p (s c) -> p s c", s=2)
    p = m.p
    P = Steps(nc, "r_pe", ["k", "v", "rest"])
    A = Steps(nc, "r_act", ["k"])
    V = Steps(nc, "r_dve", ["v", "rest"])
    stored = [nc.alloc_semaphore(f"r_stored{s}") for s in range(2)]
    lam_p = nc.alloc_semaphore("lambda_products")
    lam_e = nc.alloc_semaphore("lambda_exps")
    WSCALE = SCALE * 8 ** -0.5
    n_of = lambda t: 128 if t < 8 else TS

    with nc.Block() as block:

        @block.tensor
        def _(pe):
            for t in range(9):
                n, c = n_of(t), slice(t * 128, t * 128 + n_of(t))
                if t >= 2:
                    pe.wait_ge(A.sem, A.done(t - 2, "k"))
                    pe.wait_ge(V.sem, V.done(t - 2, "rest"))
                b = 3 * (t % 2)

                def turn(bk, at, tile, k):
                    return nc.tensor.transpose(bank(m, bk)[0:n, at:at + k], p[0:k, tile, c], m.c("ident")[0:k, 0:k])

                for h in range(4):
                    last = turn(b, h * 128, 4 + h, 128)
                last.then_inc(*P.step("k"))
                for h in range(4):
                    last = turn(b + 1, h * 128, 8 + h, 128)
                last.then_inc(*P.step("v"))
                turn(b + 2, 0, 20, 128)
                turn(b + 2, 128, 22, 128)
                turn(b + 2, 256, 21, 64)
                turn(b + 2, 320, 23, 8).then_inc(*P.step("rest"))

        @block.scalar
        def _(act):
            act.wait_ge(lam_p, 2)
            nc.scalar.activation(m.lam[:, 0:2], m.lam[:, 0:2], ACT.Exp).then_inc(lam_e, 1)
            for t in range(9):
                act.wait_ge(P.sem, P.done(t, "k"))
                if t >= 2:
                    act.wait_ge(stored[t % 2], 16 * 5 * (t // 2))
                nc.scalar.activation(rows[0:n_of(t), t % 2, 0:512], bank(m, 3 * (t % 2))[0:n_of(t), :], ACT.Copy)\
                    .then_inc(*A.step("k"))

        @block.vector
        def _(dve):
            nc.vector.tensor_tensor(m.lam_in[:, 0:4:2, :], m.lam_in[:, 0:4:2, :], m.lam_in[:, 1:4:2, :], ALU.mult)\
                .then_inc(lam_p, 1)
            dve.wait_ge(lam_p, 1)
            nc.vector.tensor_reduce(m.lam[:, 0:2], m.lam_in[:, 0:4:2, :], AX.X, ALU.add).then_inc(lam_p, 1)
            dve.wait_ge(lam_e, 1)
            nc.vector.tensor_tensor(m.lam[:, 2:3], m.lam[:, 0:1], m.lam[:, 1:2], ALU.subtract).then_inc(lam_p, 1)
            dve.wait_ge(lam_p, 3)
            nc.vector.tensor_scalar(m.lam[:, 3:4], m.lam[:, 2:3], LAM_INIT, -1.0, ALU.add, ALU.mult)\
                .then_inc(lam_p, 1)
            for t in range(9):
                n, b = n_of(t), 3 * (t % 2)
                dve.wait_ge(P.sem, P.done(t, "v"))
                nc.vector.tensor_copy(m.vn[0:n, t, :], bank(m, b + 1)[0:n, :]).then_inc(*V.step("v"))
                dve.wait_ge(P.sem, P.done(t, "rest"))
                if t >= 2:
                    dve.wait_ge(stored[t % 2], 16 * 5 * (t // 2))
                r = bank(m, b + 2)
                nc.vector.tensor_copy(rows[0:n, t % 2, 512:640], r[0:n, 0:128])
                nc.vector.tensor_copy(m.vd[0:n, t, :], r[0:n, 128:256])
                nc.vector.tensor_copy(rows[0:n, t % 2, 640:704], r[0:n, 256:320])
                nc.vector.tensor_scalar(m.wn[0:n, t, :], r[0:n, 320:328], WSCALE, None, ALU.mult)\
                    .then_inc(*V.step("rest"))

        @block.sync
        def _(sp):
            for t in range(9):
                n = n_of(t)

                def out(name):
                    o = io[name + ("_p" if t < 8 else "_s")][0, 0]
                    if len(o.shape) == 4:
                        o = o.rearrange("s h m d -> s (h m d)")
                    elif len(o.shape) == 3:
                        o = o.rearrange("s h d -> s (h d)")
                    return o[t * 128:t * 128 + n] if t < 8 else o

                sp.wait_ge(A.sem, A.done(t, "k"))
                sp.wait_ge(V.sem, V.done(t, "rest"))
                for name, src in (("c_k", rows[0:n, t % 2, 0:512]), ("c_v", m.vn[0:n, t, :]),
                                  ("d_k", rows[0:n, t % 2, 512:640]), ("d_v", m.vd[0:n, t, :]),
                                  ("d_kidx", rows[0:n, t % 2, 640:704])):
                    sp.dma_start(out(name), src).then_inc(stored[t % 2], 16)
            sp.wait_ge(stored[0], 16 * 5 * 5)
            sp.wait_ge(stored[1], 16 * 5 * 4)


def odd_attention(m):
    nc, io = m.nc, m.io
    w = m.odd_work
    take = {}

    def room(name, n):
        nonlocal w
        take[name] = m.arena[:, w:w + n]
        w += n

    room("q", 256)
    room("qi", 1024)
    room("small", 128)
    room("logits", 2 * LS)
    masks = CONST["strict"][0]
    take["pt"] = m.const[:, masks:masks + (NPT + 1) * 128]
    room("dist", LS)
    assert w <= m.limit, w
    p = m.p
    spare = p[:, 8:12, :].rearrange("p k t -> p (k t)")
    kt_s = spare[:, 0:LS]
    v_s = spare[:, LS:LS + (NPT + 1) * 128].rearrange("p (t c) -> p t c", t=NPT + 1)
    index = p[:, 22:24, :].rearrange("p k t -> p (k t)")
    cache_rows = m.vn[:, 0:4, :].rearrange("p t c -> p (t c)").rearrange("p (t c) -> p t c", t=NPT)
    q = take["q"].rearrange("p (m q) -> p m q", m=2)
    qi = take["qi"].rearrange("p (h q) -> p h q", h=8)
    logits = take["logits"].rearrange("p (m k) -> p m k", m=2)
    relu = take["logits"][:, 0:2048].rearrange("p (s k) -> p s k", s=4)
    pt = take["pt"].rearrange("p (t q) -> p t q", t=NPT + 1)
    dist = take["dist"]
    small = take["small"]
    idle = m.om[:, 5:6]
    top, low, total, inv, best = (small[:, 8 * n:8 * n + 8] for n in range(5))
    on = m.arena[:, w:w + 128]
    assert w + 128 <= m.limit, w

    made, read = nc.alloc_semaphore("scores_made"), nc.alloc_semaphore("scores_read")
    turned, moved = nc.alloc_semaphore("probs_turned"), nc.alloc_semaphore("probs_moved")
    topk = nc.alloc_semaphore("topk_steps")
    P = Steps(nc, "o_pe", ["out0", "out1", "turn"])
    V = Steps(nc, "o_dve", ["pen0", "max0", "low0", "pen1", "max1", "low1", "inv", "part", "norm"])
    A = Steps(nc, "o_act", ["q", "exp0", "exp1", "turned"])
    dist_loaded = nc.alloc_semaphore("dist_loaded")
    cleared = nc.alloc_semaphore("o_cleared")

    with nc.Block() as block:

        @block.gpsimd
        def _(pool):
            nc.gpsimd.memset(take["q"], 0.0)
            nc.gpsimd.memset(take["qi"], 0.0).then_inc(cleared, 1)

        @block.sync
        def _(sp):
            sp.dma_start(dist[:, 0:TP], io["consts"][:, CONST["distP"][0]:CONST["distP"][0] + TP])\
              .then_inc(dist_loaded, 16)
            sp.wait_ge(dist_loaded, 16)

    class Queries:
        pass

    count = {"round": 0, "made": 0, "turned": 0, "C": 0}

    def count_on(name, n):
        count[name] += n
        return count[name] - n

    def queries(qt, kind):
        t = Queries()
        t.kind, t.qt = kind, qt
        t.sample = qt == NQ
        t.n = TS if t.sample else 128
        t.cols = slice(qt * 128, qt * 128 + t.n)
        t.nk = LS if t.sample else (qt + 1) * 128
        t.pieces = [(h, b, min(512, t.nk - b)) for h in range(2) for b in range(0, t.nk, 512)]
        tiles = -(-t.nk // 128)
        cuts = list(range(0, tiles, 4)) + [tiles]
        if t.sample:
            cuts[-2] -= 1
        t.groups = list(zip(cuts, cuts[1:]))
        t.width = 128 if kind == "C" else 64
        t.penal = kind == "D" and t.nk > TOPK
        t.qtile = 0 if kind == "C" else 12
        t.load = t.sample and kind == "C"
        t.ahead = 4 if t.load else 0
        t.per = 2 * len(t.groups) + t.ahead
        t.round, t.made, t.turned = count_on("round", 4), count_on("made", 4 * len(t.pieces)), \
            count_on("turned", 4 * t.per)
        if kind == "C":
            t.c = count_on("C", 4)
        first = 0 if t.sample else TP - 128 - qt * 128
        t.dist = dist[:, first:first + t.nk]
        return t

    def flat(ap):
        return ap.rearrange("p a t -> p (a t)")

    def keys_of(t, i):
        if t.sample:
            return kt_s
        return flat(p[:, ds(i + 4, 1), :]) if t.kind == "C" else p[:, 20, :]

    def values_of(t, i, h, kt, k):
        if t.kind == "C":
            return v_s[0:k, kt, :] if t.sample else m.vn[0:k, kt, ds(i * 128, 128)]
        rows = v_s if t.sample else m.vd
        return rows[0:k, kt, 64 * h:64 * h + 64]

    def pair_tensor(pe, t, i):
        r = i + t.round
        if t.load:
            turn_cache_tensor(pe, i, i * t.per + t.turned)
        pe.wait_ge(A.sem, A.done(r, "q"))
        for c, (h, b, n) in enumerate(t.pieces):
            if c >= 4:
                pe.wait_ge(read, i * len(t.pieces) + (t.made + c - 3))
            nc.tensor.matmul(m.ps[:, (c % 4) * 512:(c % 4) * 512 + n], q[:, h, :],
                             keys_of(t, i)[:, b:b + n], start=True, stop=True).then_inc(made, 1)
        for h in range(2):
            pe.wait_ge(A.sem, A.done(r, f"exp{h}"))
            for j, (a, z) in enumerate(t.groups):
                local = t.ahead + h * len(t.groups) + j
                if t.turned + local >= 2:
                    pe.wait_ge(moved, i * t.per + (t.turned + local - 1))
                for kt in range(a, z):
                    k = min(128, t.nk - kt * 128)
                    last = nc.tensor.transpose(
                        bank(m, 4 + local % 2)[0:k, (kt - a) * 128:(kt - a) * 128 + 128],
                        logits[:, h, kt * 128:kt * 128 + k], m.c("ident"))
                last.then_inc(turned, 1)
            for j, (a, z) in enumerate(t.groups):
                pe.wait_ge(moved, i * t.per + (t.turned + t.ahead + h * len(t.groups) + j + 1))
                for kt in range(a, z):
                    k = min(128, t.nk - kt * 128)
                    last = nc.tensor.matmul(bank(m, 6)[:, h * t.width:(h + 1) * t.width], pt[0:k, kt, :],
                                            values_of(t, i, h, kt, k), start=(kt == 0),
                                            stop=(kt == t.groups[-1][1] - 1))
            last.then_inc(*P.step(f"out{h}"))
        pe.wait_ge(V.sem, V.done(r, "norm"))
        nc.tensor.transpose(bank(m, 7)[:, 0:128], on, m.c("ident")).then_inc(*P.step("turn"))

    def pair_scalar(act, t, i):
        r = i + t.round
        if t.load:
            turn_cache_scalar(act, t, i, i * t.per + t.turned)
        src = flat(p[:, ds(i + t.qtile, 1), t.cols])
        for h in range(2):
            half = slice(64 * h, 64 * h + 64)
            last = nc.scalar.activation(q[half, h, 0:t.n], src[half], ACT.Copy, scale=SCALE)
        last.then_inc(*A.step("q"))
        for h in range(2):
            act.wait_ge(V.sem, V.done(r, f"low{h}"))
            nc.scalar.activation(logits[:, h, 0:t.nk], logits[:, h, 0:t.nk], ACT.Exp, bias=low[:, h:h + 1],
                                 accum_out=total[:, h:h + 1]).then_inc(*A.step(f"exp{h}"))
        for h in range(2):
            for j, (a, z) in enumerate(t.groups):
                local = t.ahead + h * len(t.groups) + j
                act.wait_ge(turned, i * t.per + (t.turned + local + 1))
                if h == 1 and j == 0:
                    act.wait_ge(P.sem, P.done(r, "out0"))
                full = min(z, t.nk // 128)
                src = bank(m, 4 + local % 2).rearrange("p (t q) -> p t q", t=4)
                if full > a:
                    last = nc.scalar.activation(pt[:, a:full, :], src[:, 0:full - a, :], ACT.Copy)
                if full < z:
                    last = nc.scalar.activation(pt[0:TS, full:z, :], src[0:TS, full - a:z - a, :], ACT.Copy)
                last.then_inc(moved, 1)
        act.wait_ge(P.sem, P.done(r, "turn"))
        nc.scalar.activation(idle, idle, ACT.Copy)
        nc.scalar.activation(flat(p[:, ds(i + t.qtile, 1), t.cols]), bank(m, 7)[:, 0:t.n], ACT.Copy)\
            .then_inc(*A.step("turned"))

    def pair_vector(dve, t, i):
        r = i + t.round
        per = len(t.pieces)
        for h in range(2):
            slope = m.c("slopeC")[:, ds(i, 1)] if t.kind == "C" else m.c("slopeD")[:, ds(i + 4 * h, 1)]
            for c, (_, b, n) in enumerate(t.pieces):
                if c // (per // 2) != h:
                    continue
                dve.wait_ge(made, i * per + (t.made + c + 1))
                nc.vector.scalar_tensor_tensor(
                    out=logits[:, h, b:b + n], in0=t.dist[:, b:b + n], scalar=slope,
                    in1=m.ps[:, (c % 4) * 512:(c % 4) * 512 + n], op0=ALU.mult, op1=ALU.add).then_inc(read, 1)
            dve.wait_ge(read, i * per + (t.made + (per // 2) * (h + 1)))
            all_keys = logits[:, h, 0:t.nk]
            if t.penal:
                nc.vector.tensor_tensor(all_keys, all_keys, index[:, 0:t.nk], ALU.add).then_inc(*V.step(f"pen{h}"))
            else:
                nc.vector.memset(small[:, 120:121], 0.0).then_inc(*V.step(f"pen{h}"))
            dve.wait_ge(V.sem, V.done(r, f"pen{h}"))
            nc.vector.tensor_reduce(top[:, h:h + 1], all_keys, AX.X, ALU.max).then_inc(*V.step(f"max{h}"))
            dve.wait_ge(V.sem, V.done(r, f"max{h}"))
            nc.vector.tensor_scalar(low[:, h:h + 1], top[:, h:h + 1], -1.0, None, ALU.mult)\
                .then_inc(*V.step(f"low{h}"))
        dve.wait_ge(A.sem, A.done(r, "exp1"))
        nc.vector.reciprocal(inv[:, 0:2], total[:, 0:2]).then_inc(*V.step("inv"))
        dve.wait_ge(V.sem, V.done(r, "inv"))
        if t.kind == "C":
            nc.vector.tensor_scalar(inv[:, 2:3], inv[:, 1:2], m.lam[:, 3:4], None, ALU.mult).then_inc(lam_used, 1)
            dve.wait_ge(lam_used, i + (t.c + 1))
        dve.wait_ge(P.sem, P.done(r, "out1"))
        o = bank(m, 6)
        if t.kind == "C":
            nc.vector.tensor_scalar(on, o[:, 0:128], inv[:, 0:1], None, ALU.mult).then_inc(*V.step("part"))
            dve.wait_ge(V.sem, V.done(r, "part"))
            nc.vector.scalar_tensor_tensor(out=on, in0=o[:, 128:256], scalar=inv[:, 2:3], in1=on,
                                           op0=ALU.mult, op1=ALU.add).then_inc(*V.step("norm"))
        else:
            nc.vector.tensor_scalar(on[:, 0:64], o[:, 0:64], inv[:, 0:1], None, ALU.mult).then_inc(*V.step("part"))
            nc.vector.tensor_scalar(on[:, 64:128], o[:, 64:128], inv[:, 1:2], None, ALU.mult)\
                .then_inc(*V.step("norm"))

    def turn_cache_tensor(pe, n, at):
        pe.wait_ge(loaded, n * 32 + 32)
        for j in range(4):
            if not isinstance(at, int) or at + j >= 2:
                pe.wait_ge(moved, at + (j - 1))
            for kt in range(4):
                last = nc.tensor.transpose(bank(m, 4 + j % 2)[:, kt * 128:kt * 128 + 128],
                                           cache_rows[:, 4 * j + kt, :], m.c("ident"))
            last.then_inc(turned, 1)
        pe.wait_ge(fresh, n + 1)

    def turn_cache_scalar(act, t, i, at, kind="C"):
        for j in range(4):
            act.wait_ge(turned, at + (j + 1))
            nc.scalar.activation(kt_s[:, 512 * j:512 * j + 512], bank(m, 4 + j % 2), ACT.Copy).then_inc(moved, 1)
        if kind == "C":
            new_k, new_v = flat(p[:, ds(i + 4, 1), TP:T]), m.vn[0:TS, 8, ds(i * 128, 128)]
        else:
            new_k, new_v = p[:, 21 if kind == "I" else 20, TP:T], m.vd[0:TS, 8, :]
        if kind != "I":
            nc.scalar.activation(v_s[0:TS, NPT, :], new_v, ACT.Copy)
        nc.scalar.activation(kt_s[:, PAST:LS], new_k, ACT.Copy).then_inc(fresh, 1)

    def index_tile(qt, number):
        t = queries_like(qt)
        t.number = number
        t.pieces = [(s, b, min(512, t.nk - b)) for s in range(8) for b in range(0, t.nk, 512)]
        t.base = count["index"]
        count["index"] += len(t.pieces)
        return t

    def queries_like(qt):
        t = Queries()
        t.qt, t.sample = qt, qt == NQ
        t.n = TS if t.sample else 128
        t.cols = slice(qt * 128, qt * 128 + t.n)
        t.nk = LS if t.sample else (qt + 1) * 128
        return t

    def index_tensor(pe, t):
        pe.wait_ge(index_q, t.number + 1)
        keys = kt_s if t.sample else p[:, 21, :]
        for c, (s, b, n) in enumerate(t.pieces):
            if c >= 4:
                pe.wait_ge(index_relu, t.base + c - 3)
            nc.tensor.matmul(m.ps[:, (c % 4) * 512:(c % 4) * 512 + n], qi[:, s, :], keys[:, b:b + n],
                             start=True, stop=True).then_inc(index_made, 1)
        pe.wait_ge(index_relu, t.base + len(t.pieces))

    def index_scalar(act, t):
        if t.number:
            act.wait_ge(index_made, t.base)
        nc.scalar.activation(qi[0:64, 0:4, 0:t.n], p[0:64, 16:20, t.cols], ACT.Copy)
        nc.scalar.activation(qi[64:128, 4:8, 0:t.n], p[64:128, 16:20, t.cols], ACT.Copy).then_inc(index_q, 1)
        for c, (s, b, n) in enumerate(t.pieces):
            act.wait_ge(index_made, t.base + c + 1)
            if t.base + c >= 4:
                act.wait_ge(index_read, t.base + c - 3)
            nc.scalar.activation(relu[:, c % 4, 0:n], m.ps[:, (c % 4) * 512:(c % 4) * 512 + n], ACT.Relu)\
                .then_inc(index_relu, 1)

    def index_vector(dve, t):
        blocks = len(t.pieces) // 8
        for c, (s, b, n) in enumerate(t.pieces):
            dve.wait_ge(index_relu, t.base + c + 1)
            head = 2 * (s % 4) + s // 4
            wt = m.wn[:, t.qt, head:head + 1]
            if s == 0:
                nc.vector.tensor_scalar(index[:, b:b + n], relu[:, c % 4, 0:n], wt, None, ALU.mult)\
                    .then_inc(index_read, 1)
            else:
                dve.wait_ge(index_read, t.base + c + 1 - blocks)
                nc.vector.scalar_tensor_tensor(out=index[:, b:b + n], in0=relu[:, c % 4, 0:n], scalar=wt,
                                               in1=index[:, b:b + n], op0=ALU.mult, op1=ALU.add)\
                    .then_inc(index_read, 1)
        dve.wait_ge(index_read, t.base + len(t.pieces))
        if not t.sample:
            nc.vector.memset(index[0:64, t.nk - 64:t.nk], -FAR).then_inc(corner, 1)
            dve.wait_ge(corner, t.number + 1)
        steps = 2 * (TOPK // 8)
        with dve.Fori(0, TOPK // 8) as i:
            nc.vector.max(best, index[:, 0:t.nk]).then_inc(topk, 1)
            dve.wait_ge(topk, i * 2 + (t.number * steps + 1))
            nc.vector.memset(small[:, 120:121], 0.0)
            nc.vector.match_replace(index[:, 0:t.nk], best, index[:, 0:t.nk], TAKEN).then_inc(topk, 1)
            dve.wait_ge(topk, i * 2 + (t.number * steps + 2))
        nc.vector.tensor_scalar(index[:, 0:t.nk], index[:, 0:t.nk], TAKEN / 2, -FAR, ALU.is_gt, ALU.mult)\
            .then_inc(selected, 1)
        dve.wait_ge(selected, t.number + 1)

    loaded, fresh = nc.alloc_semaphore("cache_loaded"), nc.alloc_semaphore("cache_fresh")
    index_q, index_made, index_relu, index_read = (
        nc.alloc_semaphore(f"index_{n}") for n in ("queries", "made", "relu", "read"))
    corner, selected, lam_used = (nc.alloc_semaphore(n) for n in ("index_corner", "index_selected", "lambda_used"))
    count["index"] = 0

    plan = []
    number = 0
    for qt in range(NQ):
        if (qt + 1) * 128 > TOPK:
            plan.append(("index", index_tile(qt, number)))
            number += 1
        plan.append(("pairs", queries(qt, "C")))
        plan.append(("pairs", queries(qt, "D")))
    plan.append(("pairs", queries(NQ, "C")))
    plan.append(("cache", ("I", 4, count_on("turned", 4))))
    plan.append(("index", index_tile(NQ, number)))
    plan.append(("cache", ("D", 5, count_on("turned", 4))))
    plan.append(("pairs", queries(NQ, "D")))
    cache_sem_rounds = next(t for k, t in plan if k == "pairs" and t.load)
    last_index = [t for k, t in plan if k == "index"][-1]

    with nc.Block() as block:

        @block.tensor
        def _(pe):
            for kind, t in plan:
                if kind == "index":
                    index_tensor(pe, t)
                elif kind == "cache":
                    turn_cache_tensor(pe, t[1], t[2])
                else:
                    with pe.Fori(0, 4) as i:
                        pair_tensor(pe, t, i)

        @block.scalar
        def _(act):
            for kind, t in plan:
                if kind == "index":
                    index_scalar(act, t)
                elif kind == "cache":
                    turn_cache_scalar(act, None, None, t[2], t[0])
                else:
                    with act.Fori(0, 4) as i:
                        pair_scalar(act, t, i)

        @block.vector
        def _(dve):
            dve.wait_ge(dist_loaded, 16)
            for kind, t in plan:
                if kind == "index":
                    index_vector(dve, t)
                elif kind == "pairs":
                    if t.load:
                        dve.wait_ge(dist_loaded, 32)
                    with dve.Fori(0, 4) as i:
                        pair_vector(dve, t, i)

        @block.sync
        def _(sp):
            base = cache_sem_rounds.round
            ck = io["cache_c_k"][0, 0].rearrange("(t p) h m d -> p t (h m d)", p=128)
            cv = io["cache_c_v"][0, 0].rearrange("(t p) h e -> p t (h e)", p=128)
            sp.wait_ge(V.sem, V.done(base - 1, "low1"))
            sp.dma_start(dist, io["consts"][:, CONST["distS"][0]:CONST["distS"][0] + LS]).then_inc(dist_loaded, 16)
            with sp.Fori(0, 4) as i:
                sp.wait_ge(P.sem, P.done(i + (base - 1), "out1"))
                sp.dma_start(cache_rows, ck[:, :, ds(i * 128, 128)]).then_inc(loaded, 16)
                sp.dma_start(v_s[:, 0:NPT, :], cv[:, :, ds(i * 128, 128)]).then_inc(loaded, 16)
            sp.wait_ge(P.sem, P.done(base + 3, "out1"))
            ki = io["cache_d_kidx"][0, 0].rearrange("(t p) d -> p t d", p=128)
            for h in range(2):
                sp.dma_start(cache_rows[:, :, 64 * h:64 * h + 64], ki).then_inc(loaded, 16)
            sp.wait_ge(index_made, last_index.base + len(last_index.pieces))
            sp.dma_start(cache_rows, io["cache_d_k"][0, 0].rearrange("(t p) g d -> p t (g d)", p=128))\
              .then_inc(loaded, 16)
            sp.dma_start(v_s[:, 0:NPT, :], io["cache_d_v"][0, 0].rearrange("(t p) g d -> p t (g d)", p=128))\
              .then_inc(loaded, 16)


def diff_finish(m):
    nc = m.nc
    w = m.odd_work
    sq, rstd = (m.arena[:, w + n * T:w + n * T + T] for n in range(2))
    gain = m.arena[:, w + 2 * T:w + 2 * T + 129]
    ones = gain[:, 1:129]
    P, V, A = Steps(nc, "f_pe", ["sum"]), Steps(nc, "f_dve", ["rstd", "normal"]), Steps(nc, "f_act", ["sq", "std"])
    ready = nc.alloc_semaphore("f_ready")
    with nc.Block() as block:

        @block.tensor
        def _(pe):
            pe.wait_ge(ready, 1)
            for h in range(4):
                pe.wait_ge(A.sem, A.done(h, "sq"))
                for b in range(4):
                    last = nc.tensor.matmul(m.ps[:, b * 512:b * 512 + TB], ones, sq[:, b * TB:(b + 1) * TB],
                                            start=True, stop=True)
                last.then_inc(*P.step("sum"))

        @block.scalar
        def _(act):
            for h in range(4):
                nc.scalar.activation(sq, m.p[:, h, :], ACT.Square).then_inc(*A.step("sq"))
                act.wait_ge(P.sem, P.done(h, "sum"))
                if h:
                    act.wait_ge(V.sem, V.done(h - 1, "normal"))
                nc.scalar.activation(blocks4(rstd), linear_out(m, 0), ACT.Sqrt, bias=m.eps(0)).then_inc(*A.step("std"))

        @block.vector
        def _(dve):
            nc.vector.memset(ones, 1.0 / 128)
            nc.vector.tensor_scalar(gain[:, 0:1], m.col(ROWS["subln"]), 1.0 - LAM_INIT, None, ALU.mult)\
                .then_inc(ready, 1)
            dve.wait_ge(ready, 1)
            for h in range(4):
                dve.wait_ge(A.sem, A.done(h, "std"))
                nc.vector.reciprocal(rstd, rstd).then_inc(*V.step("rstd"))
                dve.wait_ge(V.sem, V.done(h, "rstd"))
                nc.vector.scalar_tensor_tensor(out=m.p[:, h, :], in0=m.p[:, h, :], scalar=gain[:, 0:1], in1=rstd,
                                               op0=ALU.mult, op1=ALU.mult).then_inc(*V.step("normal"))


def store(m):
    nc, io = m.nc, m.io
    rows = m.arena[:, m.work:m.work + 2 * D].rearrange("p (s d) -> p s d", s=2)
    turned, moved = nc.alloc_semaphore("y_turned"), nc.alloc_semaphore("y_moved")
    stored = [nc.alloc_semaphore(f"y_stored{s}") for s in range(2)]
    with nc.Block() as block:

        @block.tensor
        def _(pe):
            for t in range(9):
                n = 128 if t < 8 else TS
                if t >= 2:
                    pe.wait_ge(moved, t - 1)
                for k in range(8):
                    at = (t % 2) * 1024 + k * 128
                    last = nc.tensor.transpose(m.ps[0:n, at:at + 128], m.x[:, k, t * 128:t * 128 + n], m.c("ident"))
                last.then_inc(turned, 1)

        @block.vector
        def _(dve):
            for t in range(9):
                n = 128 if t < 8 else TS
                dve.wait_ge(turned, t + 1)
                if t >= 2:
                    dve.wait_ge(stored[t % 2], 16 * (t // 2))
                nc.vector.tensor_copy(rows[0:n, t % 2, :], m.ps[0:n, (t % 2) * 1024:(t % 2) * 1024 + 1024])\
                    .then_inc(moved, 1)

        @block.sync
        def _(sp):
            for t in range(9):
                sp.wait_ge(moved, t + 1)
                out = io["y_prompt"][0, t * 128:t * 128 + 128] if t < 8 else io["y_sample"][0]
                sp.dma_start(out, rows[0:128 if t < 8 else TS, t % 2, :]).then_inc(stored[t % 2], 16)
            sp.wait_ge(stored[0], 16 * 5)
            sp.wait_ge(stored[1], 16 * 4)


def build(nc, io, until=99):
    m = Core()
    m.nc, m.io = nc, io
    columns = 53200
    m.arena = nc.alloc_sbuf_tensor("arena", [128, columns], F32)
    m.ps = nc.alloc_psum_tensor("psum", [128, 4096], F32)
    at = [0]

    def room(n):
        at[0] += n
        return m.arena[:, at[0] - n:at[0]]

    m.nconst = CONST["distP"][0]
    m.const = room(m.nconst)
    m.cols = room(128)
    m.sink = room(8)
    m.lam_in = room(256).rearrange("p (v d) -> p v d", v=4)
    m.lam = room(8)
    m.om = room(8)
    m.c = lambda name: m.const[:, CONST[name][0]:CONST[name][0] + CONST[name][1]]
    m.eps = lambda n: m.c("eps")[:, n:n + 1]
    m.col = lambda n: m.cols[:, n:n + 1]
    m.x = room(KD * T).rearrange("p (k t) -> p k t", k=KD)
    after_x = at[0]
    m.limit = columns
    m.work = after_x
    start(m)

    m.p = m.arena[:, after_x:after_x + 21 * T].rearrange("p (k t) -> p k t", k=21)
    m.work = after_x + 21 * T
    m.ring = m.work
    project_even(m)
    window_attention(m)
    m.state = m.arena[:, m.work:m.work + 512]
    m.work += 512
    rwkv_prepare(m)
    rwkv_chunks(m)
    rwkv_finish(m)
    m.ring = m.work
    project_out(m, "out0", io["w_out_even"][0], [m.p[:, k, :] for k in range(8)], 0)
    layer_norm(m, "ln0", ROWS["mixg"], ROWS["mixb"])
    m.work = after_x
    mlp(m, 0)
    layer_norm(m, "ln1", ROWS["ffng"], ROWS["ffnb"])
    m.p = m.arena[:, after_x:after_x + 24 * T].rearrange("p (k t) -> p k t", k=24)
    m.work = after_x + 24 * T
    m.ring = m.work
    project_odd(m)
    turn_rows(m)
    odd_attention(m)
    diff_finish(m)
    m.ring = m.work
    project_out(m, "out1", io["w_out_odd"][0], [m.p[:, k, :] for k in (0, 1, 2, 3, 12, 13, 14, 15)], 4)
    layer_norm(m, "ln2", ROWS["mixg"] + 8, ROWS["mixb"] + 8)
    m.work = after_x
    mlp(m, 1)
    layer_norm(m, "ln3", ROWS["ffng"] + 8, ROWS["ffnb"] + 8)
    store(m)


_INS = ["x_prompt", "x_sample", "cache_a_k", "cache_a_v", "state_b_shift", "state_b_wkv", "cache_c_k", "cache_c_v",
        "cache_d_k", "cache_d_v", "cache_d_kidx", "w_in_even", "sink_a", "mu_b", "w0_b", "w_up_b", "a0_b", "a_up_b",
        "g_up_b", "k_k_b", "k_a_b", "r_k_b", "lnx_g_b", "lnx_b_b", "w_out_even", "w_in_odd", "lam_q1_c", "lam_k1_c",
        "lam_q2_c", "lam_k2_c", "subln_g_c", "w_out_odd", "ln_mix_g", "ln_mix_b", "ln_ffn_g", "ln_ffn_b",
        "w_ff_up", "w_ff_down"]
_OUTS = [("y_prompt", (1, TP, D)), ("y_sample", (1, TS, D)),
         ("a_k_p", (1, 1, 128, 2, HD)), ("a_v_p", (1, 1, 128, 2, HD)), ("b_shift_p", (1, 1, 1, 1792)),
         ("b_wkv_p", (1, 1, 8, HD, HD)), ("c_k_p", (1, 1, TP, 4, 2, HD)), ("c_v_p", (1, 1, TP, 4, 128)),
         ("d_k_p", (1, 1, TP, 2, HD)), ("d_v_p", (1, 1, TP, 2, HD)), ("d_kidx_p", (1, 1, TP, HD)),
         ("a_k_s", (1, 1, 128, 2, HD)), ("a_v_s", (1, 1, 128, 2, HD)), ("b_shift_s", (1, 1, 1, 1792)),
         ("b_wkv_s", (1, 1, 8, HD, HD)), ("c_k_s", (1, 1, TS, 4, 2, HD)), ("c_v_s", (1, 1, TS, 4, 128)),
         ("d_k_s", (1, 1, TS, 2, HD)), ("d_v_s", (1, 1, TS, 2, HD)), ("d_kidx_s", (1, 1, TS, HD))]


def kernel(**inputs):
    import concourse.bacc as _bacc
    from concourse.bass_utils import run_bass_kernel_spmd as _run

    nc = _bacc.Bacc("TRN2", target_bir_lowering=False, num_devices=1)
    arrays, io = {}, {}
    for name in _INS:
        a = np.ascontiguousarray(inputs[name])
        arrays[f"in_{name}"] = a
        io[name] = nc.dram_tensor(f"in_{name}", a.shape, F32, kind="ExternalInput").ap()
    arrays["in_consts"] = constants()
    io["consts"] = nc.dram_tensor("in_consts", (128, NCONST), F32, kind="ExternalInput").ap()
    for name, shape in _OUTS:
        io[name] = nc.dram_tensor(f"out_{name}", shape, F32, kind="ExternalOutput").ap()
    build(nc, io)
    r = _run(nc, [arrays], core_ids=[0])
    return tuple(r.results[0][f"out_{name}"] for name, _ in _OUTS)
```

```python
import math

import numpy as np
import concourse.bass as bass
from concourse import mybir

F32 = mybir.dt.float32
F32R = mybir.dt.float32r
F16 = mybir.dt.float16
BF16 = mybir.dt.bfloat16
ALU = mybir.AluOpType
ACT = mybir.ActivationFunctionType
AX = mybir.AxisListType

D = 1024
KD = D // 128
TP = 1024
TS = 64
T = TP + TS
TB = T // 4
NQ = TP // 128
PAST = 2048
LS = PAST + TS
NPT = PAST // 128
CH = 64
HD = 64
NCHUNK = TP // CH
FF = 4096
ALPHA = 4 ** 0.25
LN_EPS = 1e-5
GN_EPS = 64e-5
DECAY = math.exp(-0.5)
LAM_INIT = 0.8 - 0.6 * math.exp(-0.3)
TOPK = 256
SCALE = HD ** -0.5
FAR = 1e30
TAKEN = -3e38

ROWS = {}
_at = 0
for _n, _c in (("mu", 14), ("w0", 4), ("a0", 4), ("kk", 4), ("ka", 4), ("rk", 4), ("lnxg", 4), ("lnxb", 4),
               ("mixg", 16), ("mixb", 16), ("ffng", 16), ("ffnb", 16), ("subln", 1), ("shift", 14)):
    ROWS[_n] = _at
    _at += _c
NROWS = _at

CONST = {}
_at = 0
for _n, _c in (("ident", 128), ("mean", 128), ("heads", 128), ("slopeC", 4), ("slopeD", 8), ("eps", 3),
               ("strict", 128), ("upto", 128), ("low1", 128), ("up1", 128), ("low2", 128), ("low4", 128),
               ("low8", 128), ("low16", 128), ("low32", 128), ("reset", T), ("distA", 256),
               ("distP", TP), ("distS", LS), ("corner", 128), ("both", 128)):
    CONST[_n] = (_at, _c)
    _at += _c
NCONST = _at


def constants():
    c = np.zeros((128, NCONST), np.float32)

    def put(name, a):
        o, n = CONST[name]
        c[:, o:o + n] = a

    i = np.arange(128)
    p, q = i[:, None], i[None, :]
    same = (p // 64) == (q // 64)
    put("ident", p == q)
    put("mean", 1.0 / D)
    put("heads", same)
    put("slopeC", -2.0 ** (-8.0 * np.arange(1, 5) / 4)[None, :])
    put("slopeD", -2.0 ** (-8.0 * np.arange(1, 9) / 8)[None, :])
    put("eps", np.array([LN_EPS, 1e-12, GN_EPS])[None, :])
    put("strict", same & (p < q))
    put("upto", same & (p <= q))
    for n in (1, 2, 4, 8, 16, 32):
        low = (p // (2 * n) == q // (2 * n)) & (p // n > q // n)
        put(f"low{n}", low)
        if n == 1:
            put("up1", low.T)
    put("reset", (np.arange(T) % CH != 0)[None, :])
    x = np.arange(256)[None, :]
    dist = np.abs(p + 128 - x).astype(np.float64)
    put("distA", np.where(np.where(p < 64, x < 192, x >= 64), dist, FAR))
    x = np.arange(TP)[None, :]
    dist = np.abs(p + TP - 128 - x).astype(np.float64)
    put("distP", dist)
    put("corner", np.where((p < 64) & (q >= 64), -FAR, 0.0))
    put("both", p % 64 == q % 64)
    x = np.arange(LS)[None, :]
    put("distS", np.abs(p % 64 + PAST - x) - 1024)
    return c


class Steps:

    def __init__(self, nc, name, steps):
        self.sem, self.steps, self.at = nc.alloc_semaphore(name), list(steps), 0

    def step(self, name):
        assert self.steps[self.at % len(self.steps)] == name, (name, self.steps[self.at % len(self.steps)])
        self.at += 1
        return self.sem, 1

    def done(self, t, name):
        return t * len(self.steps) + self.steps.index(name) + 1

    def rounds(self, t):
        return t * len(self.steps)


def ds(start, n):
    return bass.ds(start, n) if not isinstance(start, int) else slice(start, start + n)


def repeat(engine, parts, body):
    for start, end in parts:
        if end - start == 1:
            body(start, start == 0)
        else:
            with engine.Fori(start, end) as i:
                body(i, False)


class Core:
    pass


def blocks4(ap):
    return ap.rearrange("p (b t) -> p b t", b=4)


def bank(m, b):
    return m.ps[:, b * 512:(b + 1) * 512]


def linear_out(m, buf):
    return m.ps[:, buf * 2048:(buf + 1) * 2048].rearrange("p (b t) -> p b t", b=4)[:, :, 0:TB]


def heads4(ap):
    return ap.rearrange("p (h c) -> p h c", h=4)


SLOTS = 4
HIGHS = 2
RING = (SLOTS + HIGHS) * 1024


def rounded(m, ap):
    size = math.prod(ap.shape[1:])
    key = (ap.offset, size)
    if key not in m.rounded:
        m.rounded[key] = m.nc.alloc_sbuf_tensor_at(f"rounded_{ap.offset}_{size}", [128, size], F32R,
                                                   offset=m.arena_at + 4 * ap.offset)
    whole = m.rounded[key][:, 0:size]
    return whole if len(ap.shape) == 2 else whole.rearrange("p (k c) -> p k c", k=ap.shape[1])


class Ring:

    def __init__(self, m):
        nc, self.m = m.nc, m
        self.loaded = [nc.alloc_semaphore(f"weights_loaded{s}") for s in range(SLOTS)]
        self.weights_high = nc.alloc_semaphore("weights_high")
        self.weights_split = nc.alloc_semaphore("weights_split")
        self.used = nc.alloc_semaphore("weights_used")
        self.freed = nc.alloc_semaphore("linear_freed")
        self.x_high, self.x_split = nc.alloc_semaphore("operand_high"), nc.alloc_semaphore("operand_split")
        self.next = (0, 0, 0, 0)

    def begin(self, at, ndma, pieces, tiles):
        self.pieces, self.loads, self.operands, self.tiles = self.next
        self.ndma = ndma
        self.next = (self.pieces + pieces, self.loads + pieces // SLOTS * ndma * 16,
                     self.operands + 8, self.tiles + tiles)
        arena = self.m.arena
        self.low = arena[:, at:at + SLOTS * 1024].rearrange("p (s k c) -> p s k c", s=SLOTS, k=8)
        self.high = arena[:, at + SLOTS * 1024:at + RING].rearrange("p (s k c) -> p s k c", s=HIGHS, k=8)
        return self

    def load(self, sp, at, u, first, pairs):
        if not first or u >= SLOTS:
            sp.wait_ge(self.used, at + (self.pieces + u + 1 - SLOTS))
        for dst, src in pairs(self.low[:, u % SLOTS]):
            sp.dma_start(dst, src).then_inc(self.loaded[u % SLOTS], 16)

    def split(self, dve, at, fills, u, first):
        nc, m = self.m.nc, self.m
        low, high = self.low[:, u % SLOTS], self.high[:, u % HIGHS]
        dve.wait_ge(self.loaded[u % SLOTS], fills * 16 * self.ndma + (self.loads + (u // SLOTS + 1) * 16 * self.ndma))
        if not first or u >= HIGHS:
            dve.wait_ge(self.used, at + (self.pieces + u + 1 - HIGHS))
        nc.vector.tensor_copy(rounded(m, high), low).then_inc(self.weights_high, 1)
        dve.wait_ge(self.weights_high, at + (self.pieces + u + 1))
        nc.vector.tensor_tensor(rounded(m, low), low, rounded(m, high), ALU.subtract).then_inc(self.weights_split, 1)

    def multiply(self, pe, at, u, x_high, x_low, ready=None):
        nc, m = self.m.nc, self.m
        pe.wait_ge(self.weights_split, at + (self.pieces + u + 1))
        low, high = self.low[:, u % SLOTS], self.high[:, u % HIGHS]
        for k in range(8):
            if ready:
                ready(k)
            terms = ((low, x_high), (high, x_low), (high, x_high))
            for n, (w, x) in enumerate(terms):
                for b in range(4):
                    out = (u % 2) * 2048 + b * 512
                    last = nc.tensor.matmul(
                        m.ps[:, out:out + TB], rounded(m, w)[:, k, :], rounded(m, x(k))[:, b * TB:(b + 1) * TB],
                        start=(k == 0 and n == 0), stop=(k == 7 and n == 2), skip_group_check=True)
        last.then_inc(self.used, 1)


def linear(m, name, tiles, loads, ndma, parts, operand, evacuate, on_vector=False):
    nc = m.nc
    per = 4
    rounds = tiles // per
    ring = m.linears.begin(m.ring, ndma, tiles, tiles)
    high = m.high.rearrange("p (k t) -> p k t", k=8)
    with nc.Block() as block:

        @block.sync
        def _(sp):
            def fill(i, first):
                for u in range(per):
                    ring.load(sp, i * per, u, first, lambda slot: loads(i, u, slot))

            repeat(sp, parts, fill)

        @block.tensor
        def _(pe):
            def multiply(i, first):
                for u in range(per):
                    if not first or u >= 2:
                        pe.wait_ge(ring.freed, i * per + (ring.tiles + u - 1))
                    ready = (lambda k: pe.wait_ge(ring.x_split, ring.operands + k + 1)) if first and u == 0 else None
                    ring.multiply(pe, i * per, u, lambda k: high[:, k, :], operand, ready)

            repeat(pe, [(0, 1), (1, rounds)], multiply)

        def leave(engine, i, u):
            engine.wait_ge(ring.used, i * per + (ring.pieces + u + 1))
            evacuate(engine, i * per + u, linear_out(m, u % 2)).then_inc(ring.freed, 1)

        @block.scalar
        def _(act):
            for k in range(8):
                nc.scalar.activation(rounded(m, high[:, k, :]), operand(k), ACT.Copy).then_inc(ring.x_high, 1)
            if not on_vector:
                repeat(act, [(0, 1), (1, rounds)], lambda i, first: [leave(act, i, u) for u in range(per)])

        @block.vector
        def _(dve):
            def body(i, first):
                for u in range(per):
                    ring.split(dve, i * per, i, u, first)
                    if first and u == 0:
                        for k in range(8):
                            dve.wait_ge(ring.x_high, ring.operands + k + 1)
                            nc.vector.tensor_tensor(rounded(m, operand(k)), operand(k), rounded(m, high[:, k, :]),
                                                    ALU.subtract)\
                                .then_inc(ring.x_split, 1)
                    if on_vector and not (first and u == 0):
                        if u:
                            leave(dve, i, u - 1)
                        else:
                            leave(dve, i - 1, per - 1)

            repeat(dve, [(0, 1), (1, rounds)], body)
            if on_vector:
                leave(dve, rounds - 1, per - 1)


def join(m, pool, joined):
    high = m.high.rearrange("p (k t) -> p k t", k=8)
    for k in range(8):
        m.nc.gpsimd.tensor_tensor(m.x[:, k, :], rounded(m, m.x[:, k, :]), rounded(m, high[:, k, :]), ALU.add)\
            .then_inc(joined, 1)


def weight_view(w):
    return w.rearrange("(k p) c -> p k c", p=128)


def halves(slot, src):
    return [(slot[:, 0:4], src[:, 0:4]), (slot[:, 4:8], src[:, 4:8])]


def grouped_columns(slot, w, base, a):
    return [(slot[:, :, 64 * g:64 * g + 64], w[:, :, base + 256 * g + 64 * a:base + 256 * g + 64 * a + 64])
            for g in range(2)]


def project_even(m):
    w = weight_view(m.io["w_in_even"][0])

    def loads(i, u, slot):
        if isinstance(i, int) and i == 0:
            return grouped_columns(slot, w, 0, u)
        if isinstance(i, int):
            at = (512, 640, 2304, 2432)[u]
            return halves(slot, w[:, :, at:at + 128])
        return halves(slot, w[:, :, ds(i * 512 + (256 + 128 * u), 128)])

    def evacuate(act, tile, out):
        return m.nc.scalar.activation(blocks4(tile_of(m.p, tile)), out, ACT.Copy)

    linear(m, "in0", 20, loads, 2, [(0, 1), (1, 4), (4, 5)], lambda k: m.x[:, k, :], evacuate)


def tile_of(p, tile):
    if isinstance(tile, int):
        return p[:, tile, :]
    return p[:, ds(tile, 1), :].rearrange("p a t -> p (a t)")


def project_odd(m):
    w = weight_view(m.io["w_in_odd"][0])

    def loads(i, u, slot):
        if isinstance(i, int) and i == 3:
            return grouped_columns(slot, w, 1536, u)
        if isinstance(i, int) and i == 5:
            if u == 1:
                return [(slot[:, :, 0:64], w[:, :, 2816:2880]), (slot[:, :, 64:128], w[:, :, 2816:2880])]
            if u == 3:
                return [(slot[:, :, 0:8], w[:, :, 2880:2888]), (slot[:, :, 8:128], w[:, :, 0:120])]
            at = {0: 2048, 2: 2176}[u]
            return halves(slot, w[:, :, at:at + 128])
        if isinstance(i, int) and i == 4:
            return halves(slot, w[:, :, 2304 + 128 * u:2304 + 128 * u + 128])
        return halves(slot, w[:, :, ds(i * 512 + 128 * u, 128)])

    def evacuate(act, tile, out):
        return m.nc.scalar.activation(blocks4(tile_of(m.p, tile)), out, ACT.Copy)

    linear(m, "in1", 24, loads, 2, [(0, 1), (1, 3), (3, 4), (4, 5), (5, 6)], lambda k: m.x[:, k, :],
           evacuate)


def add_residual(m):
    def evacuate(dve, tile, out):
        x = blocks4(tile_of(m.x, tile))
        return m.nc.vector.scalar_tensor_tensor(out=x, in0=x, scalar=ALPHA, in1=out, op0=ALU.mult, op1=ALU.add)
    return evacuate


def project_out(m, name, w, mixed, grouped):
    rows = w.rearrange("(k p) c -> p k c", p=128)
    plain = 4 - grouped
    by_group = w[128 * grouped:128 * grouped + 512, :].rearrange("(g a d) c -> g d a c", g=2, a=4)

    def loads(i, u, slot):
        cols = ds(i * 512 + 128 * u, 128)
        return [(slot[0:64, grouped:grouped + 4], by_group[0][:, :, cols]),
                (slot[64:128, grouped:grouped + 4], by_group[1][:, :, cols]),
                (slot[:, plain:plain + 4], rows[:, plain:plain + 4, cols])]

    linear(m, name, 8, loads, 3, [(0, 1), (1, 2)], mixed, add_residual(m), on_vector=True)


def mlp(m, layer):
    nc = m.nc
    QUARTERS = FF // D
    up = weight_view(m.io["w_ff_up"][layer])
    down = m.io["w_ff_down"][layer].rearrange("(r p) c -> p r c", p=128)
    w = m.work
    m.acc, high, hidden, hidden_high = (m.arena[:, w + n * 8 * T:w + (n + 1) * 8 * T]
                                        .rearrange("p (k t) -> p k t", k=8) for n in range(4))
    assert w + 32 * T + RING <= m.limit
    ring = m.linears.begin(w + 32 * T, 2, 64, 0)
    relu, added, squared, hidden_rounded, hidden_split, scaled = m.mlp_sems
    had = layer * FF // 128
    scaled_before = layer * 8
    quarters = [(0, 1), (1, QUARTERS)]

    with nc.Block() as block:

        @block.sync
        def _(sp):
            def fill(q, first):
                for u in range(8):
                    ring.load(sp, q * 16, u, first,
                              lambda slot: halves(slot, up[:, :, ds(q * D + 128 * u, 128)]))
                for u in range(8):
                    ring.load(sp, q * 16, 8 + u, first,
                              lambda slot: halves(slot, down[:, ds(q * 8, 8), 128 * u:128 * u + 128]))

            repeat(sp, quarters, fill)

        @block.gpsimd
        def _(pool):
            for k in range(8):
                nc.gpsimd.tensor_scalar(m.acc[:, k, :], m.x[:, k, :], ALPHA, None, ALU.mult).then_inc(scaled, 1)

        @block.tensor
        def _(pe):
            def multiply(q, first):
                for u in range(8):
                    if u >= 2:
                        pe.wait_ge(relu, q * 8 + (had + u - 1))
                    elif not first:
                        pe.wait_ge(added, q * 8 + (had + u - 1))
                    ready = (lambda k: pe.wait_ge(ring.x_split, ring.operands + k + 1)) if first and u == 0 else None
                    ring.multiply(pe, q * 16, u, lambda k: high[:, k, :], lambda k: m.x[:, k, :], ready)
                for u in range(8):
                    if u >= 2:
                        pe.wait_ge(added, q * 8 + (had + u - 1))
                    else:
                        pe.wait_ge(relu, q * 8 + (had + 7 + u))
                    ready = (lambda k: pe.wait_ge(hidden_split, q * 8 + (had + k + 1))) if u == 0 else None
                    ring.multiply(pe, q * 16, 8 + u, lambda k: hidden_high[:, k, :], lambda k: hidden[:, k, :], ready)

            repeat(pe, quarters, multiply)

        @block.scalar
        def _(act):
            for k in range(8):
                nc.scalar.activation(rounded(m, high[:, k, :]), m.x[:, k, :], ACT.Copy).then_inc(ring.x_high, 1)

            def square(q, first):
                for u in range(8):
                    act.wait_ge(ring.used, q * 16 + (ring.pieces + u + 1))
                    nc.scalar.activation(blocks4(hidden[:, u, :]), linear_out(m, u % 2), ACT.Relu)\
                        .then_inc(relu, 1)
                    act.wait_ge(relu, q * 8 + (had + u + 1))
                    nc.scalar.activation(hidden[:, u, :], hidden[:, u, :], ACT.Square).then_inc(squared, 1)

            repeat(act, quarters, square)

        @block.vector
        def _(dve):
            def split_hidden(q, u):
                dve.wait_ge(squared, q * 8 + (had + u + 1))
                nc.vector.tensor_copy(rounded(m, hidden_high[:, u, :]), hidden[:, u, :]).then_inc(hidden_rounded, 1)
                dve.wait_ge(hidden_rounded, q * 8 + (had + u + 1))
                nc.vector.tensor_tensor(rounded(m, hidden[:, u, :]), hidden[:, u, :],
                                        rounded(m, hidden_high[:, u, :]),
                                        ALU.subtract).then_inc(hidden_split, 1)

            def add(q, u):
                dve.wait_ge(ring.used, q * 16 + (ring.pieces + 9 + u))
                acc = blocks4(m.acc[:, u, :])
                nc.vector.tensor_tensor(acc, acc, linear_out(m, u % 2), ALU.add).then_inc(added, 1)

            def body(q, first):
                for u in range(16):
                    ring.split(dve, q * 16, q * 4, u, first)
                    if first and u == 0:
                        for k in range(8):
                            dve.wait_ge(ring.x_high, ring.operands + k + 1)
                            dve.wait_ge(scaled, scaled_before + k + 1)
                            nc.vector.tensor_tensor(rounded(m, m.x[:, k, :]), m.x[:, k, :], rounded(m, high[:, k, :]),
                                                    ALU.subtract).then_inc(ring.x_split, 1)
                    if 1 <= u <= 8:
                        split_hidden(q, u - 1)
                    elif u:
                        add(q, u - 9)
                    elif not first:
                        add(q - 1, 7)

            repeat(dve, quarters, body)
            add(QUARTERS - 1, 7)


def layer_norm(m, name, gain, shift, source=None):
    nc = m.nc
    P = Steps(nc, f"{name}_pe", ["mean"] + [f"v{k}" for k in range(8)])
    V = Steps(nc, f"{name}_dve", [f"c{k}" for k in range(8)] + ["rstd"] + [f"n{k}" for k in range(8)])
    A = Steps(nc, f"{name}_act", [f"s{k}" for k in range(8)] + ["std"] + [f"g{k}" for k in range(8)])
    sq = m.arena[:, m.work:m.work + 2 * T].rearrange("p (s t) -> p s t", s=2)
    rstd = m.arena[:, m.work + 2 * T:m.work + 3 * T]
    source = m.x if source is None else source
    with nc.Block() as block:

        @block.tensor
        def _(pe):
            for b in range(4):
                for k in range(8):
                    last = nc.tensor.matmul(m.ps[:, b * 512:b * 512 + TB], m.c("mean"),
                                            source[:, k, b * TB:(b + 1) * TB], start=(k == 0), stop=(k == 7))
            last.then_inc(*P.step("mean"))
            for k in range(8):
                pe.wait_ge(A.sem, A.done(0, f"s{k}"))
                for b in range(4):
                    at = 2048 + b * 512
                    last = nc.tensor.matmul(m.ps[:, at:at + TB], m.c("mean"), sq[:, k % 2, b * TB:(b + 1) * TB],
                                            start=(k == 0), stop=(k == 7), skip_group_check=True)
                last.then_inc(*P.step(f"v{k}"))

        @block.vector
        def _(dve):
            dve.wait_ge(P.sem, P.done(0, "mean"))
            for k in range(8):
                nc.vector.tensor_tensor(blocks4(m.x[:, k, :]), blocks4(source[:, k, :]), linear_out(m, 0),
                                        ALU.subtract).then_inc(*V.step(f"c{k}"))
            dve.wait_ge(A.sem, A.done(0, "std"))
            nc.vector.reciprocal(rstd, rstd).then_inc(*V.step("rstd"))
            dve.wait_ge(V.sem, V.done(0, "rstd"))
            for k in range(8):
                nc.vector.tensor_tensor(m.x[:, k, :], m.x[:, k, :], rstd, ALU.mult).then_inc(*V.step(f"n{k}"))

        @block.scalar
        def _(act):
            for k in range(8):
                act.wait_ge(V.sem, V.done(0, f"c{k}"))
                if k >= 2:
                    act.wait_ge(P.sem, P.done(0, f"v{k - 2}"))
                nc.scalar.activation(sq[:, k % 2], m.x[:, k, :], ACT.Square).then_inc(*A.step(f"s{k}"))
            act.wait_ge(P.sem, P.done(0, "v7"))
            nc.scalar.activation(blocks4(rstd), linear_out(m, 1), ACT.Sqrt,
                                 bias=m.eps(0)).then_inc(*A.step("std"))
            for k in range(8):
                act.wait_ge(V.sem, V.done(0, f"n{k}"))
                nc.scalar.activation(m.x[:, k, :], m.x[:, k, :], ACT.Identity, scale=m.col(gain + k),
                                     bias=m.col(shift + k)).then_inc(*A.step(f"g{k}"))


def start(m):
    nc, io = m.nc, m.io
    natural = m.arena[:, m.work:m.work + 9 * D].rearrange("p (t d) -> p t d", t=9)
    rows = m.arena[:, m.work + 9 * D:m.work + 9 * D + 128]
    consts = nc.alloc_semaphore("consts_loaded")
    params = nc.alloc_semaphore("params_loaded")
    prompt = nc.alloc_semaphore("prompt_loaded")
    sample = nc.alloc_semaphore("sample_loaded")
    sinks = m.sinks_loaded = nc.alloc_semaphore("sinks_loaded")
    cleared = nc.alloc_semaphore("rows_cleared")
    turned = nc.alloc_semaphore("turned")
    moved = nc.alloc_semaphore("turned_moved")
    by_rows = [("mu", io["mu_b"], 14), ("w0", io["w0_b"], 4), ("a0", io["a0_b"], 4), ("kk", io["k_k_b"], 4),
               ("ka", io["k_a_b"], 4), ("lnxg", io["lnx_g_b"], 4), ("lnxb", io["lnx_b_b"], 4),
               ("subln", io["subln_g_c"], 1)]
    with nc.Block() as block:

        @block.sync
        def _(sp):
            sp.dma_start(m.const, io["consts"][:, 0:m.nconst]).then_inc(consts, 16)
            sp.dma_start(natural[:, 0:8, :], io["x_prompt"][0].rearrange("(t p) d -> p t d", p=128))\
              .then_inc(prompt, 16)
            sp.dma_start(natural[0:TS, 8, :], io["x_sample"][0]).then_inc(sample, 16)

        @block.scalar
        def _(act):
            act.wait_ge(cleared, 1)
            n = 0
            for name, src, count in by_rows:
                act.dma_start(rows[ROWS[name]:ROWS[name] + count, :],
                              src[0].rearrange("(k p) -> k p", p=128)).then_inc(params, 16)
                n += 1
            act.dma_start(rows[ROWS["rk"]:ROWS["rk"] + 4, :],
                          io["r_k_b"][0].rearrange("(k h) d -> k (h d)", h=2)).then_inc(params, 16)
            act.dma_start(rows[ROWS["shift"]:ROWS["shift"] + 14, :],
                          io["state_b_shift"][0, 0, 0].rearrange("(k p) -> k p", p=128)).then_inc(params, 16)
            for name, src in (("mixg", "ln_mix_g"), ("mixb", "ln_mix_b"), ("ffng", "ln_ffn_g"), ("ffnb", "ln_ffn_b")):
                act.dma_start(rows[ROWS[name]:ROWS[name] + 16, :],
                              io[src].rearrange("l (k p) -> (l k) p", p=128)).then_inc(params, 16)
            act.dma_start(m.sink, io["sink_a"].partition_broadcast(128).rearrange("p a h -> p (a h)"))\
               .then_inc(sinks, 16)
            for v, name in enumerate(("lam_q1_c", "lam_k1_c", "lam_q2_c", "lam_k2_c")):
                act.dma_start(m.lam_in[:, v, :], io[name].partition_broadcast(128).rearrange("p a h -> p (a h)"))\
                   .then_inc(sinks, 16)
            act.wait_ge(sinks, 16 * 5)

        @block.vector
        def _(dve):
            nc.vector.memset(m.om, 0.0)
            nc.vector.memset(rows, 0.0).then_inc(cleared, 1)
            for t in range(9):
                n = 128 if t < 8 else TS
                dve.wait_ge(turned, t + 1)
                nc.vector.tensor_copy(m.x[:, :, t * 128:t * 128 + n],
                                      m.ps[:, (t % 2) * 1024:(t % 2) * 1024 + 1024]
                                      .rearrange("p (k t) -> p k t", k=8)[:, :, 0:n]).then_inc(moved, 1)
            dve.wait_ge(turned, 10)
            nc.vector.tensor_copy(m.cols, bank(m, 4)[:, 0:128]).then_inc(moved, 1)

        @block.tensor
        def _(pe):
            pe.wait_ge(consts, 16)
            pe.wait_ge(prompt, 16)
            for t in range(9):
                n = 128 if t < 8 else TS
                if t == 8:
                    pe.wait_ge(sample, 16)
                if t >= 2:
                    pe.wait_ge(moved, t - 1)
                for k in range(8):
                    at = (t % 2) * 1024 + k * 128
                    last = nc.tensor.transpose(m.ps[:, at:at + n], natural[0:n, t, k * 128:(k + 1) * 128],
                                               m.c("ident")[0:n, 0:n])
                last.then_inc(turned, 1)
            pe.wait_ge(params, 16 * 14)
            nc.tensor.transpose(bank(m, 4)[:, 0:128], rows, m.c("ident")).then_inc(turned, 1)


def window_attention(m):
    nc, io = m.nc, m.io
    w = m.work
    vn = m.arena[:, w:w + 1280].rearrange("p (t c) -> p t c", t=10)
    kcache = m.arena[:, w + 1280:w + 1408]
    kct = m.arena[:, w + 1408:w + 1536]
    out_rows = m.arena[:, w + 1536:w + 2048].rearrange("p (a c) -> p a c", a=4)
    w += 2048
    qz = m.arena[:, w:w + 1024].rearrange("p (h q) -> p h q", h=8)
    idle = m.om[:, 5:6]
    logits = m.arena[:, w + 1024:w + 3072].rearrange("p (h k) -> p h k", h=8)
    pt = m.arena[:, w + 3072:w + 5120].rearrange("p (h j q) -> p h j q", h=8, j=2)
    on = m.arena[:, w + 5120:w + 5632]
    st = m.arena[:, w + 5632:w + 5696]
    top, low, total, sink_e, inv = (st[:, 8 * n:8 * n + 8] for n in range(5))
    q, kT, vT = m.p[:, 0:4, :], m.p[:, 16, :], m.p[:, 17, :]

    cached = nc.alloc_semaphore("a_cache_loaded")
    stored = nc.alloc_semaphore("a_stored")
    pre = Steps(nc, "a_pre_pe", [f"v{t}" for t in range(9)] + ["kc", "k7", "k8"])
    prev = Steps(nc, "a_pre_dve", [f"v{t}" for t in range(9)] + ["kc", "k7", "k8"])
    with nc.Block() as block:

        @block.sync
        def _(sp):
            sp.dma_start(kcache, io["cache_a_k"][0, 0].rearrange("s g d -> s (g d)")).then_inc(cached, 16)
            sp.dma_start(vn[:, 9, :], io["cache_a_v"][0, 0].rearrange("s g d -> s (g d)")).then_inc(cached, 16)
            rows = lambda o: o[0, 0].rearrange("s g d -> s (g d)")
            sp.dma_start(rows(io["a_k_s"])[0:64], io["cache_a_k"][0, 0, 64:128].rearrange("s g d -> s (g d)"))\
              .then_inc(stored, 16)
            sp.dma_start(rows(io["a_v_s"])[0:64], io["cache_a_v"][0, 0, 64:128].rearrange("s g d -> s (g d)"))\
              .then_inc(stored, 16)
            sp.wait_ge(prev.sem, prev.done(0, "k8"))
            sp.dma_start(rows(io["a_v_p"]), vn[:, 7, :]).then_inc(stored, 16)
            sp.dma_start(rows(io["a_v_s"])[64:128], vn[0:64, 8, :]).then_inc(stored, 16)
            sp.dma_start(rows(io["a_k_p"]), out_rows[:, 0, :]).then_inc(stored, 16)
            sp.dma_start(rows(io["a_k_s"])[64:128], out_rows[0:64, 1, :]).then_inc(stored, 16)
            sp.wait_ge(stored, 16 * 6)

        @block.gpsimd
        def _(pool):
            nc.gpsimd.memset(qz, 0.0)
            join(m, pool, m.joined)

        @block.tensor
        def _(pe):
            def turn(bk, src, n, name):
                nc.tensor.transpose(bank(m, bk)[0:n, 0:128], src, m.c("ident")).then_inc(*pre.step(name))

            for t in range(9):
                n = 128 if t < 8 else TS
                if t >= 4:
                    pe.wait_ge(prev.sem, prev.done(0, f"v{t - 4}"))
                turn(t % 4, vT[:, t * 128:t * 128 + n], n, f"v{t}")
            pe.wait_ge(cached, 32)
            turn(4, kcache, 128, "kc")
            turn(5, kT[:, TP - 128:TP], 128, "k7")
            turn(6, kT[:, TP:T], TS, "k8")

        @block.vector
        def _(dve):
            for t in range(9):
                n = 128 if t < 8 else TS
                dve.wait_ge(pre.sem, pre.done(0, f"v{t}"))
                nc.vector.tensor_copy(vn[0:n, t, :], bank(m, t % 4)[0:n, 0:128]).then_inc(*prev.step(f"v{t}"))
            for name, bk, dst in (("kc", 4, kct), ("k7", 5, out_rows[:, 0, :]), ("k8", 6, out_rows[0:64, 1, :])):
                dve.wait_ge(pre.sem, pre.done(0, name))
                n = dst.shape[0]
                nc.vector.tensor_copy(dst, bank(m, bk)[0:n, 0:128]).then_inc(*prev.step(name))

    P = Steps(nc, "a_pe", ["scores", "pt0", "pt1", "out", "turn"])
    V = Steps(nc, "a_dve", [f"logits{h}" for h in range(8)] + ["max", "top", "low", "pt1", "sum", "inv", "norm"])
    A = Steps(nc, "a_act", ["q0", "q1"] + [f"exp{h}" for h in range(8)] + ["sink", "pt0", "turned"])

    def keys(first, sample):
        return (1, 2, 256) if first else (0, 2, 192) if sample else (0, 2, 256)

    kept = nc.alloc_semaphore("x_kept")

    with nc.Block() as block:

        @block.sync
        def _(sp):
            sp.dma_start(io["x_kept"], m.arena[:, m.x_at:m.x_at + 8 * T]).then_inc(kept, 16)
            sp.wait_ge(kept, 16)

        def rounds(engine, body):
            body(0, True, False)
            with engine.Fori(1, NQ) as t:
                body(t, False, False)
            body(NQ, False, True)

        @block.scalar
        def _(act):
            def body(t, first, sample):
                n = TS if sample else 128
                qs = q[:, :, ds(t * 128, n)]
                if not first:
                    act.wait_ge(P.sem, P.done(t - 1, "scores"))
                nc.scalar.activation(qz[0:64, 0:4, 0:n], qs[0:64], ACT.Copy, scale=SCALE).then_inc(*A.step("q0"))
                nc.scalar.activation(qz[64:128, 4:8, 0:n], qs[64:128], ACT.Copy, scale=SCALE)\
                    .then_inc(*A.step("q1"))
                a, _, z = keys(first, sample)
                act.wait_ge(V.sem, V.done(t, "low"))
                for h in range(8):
                    e = logits[:, h, a * 128:z]
                    nc.scalar.activation(e, e, ACT.Exp, bias=low[:, h:h + 1], accum_out=total[:, h:h + 1])\
                        .then_inc(*A.step(f"exp{h}"))
                nc.scalar.activation(sink_e, top, ACT.Exp).then_inc(*A.step("sink"))
                act.wait_ge(P.sem, P.done(t, "pt0"))
                move = m.ps[:, 2048:3072].rearrange("p (h j q) -> p h j q", h=4, j=2)
                if first:
                    nc.scalar.activation(pt[:, 0:4, 1, :], move[:, :, 1, :], ACT.Copy).then_inc(*A.step("pt0"))
                elif sample:
                    nc.scalar.activation(pt[:, 0:4, 0, :], move[:, :, 0, :], ACT.Copy)
                    nc.scalar.activation(pt[0:64, 0:4, 1, :], move[0:64, :, 1, :], ACT.Copy)\
                        .then_inc(*A.step("pt0"))
                else:
                    nc.scalar.activation(pt[:, 0:4], move, ACT.Copy).then_inc(*A.step("pt0"))
                act.wait_ge(P.sem, P.done(t, "turn"))
                nc.scalar.activation(idle, idle, ACT.Copy)
                nc.scalar.activation(q[:, :, ds(t * 128, n)],
                                     bank(m, 6).rearrange("p (a q) -> p a q", a=4)[:, :, 0:n], ACT.Copy)\
                    .then_inc(*A.step("turned"))

            rounds(act, body)

        @block.vector
        def _(dve):
            def body(t, first, sample):
                a, _, z = keys(first, sample)
                dve.wait_ge(P.sem, P.done(t, "scores"))
                for h in range(8):
                    at = h * 256
                    nc.vector.scalar_tensor_tensor(
                        out=logits[:, h, a * 128:z], in0=m.c("distA")[:, a * 128:z],
                        scalar=-2.0 ** (-(h + 1)), in1=m.ps[:, at + a * 128:at + z],
                        op0=ALU.mult, op1=ALU.add).then_inc(*V.step(f"logits{h}"))
                dve.wait_ge(V.sem, V.done(t, "logits7"))
                nc.vector.tensor_reduce(top, logits[:, :, a * 128:z], AX.X, ALU.max).then_inc(*V.step("max"))
                dve.wait_ge(V.sem, V.done(t, "max"))
                nc.vector.tensor_tensor(inv, top, m.sink, ALU.max).then_inc(*V.step("top"))
                dve.wait_ge(V.sem, V.done(t, "top"))
                nc.vector.tensor_tensor(top, m.sink, inv, ALU.subtract)
                nc.vector.tensor_scalar(low, inv, -1.0, None, ALU.mult).then_inc(*V.step("low"))
                dve.wait_ge(P.sem, P.done(t, "pt1"))
                move = m.ps[:, 0:1024].rearrange("p (h j q) -> p h j q", h=4, j=2)
                if first:
                    nc.vector.tensor_copy(pt[:, 4:8, 1, :], move[:, :, 1, :]).then_inc(*V.step("pt1"))
                elif sample:
                    nc.vector.tensor_copy(pt[:, 4:8, 0, :], move[:, :, 0, :])
                    nc.vector.tensor_copy(pt[0:64, 4:8, 1, :], move[0:64, :, 1, :]).then_inc(*V.step("pt1"))
                else:
                    nc.vector.tensor_copy(pt[:, 4:8], move).then_inc(*V.step("pt1"))
                dve.wait_ge(A.sem, A.done(t, "sink"))
                nc.vector.tensor_tensor(total, total, sink_e, ALU.add).then_inc(*V.step("sum"))
                dve.wait_ge(V.sem, V.done(t, "sum"))
                nc.vector.reciprocal(inv, total).then_inc(*V.step("inv"))
                dve.wait_ge(V.sem, V.done(t, "inv"))
                dve.wait_ge(P.sem, P.done(t, "out"))
                nc.vector.tensor_tensor(
                    on.rearrange("p (a g d) -> p g a d", a=4, g=2),
                    bank(m, 7).rearrange("p (g a d) -> p g a d", g=2, a=4),
                    inv.rearrange("p (g a) -> p g a", g=2).unsqueeze(3).to_broadcast([128, 2, 4, 64]),
                    ALU.mult).then_inc(*V.step("norm"))

            rounds(dve, body)

        @block.tensor
        def _(pe):
            def turn_probs(t, first, sample, base, heads, name):
                for n, h in enumerate(heads):
                    for j in (1,) if first else (0, 1):
                        k = TS if sample and j == 1 else 128
                        at = base + n * 256 + j * 128
                        last = nc.tensor.transpose(m.ps[0:k, at:at + 128], logits[:, h, j * 128:j * 128 + k],
                                                   m.c("ident"))
                last.then_inc(*P.step(name))

            def body(t, first, sample):
                pe.wait_ge(A.sem, A.done(t, "q1"))
                for h in range(8):
                    at = h * 256
                    if sample:
                        nc.tensor.matmul(m.ps[:, at:at + 128], qz[:, h, :], kct, start=True, stop=True)
                        last = nc.tensor.matmul(m.ps[:, at + 128:at + 192], qz[:, h, :], kT[:, TP:T],
                                                start=True, stop=True)
                    elif first:
                        last = nc.tensor.matmul(m.ps[:, at + 128:at + 256], qz[:, h, :], kT[:, 0:128],
                                                start=True, stop=True)
                    else:
                        last = nc.tensor.matmul(m.ps[:, at:at + 256], qz[:, h, :], kT[:, ds(t * 128 - 128, 256)],
                                                start=True, stop=True)
                last.then_inc(*P.step("scores"))
                pe.wait_ge(A.sem, A.done(t, "exp3"))
                turn_probs(t, first, sample, 2048, range(4), "pt0")
                pe.wait_ge(A.sem, A.done(t, "exp7"))
                turn_probs(t, first, sample, 0, range(4, 8), "pt1")
                pe.wait_ge(A.sem, A.done(t, "pt0"))
                pe.wait_ge(V.sem, V.done(t, "pt1"))
                for h in range(8):
                    g = h // 4
                    for j in (1,) if first else (0, 1):
                        k = TS if sample and j == 1 else 128
                        if sample or first:
                            v = vn[0:k, (9, 8)[j] if sample else 0, 64 * g:64 * g + 64]
                        else:
                            v = vn[:, ds(t + (j - 1), 1), 64 * g:64 * g + 64].rearrange("p a d -> p (a d)")
                        last = nc.tensor.matmul(bank(m, 7)[:, h * 64:h * 64 + 64], pt[0:k, h, j, :], v,
                                                start=(j == 0 or first), stop=(j == 1))
                last.then_inc(*P.step("out"))
                pe.wait_ge(V.sem, V.done(t, "norm"))
                if not first:
                    pe.wait_ge(A.sem, A.done(t - 1, "turned"))
                for a in range(4):
                    last = nc.tensor.transpose(bank(m, 6)[:, a * 128:a * 128 + 128], on[:, a * 128:a * 128 + 128],
                                               m.c("ident"))
                last.then_inc(*P.step("turn"))

            rounds(pe, body)


def rwkv_prepare(m):
    nc, io = m.nc, m.io
    w = m.work
    m.kk = m.arena[:, w:w + 4 * T].rearrange("p (h t) -> p h t", h=4)
    m.a = m.arena[:, w + 4 * T:w + 8 * T].rearrange("p (h t) -> p h t", h=4)
    m.pc = m.arena[:, w + 8 * T:w + 8 * T + 68].rearrange("p (h c) -> p h c", h=4)
    m.g_up = m.arena[:, w + 8 * T + 68:w + 8 * T + 580]
    w += 8 * T + 580
    m.chunk_at = w
    diff = m.arena[:, w:w + 2 * T].rearrange("p (s t) -> p s t", s=2)
    edge = m.arena[:, w + 2 * T:w + 2 * T + 28].rearrange("p (k e) -> p k e", e=2)
    lastc = m.arena[:, w + 2 * T + 28:w + 2 * T + 56]
    lastr = m.arena[:, w + 2 * T + 64:w + 2 * T + 192]
    wa_up = m.arena[:, w + 2 * T + 192:w + 2 * T + 704]
    w += 2 * T + 704
    sg, cum, before, tmp = (m.arena[:, w + n * T:w + n * T + T] for n in range(4))
    assert w + 4 * T <= m.limit, w + 4 * T
    p = m.p
    r, k, v = p[:, 4:8, :], p[:, 8:12, :], p[:, 12:16, :]
    spots = [(0, 12, 4), (12, 14, 18)]

    loaded = nc.alloc_semaphore("b_weights_loaded")
    stored = nc.alloc_semaphore("b_shift_stored")
    S = Steps(nc, "b_shift_dve", ["edge"] + [f"t{j}" for j in range(3 * 14)] + ["last"])
    S2 = nc.alloc_semaphore("b_shift_turned")
    with nc.Block() as block:

        @block.sync
        def _(sp):
            sp.dma_start(wa_up[0:64], io["w_up_b"][0]).then_inc(loaded, 16)
            sp.dma_start(wa_up[64:128], io["a_up_b"][0]).then_inc(loaded, 16)
            sp.dma_start(m.g_up, io["g_up_b"][0]).then_inc(loaded, 16)
            sp.wait_ge(S.sem, S.done(0, "last"))
            for n, out in enumerate(("b_shift_p", "b_shift_s")):
                sp.dma_start(io[out][0, 0, 0].rearrange("(k p) -> k p", p=128), lastr[14 * n:14 * n + 14, :])                  .then_inc(stored, 16)
            sp.wait_ge(stored, 32)

        @block.vector
        def _(dve):
            for a, b, at in spots:
                nc.vector.tensor_copy(lastc[:, a:b], p[:, at:at + b - a, TP - 1])
                nc.vector.tensor_copy(lastc[:, 14 + a:14 + b], p[:, at:at + b - a, T - 1])
            for a, b, at in spots:
                nc.vector.tensor_scalar(edge[:, a:b, 0], p[:, at:at + b - a, 0], -1.0, None, ALU.mult)
                last = nc.vector.tensor_tensor(edge[:, a:b, 1], m.cols[:, ROWS["shift"] + a:ROWS["shift"] + b],
                                               p[:, at:at + b - a, TP], ALU.subtract)
            last.then_inc(*S.step("edge"))
            dve.wait_ge(S.sem, S.done(0, "edge"))
            for j in range(14):
                x = p[:, 4 + j if j < 12 else 6 + j, :]
                d = diff[:, j % 2]
                nc.vector.tensor_tensor(d[:, 1:T], x[:, 0:T - 1], x[:, 1:T], ALU.subtract)                    .then_inc(*S.step(f"t{3 * j}"))
                dve.wait_ge(S.sem, S.done(0, f"t{3 * j}"))
                nc.vector.tensor_copy(d[:, 0:T:TP], edge[:, j, :]).then_inc(*S.step(f"t{3 * j + 1}"))
                dve.wait_ge(S.sem, S.done(0, f"t{3 * j + 1}"))
                nc.vector.scalar_tensor_tensor(out=x, in0=d, scalar=m.col(ROWS["mu"] + j), in1=x,
                                               op0=ALU.mult, op1=ALU.add).then_inc(*S.step(f"t{3 * j + 2}"))
            dve.wait_ge(S2, 1)
            nc.vector.tensor_copy(lastr[0:28, :], bank(m, 0)[0:28, 0:128]).then_inc(*S.step("last"))

        @block.tensor
        def _(pe):
            pe.wait_ge(S.sem, S.done(0, "edge"))
            nc.tensor.transpose(bank(m, 0)[0:28, 0:128], lastc, m.c("ident")).then_inc(S2, 1)

    bonus = [16, 17, 20, 18]
    m.bonus = bonus
    m.y = r
    P = Steps(nc, "b_pe", ["w", "a", "norm", "bonus"])
    V = Steps(nc, "b_dve", ["kk", "kk2", "cum", "before", "ak", "k", "rk", "rkk", "rnorm", "kkn", "bon", "b",
                            "A", "K", "B", "pc"])
    A = Steps(nc, "b_act", ["sg", "a", "norm", "e1", "e2", "e3"])
    om = m.om
    pre = nc.alloc_semaphore("b_one_minus_ka")
    gates = nc.alloc_semaphore("b_gates")
    e1, e2, e3 = diff[:, 0], diff[:, 1], sg

    with nc.Block() as block:

        @block.tensor
        def _(pe):
            pe.wait_ge(loaded, 48)
            for h in range(4):
                cols = slice(128 * h, 128 * h + 128)

                def product(base, lhsT, src, name):
                    for b in range(4):
                        at = base + 512 * b
                        last = nc.tensor.matmul(m.ps[:, at:at + TB], lhsT, src[:, b * TB:(b + 1) * TB],
                                                start=True, stop=True)
                    last.then_inc(*P.step(name))

                if h:
                    pe.wait_ge(A.sem, A.done(h - 1, "norm"))
                pe.wait_ge(gates, 1)
                product(0, wa_up[0:64, cols], p[0:64, 18, :], "w")
                if h:
                    pe.wait_ge(V.sem, V.done(h - 1, "bon"))
                product(2048, wa_up[64:128, cols], p[64:128, 18, :], "a")
                pe.wait_ge(A.sem, A.done(h, "a"))
                pe.wait_ge(V.sem, V.done(h, "kk2"))
                product(0, m.c("heads"), tmp, "norm")
                pe.wait_ge(V.sem, V.done(h, "rkk"))
                product(2048, m.c("heads"), before, "bonus")

        @block.scalar
        def _(act):
            for h in range(4):
                if h == 0:
                    nc.scalar.activation(p[0:64, 18, :], p[0:64, 18, :], ACT.Tanh).then_inc(gates, 1)
                    nc.scalar.activation(p[:, 19, :], p[:, 19, :], ACT.Sigmoid).then_inc(gates, 1)
                act.wait_ge(P.sem, P.done(h, "w"))
                if h:
                    act.wait_ge(V.sem, V.done(h - 1, "B"))
                nc.scalar.activation(blocks4(sg), linear_out(m, 0), ACT.Sigmoid, bias=m.col(ROWS["w0"] + h))                    .then_inc(*A.step("sg"))
                act.wait_ge(P.sem, P.done(h, "a"))
                nc.scalar.activation(blocks4(m.a[:, h]), linear_out(m, 1), ACT.Sigmoid,
                                     bias=m.col(ROWS["a0"] + h)).then_inc(*A.step("a"))
                act.wait_ge(P.sem, P.done(h, "norm"))
                nc.scalar.activation(blocks4(tmp), linear_out(m, 0), ACT.Sqrt, bias=m.eps(1))                    .then_inc(*A.step("norm"))
                act.wait_ge(V.sem, V.done(h, "k"))
                nc.scalar.activation(e1, cum, ACT.Exp, scale=-DECAY).then_inc(*A.step("e1"))
                nc.scalar.activation(e2, e2, ACT.Exp, scale=-DECAY).then_inc(*A.step("e2"))
                nc.scalar.activation(e3, cum, ACT.Exp, scale=DECAY).then_inc(*A.step("e3"))

        @block.vector
        def _(dve):
            dve.wait_ge(S.sem, S.done(0, "last"))
            nc.vector.tensor_scalar(om[:, 0:4], m.cols[:, ROWS["ka"]:ROWS["ka"] + 4], -1.0, 1.0,
                                    ALU.mult, ALU.add).then_inc(pre, 1)
            dve.wait_ge(pre, 1)
            tt, stt = nc.vector.tensor_tensor, nc.vector.scalar_tensor_tensor

            for h in range(4):
                kk, a = m.kk[:, h], m.a[:, h]

                def after(name, t=h):
                    dve.wait_ge(V.sem, V.done(t, name))

                nc.vector.tensor_scalar(kk, k[:, h], m.col(ROWS["kk"] + h), None, ALU.mult).then_inc(*V.step("kk"))
                after("kk")
                tt(tmp, kk, kk, ALU.mult).then_inc(*V.step("kk2"))
                dve.wait_ge(A.sem, A.done(h, "a"))
                nc.vector.tensor_tensor_scan(cum, m.c("reset"), sg, 0.0, ALU.mult, ALU.add)                    .then_inc(*V.step("cum"))
                after("cum")
                tt(e2, cum, sg, ALU.subtract).then_inc(*V.step("before"))
                nc.vector.tensor_scalar(e1, a, m.col(ROWS["ka"] + h), om[:, h:h + 1], ALU.mult, ALU.add)                    .then_inc(*V.step("ak"))
                after("ak")
                tt(k[:, h], k[:, h], e1, ALU.mult).then_inc(*V.step("k"))
                nc.vector.tensor_scalar(before, r[:, h], m.col(ROWS["rk"] + h), None, ALU.mult)                    .then_inc(*V.step("rk"))
                after("rk")
                tt(before, before, k[:, h], ALU.mult).then_inc(*V.step("rkk"))
                dve.wait_ge(A.sem, A.done(h, "norm"))
                nc.vector.reciprocal(tmp, tmp).then_inc(*V.step("rnorm"))
                after("rnorm")
                stt(out=kk, in0=kk, scalar=-1.0, in1=tmp, op0=ALU.mult, op1=ALU.mult).then_inc(*V.step("kkn"))
                dve.wait_ge(P.sem, P.done(h, "bonus"))
                tt(blocks4(p[:, bonus[h], :]), linear_out(m, 1), blocks4(v[:, h]), ALU.mult)                    .then_inc(*V.step("bon"))
                after("kkn")
                stt(out=a, in0=a, scalar=-1.0, in1=kk, op0=ALU.mult, op1=ALU.mult).then_inc(*V.step("b"))
                dve.wait_ge(A.sem, A.done(h, "e3"))
                after("b")
                tt(r[:, h], r[:, h], e1, ALU.mult)
                tt(kk, kk, e2, ALU.mult).then_inc(*V.step("A"))
                tt(k[:, h], k[:, h], e3, ALU.mult).then_inc(*V.step("K"))
                tt(a, a, e3, ALU.mult).then_inc(*V.step("B"))
                nc.vector.tensor_copy(m.pc[:, h, :], e1[:, CH - 1:T:CH]).then_inc(*V.step("pc"))
                after("pc")


def rwkv_chunks(m):
    nc, io = m.nc, m.io
    room = {"spare": (m.chunk_at, m.limit), "x": (m.x_at, m.x_at + 8 * T)}
    handed = ("R", "A", "XT1", "LkT", "MbT", "MkT", "Vn", "Bn", "Kn")
    names = [f"{n}{i}" for n in handed for i in range(2)]
    names += ["B", "K", "V", "X0", "X1", "Xt0", "Xt1", "LT", "T1", "U", "SA", "Sn", "state_in", "state_out"]
    at = {n: lo for n, (lo, _) in room.items()}
    slot = {"S": m.state}
    for name in names:
        where = "x" if at["x"] + 512 <= room["x"][1] else "spare"
        slot[name] = m.arena[:, at[where]:at[where] + 512]
        at[where] += 512
        assert at[where] <= room[where][1]
    S = slot["S"]
    block4 = {n: heads4(a) for n, a in slot.items()}
    p = m.p
    src = {"R": p[:, 4:8, :], "A": m.kk, "B": m.a, "K": p[:, 8:12, :], "V": p[:, 12:16, :]}
    LEVELS = (2, 4, 8, 16, 32)
    pairs = (("L", "A", "B"), ("LT", "B", "A"), ("LkT", "K", "A"), ("MbT", "B", "R"), ("MkT", "K", "R"))
    free_steps = ["L", "LT", "LkT", "MbT", "MkT", "T2", "Vn", "X2", "XT2", "T4", "Bn", "X4", "XT4", "T8", "Kn",
                  "X8", "XT8", "T16", "X16", "XT16", "T32", "XT32"]
    banks = {n: i % 6 for i, n in enumerate(free_steps)}
    banks.update(U=6, SA=7, S=6, Y=7)
    by_scalar = ("Vn", "Bn", "Kn")
    FP, SP = Steps(nc, "w_free_pe", free_steps), Steps(nc, "w_state_pe", ["U", "SA", "S", "Y"])
    FV = Steps(nc, "w_free_dve", ["L", "X1", "LT", "XT1m", "XT1", "LkT", "MbT", "T2", "MkT",
                                  "X2", "XT2"]
               + sum([[f"T{n}"] + ([f"X{n}"] if n < 32 else []) + [f"XT{n}"] for n in LEVELS[1:]], []))
    SV = Steps(nc, "w_state_dve", ["Sadd", "S"])
    FA = Steps(nc, "w_free_act", ["Vn", "Bn", "Kn"])
    CV, CA = Steps(nc, "w_copies_dve", ["R", "A"]), Steps(nc, "w_copies_act", ["B", "K", "V"])
    SA = Steps(nc, "w_state_act", ["U", "SA", "Y"])
    st_load = nc.alloc_semaphore("w_state_loaded")
    st_turn = nc.alloc_semaphore("w_state_turned")
    st_move = nc.alloc_semaphore("w_state_moved")
    cleared = nc.alloc_semaphore("w_cleared")
    stored = nc.alloc_semaphore("w_stored")
    state_in, state_out = slot["state_in"], slot["state_out"]

    def mask(name):
        return m.c(name).unsqueeze(1).to_broadcast([128, 4, 128])

    def halves_copy(op, out, name, t):
        cols = ds(t * CH, CH)
        op(out[0:64, :, 0:64], src[name][0:64, :, cols])
        return op(out[64:128, :, 64:128], src[name][64:128, :, cols])

    def psum(name):
        return heads4(bank(m, banks[name]))


    def copies_vector(dve, t, odd, first):
        if not first:
            dve.wait_ge(SP.sem, SP.done(t - 2, "Y"))
        halves_copy(nc.vector.tensor_copy, block4[f"R{odd}"], "R", t).then_inc(*CV.step("R"))
        halves_copy(nc.vector.tensor_copy, block4[f"A{odd}"], "A", t).then_inc(*CV.step("A"))

    def copies_scalar(act, t):
        def copy(out, in_):
            return nc.scalar.activation(out, in_, ACT.Copy)

        for name in ("B", "K", "V"):
            halves_copy(copy, block4[name], name, t).then_inc(*CA.step(name))

    def chunk_vector(dve, t, odd, free, state, following):
        tt = nc.vector.tensor_tensor
        mine = {n: block4[f"{n}{odd}"] for n in handed}

        def after(name):
            dve.wait_ge(FV.sem, FV.done(t, name))

        def product(name):
            dve.wait_ge(FP.sem, FP.done(t, name))
            return psum(name)

        def masked(name, out, by):
            tt(out, product(name), mask(by), ALU.mult).then_inc(*FV.step(name))

        def state_sum():
            if state:
                dve.wait_ge(SP.sem, SP.done(t - 1, "S"))
                tt(block4["Sn"], psum("S"), block4["S"], ALU.add).then_inc(*SV.step("Sadd"))

        def state_decay():
            if state:
                dve.wait_ge(SP.sem, SP.done(t - 1, "Y"))
                dve.wait_ge(SV.sem, SV.done(t - 1, "Sadd"))
                tt(block4["S"], block4["Sn"], m.pc[:, :, ds(t - 1, 1)].to_broadcast([128, 4, 128]), ALU.mult)\
                    .then_inc(*SV.step("S"))

        if not free:
            state_sum()
            state_decay()
            return
        masked("L", block4["T1"], "low1")
        after("L")
        tt(block4["X0"], block4["T1"], mask("ident"), ALU.add).then_inc(*FV.step("X1"))
        masked("LT", block4["LT"], "strict")
        after("LT")
        tt(block4["T1"], block4["LT"], mask("up1"), ALU.mult).then_inc(*FV.step("XT1m"))
        after("XT1m")
        tt(block4["Xt0"], block4["T1"], mask("ident"), ALU.add).then_inc(*FV.step("XT1"))
        masked("LkT", mine["LkT"], "strict")
        masked("MbT", mine["MbT"], "upto")
        masked("T2", block4["T1"], "low2")
        masked("MkT", mine["MkT"], "upto")
        for i, n in enumerate(LEVELS):
            old, new = i % 2, 1 - i % 2
            if i:
                masked(f"T{n}", block4["T1"], f"low{n}")
            if n == 16:
                state_sum()
            if n < 32:
                tt(block4[f"X{new}"], product(f"X{n}"), block4[f"X{old}"], ALU.add).then_inc(*FV.step(f"X{n}"))
            out = mine["XT1"] if n == 32 else block4[f"Xt{new}"]
            tt(out, product(f"XT{n}"), block4[f"Xt{old}"], ALU.add).then_inc(*FV.step(f"XT{n}"))
            if n == 16:
                state_decay()
                if following:
                    copies_vector(dve, t + 1, 1 - odd, not state)

    def chunk_scalar(act, t, odd, free, state, following):
        def copy(out, in_):
            return nc.scalar.activation(out, in_, ACT.Copy)

        def turned(name):
            if free:
                act.wait_ge(FP.sem, FP.done(t, name))
                copy(slot[f"{name}{odd}"], bank(m, banks[name])).then_inc(*FA.step(name))

        def through(name):
            if state:
                act.wait_ge(SP.sem, SP.done(t - 1, name))
                copy(slot[name], bank(m, banks[name])).then_inc(*SA.step(name))

        turned("Vn")
        through("U")
        turned("Bn")
        through("SA")
        turned("Kn")
        if following:
            copies_scalar(act, t + 1)
        if state:
            act.wait_ge(SP.sem, SP.done(t - 1, "Y"))
            y = psum("Y")
            cols = ds((t - 1) * CH, CH)
            copy(m.y[0:64, :, cols], y[0:64, :, 0:64])
            copy(m.y[64:128, :, cols], y[64:128, :, 64:128]).then_inc(*SA.step("Y"))

    def chunk_tensor(pe, t, odd, free, state, following):
        def product(steps, name, *terms):
            for h in range(4):
                out = bank(m, banks[name])[:, h * 128:h * 128 + 128]
                for i, (lhsT, rhs) in enumerate(terms):
                    last = nc.tensor.matmul(out, block4[lhsT][:, h, :], block4[rhs][:, h, :], start=(i == 0),
                                            stop=(i == len(terms) - 1))
            last.then_inc(*steps.step(name))

        def turn(name, src_name):
            room_of(name)
            for h in range(4):
                last = nc.tensor.transpose(bank(m, banks[name])[:, h * 128:h * 128 + 128], block4[src_name][:, h, :],
                                           m.c("ident"))
            last.then_inc(*FP.step(name))

        def room_of(name):
            i = free_steps.index(name) - 6
            if i < 0:
                return
            if free_steps[i] in by_scalar:
                pe.wait_ge(FA.sem, FA.done(t, free_steps[i]))
            else:
                pe.wait_ge(FV.sem, FV.done(t, free_steps[i]))

        other = 1 - odd

        def through(name):
            if not state:
                return
            if name == "U":
                pe.wait_ge(FV.sem, FV.done(t - 1, "XT32"))
                if not (isinstance(t, int) and t == 1):
                    pe.wait_ge(SV.sem, SV.done(t - 2, "S"))
                    pe.wait_ge(SA.sem, SA.done(t - 2, "Y"))
                product(SP, "U", (f"A{other}", "S"), (f"LkT{other}", f"Vn{other}"))
            elif name == "SA":
                pe.wait_ge(SA.sem, SA.done(t - 1, "U"))
                product(SP, "SA", (f"XT1{other}", "U"))
            elif name == "S":
                pe.wait_ge(SA.sem, SA.done(t - 1, "SA"))
                product(SP, "S", (f"Bn{other}", "SA"), (f"Kn{other}", f"Vn{other}"))
            else:
                product(SP, "Y", ("S", f"R{other}"), ("SA", f"MbT{other}"), (f"Vn{other}", f"MkT{other}"))

        if not free:
            for name in ("U", "SA", "S", "Y"):
                through(name)
            return
        pe.wait_ge(CV.sem, CV.done(t, "A"))
        pe.wait_ge(CA.sem, CA.done(t, "V"))
        for name, lhsT, rhs in pairs:
            if name == "MbT" and state:
                pe.wait_ge(FV.sem, FV.done(t - 1, "XT32"))
            left, right = (n if n in "BK" else f"{n}{odd}" for n in (lhsT, rhs))
            product(FP, name, (left, right))
        between = {2: ("Vn", "V", "U"), 4: ("Bn", "B", "SA"), 8: ("Kn", "K", "S"), 16: (None, None, None),
                   32: (None, None, None)}
        for i, n in enumerate(LEVELS):
            old = i % 2
            if i == 0:
                pe.wait_ge(FV.sem, FV.done(t, "XT1"))
            else:
                pe.wait_ge(FV.sem, FV.done(t, f"XT{LEVELS[i - 1]}"))
            room_of(f"T{n}")
            product(FP, f"T{n}", ("LT", f"X{old}"))
            turned, source, passed = between[n]
            if turned:
                turn(turned, source)
            if n == 16:
                through("Y")
            pe.wait_ge(FV.sem, FV.done(t, f"T{n}"))
            if n < 32:
                room_of(f"X{n}")
                product(FP, f"X{n}", (f"Xt{old}", "T1"))
            room_of(f"XT{n}")
            product(FP, f"XT{n}", ("T1", f"Xt{old}"))
            if passed:
                through(passed)

    def over_chunks(engine, body, before, between):
        before(engine)
        body(engine, 0, 0, True, False, True)
        with engine.Fori(0, NCHUNK // 2 - 1) as i:
            body(engine, i * 2 + 1, 1, True, True, True)
            body(engine, i * 2 + 2, 0, True, True, True)
        body(engine, NCHUNK - 1, 1, True, True, True)
        body(engine, NCHUNK, 0, True, True, False)
        between(engine)
        body(engine, NCHUNK + 1, 1, False, True, False)

    heads_out = io["b_wkv_p"][0, 0], io["b_wkv_s"][0, 0]

    with nc.Block() as block:

        @block.gpsimd
        def _(pool):
            for n in ("R0", "A0", "B", "K", "V", "S", "R1", "A1", "state_in"):
                nc.gpsimd.memset(slot[n], 0.0).then_inc(cleared, 1)

        @block.vector
        def _(dve):
            def before(engine):
                dve.wait_ge(cleared, 8)
                copies_vector(dve, 0, 0, True)

            def save(n):
                dve.wait_ge(st_turn, 2 * n + 1)
                nc.vector.tensor_copy(state_out, bank(m, 0)).then_inc(st_move, 1)

            def between(engine):
                save(0)
                dve.wait_ge(st_turn, 2)
                nc.vector.tensor_copy(S, bank(m, 1)).then_inc(st_move, 1)

            over_chunks(dve, chunk_vector, before, between)
            dve.wait_ge(stored, 32 * 4)
            save(1)

        @block.scalar
        def _(act):
            def before(engine):
                act.wait_ge(cleared, 5)
                copies_scalar(act, 0)

            over_chunks(act, chunk_scalar, before, lambda engine: None)

        @block.tensor
        def _(pe):
            def save(t):
                pe.wait_ge(SV.sem, SV.done(t, "S"))
                for h in range(4):
                    last = nc.tensor.transpose(bank(m, 0)[:, h * 128:h * 128 + 128], block4["S"][:, h, :],
                                               m.c("ident"))
                last.then_inc(st_turn, 1)

            def between(engine):
                pe.wait_ge(FV.sem, FV.done(NCHUNK, "XT32"))
                save(NCHUNK - 1)
                pe.wait_ge(st_load, 32 * 4)
                for h in range(4):
                    last = nc.tensor.transpose(bank(m, 1)[:, h * 128:h * 128 + 128],
                                               heads4(state_in)[:, h, :], m.c("ident"))
                last.then_inc(st_turn, 1)
                pe.wait_ge(st_move, 2)

            over_chunks(pe, chunk_tensor, lambda engine: None, between)
            save(NCHUNK)

        @block.sync
        def _(sp):
            sp.wait_ge(cleared, 9)
            for h in range(8):
                o = 64 * (h % 2)
                sp.dma_start(heads4(state_in)[o:o + 64, h // 2, o:o + 64], io["state_b_wkv"][0, 0, h])\
                  .then_inc(st_load, 16)
            for n in range(2):
                sp.wait_ge(st_move, 2 * n + 1)
                for h in range(8):
                    o = 64 * (h % 2)
                    sp.dma_start(heads_out[n][h], heads4(state_out)[o:o + 64, h // 2, o:o + 64])\
                      .then_inc(stored, 16)
            sp.wait_ge(stored, 32 * 8)


def rwkv_finish(m):
    nc = m.nc
    w = m.chunk_at
    sq, tmp = (m.arena[:, w + n * T:w + n * T + T] for n in range(2))
    P = Steps(nc, "e_pe", ["mean", "gate", "var"])
    V = Steps(nc, "e_dve", ["mean", "centred", "rstd", "normal", "bonus", "gated"])
    A = Steps(nc, "e_act", ["square", "std", "affine"])
    y = m.y
    back = nc.alloc_semaphore("x_back")
    with nc.Block() as block:

        @block.sync
        def _(sp):
            sp.dma_start(m.arena[:, m.x_at:m.x_at + 8 * T], m.io["x_kept"]).then_inc(back, 16)
            sp.wait_ge(back, 16)

        def sums(base, lhsT, src, name):
            for b in range(4):
                at = base + 512 * b
                last = nc.tensor.matmul(m.ps[:, at:at + TB], lhsT, src[:, b * TB:(b + 1) * TB], start=True, stop=True)
            last.then_inc(*P.step(name))

        @block.tensor
        def _(pe):
            for h in range(4):
                if h:
                    pe.wait_ge(V.sem, V.done(h - 1, "gated"))
                sums(0, m.c("heads"), y[:, h], "mean")
                sums(2048, m.g_up[:, h * 128:h * 128 + 128], m.p[:, 19, :], "gate")
                pe.wait_ge(A.sem, A.done(h, "square"))
                sums(0, m.c("heads"), sq, "var")

        @block.vector
        def _(dve):
            for h in range(4):
                def after(name, t=h):
                    dve.wait_ge(V.sem, V.done(t, name))

                dve.wait_ge(P.sem, P.done(h, "mean"))
                nc.vector.tensor_scalar(blocks4(tmp), linear_out(m, 0), 1.0 / HD, None, ALU.mult)\
                    .then_inc(*V.step("mean"))
                after("mean")
                nc.vector.tensor_tensor(y[:, h], y[:, h], tmp, ALU.subtract).then_inc(*V.step("centred"))
                dve.wait_ge(A.sem, A.done(h, "std"))
                nc.vector.reciprocal(tmp, tmp).then_inc(*V.step("rstd"))
                after("rstd")
                nc.vector.tensor_tensor(y[:, h], y[:, h], tmp, ALU.mult).then_inc(*V.step("normal"))
                dve.wait_ge(A.sem, A.done(h, "affine"))
                nc.vector.tensor_tensor(y[:, h], y[:, h], m.p[:, m.bonus[h], :], ALU.add).then_inc(*V.step("bonus"))
                dve.wait_ge(P.sem, P.done(h, "gate"))
                after("bonus")
                nc.vector.tensor_tensor(blocks4(y[:, h]), blocks4(y[:, h]), linear_out(m, 1), ALU.mult)\
                    .then_inc(*V.step("gated"))

        @block.scalar
        def _(act):
            for h in range(4):
                act.wait_ge(V.sem, V.done(h, "centred"))
                nc.scalar.activation(sq, y[:, h], ACT.Square).then_inc(*A.step("square"))
                act.wait_ge(P.sem, P.done(h, "var"))
                nc.scalar.activation(blocks4(tmp), linear_out(m, 0), ACT.Sqrt, bias=m.eps(2), scale=1.0 / HD)\
                    .then_inc(*A.step("std"))
                act.wait_ge(V.sem, V.done(h, "normal"))
                nc.scalar.activation(y[:, h], y[:, h], ACT.Identity, scale=m.col(ROWS["lnxg"] + h),
                                     bias=m.col(ROWS["lnxb"] + h)).then_inc(*A.step("affine"))


def turn_rows(m):
    nc, io = m.nc, m.io
    w = m.work
    m.vn = m.arena[:, w:w + 9 * 512].rearrange("p (t c) -> p t c", t=9)
    w += 9 * 512
    m.vd = m.arena[:, w:w + 9 * 128].rearrange("p (t c) -> p t c", t=9)
    w += 9 * 128
    m.wn = m.arena[:, w:w + 72].rearrange("p (t h) -> p t h", t=9)
    w += 72
    m.odd_work = w
    rows = m.arena[:, w:w + 2 * 704].rearrange("p (s c) -> p s c", s=2)
    p = m.p
    P = Steps(nc, "r_pe", ["k", "v", "rest"])
    A = Steps(nc, "r_act", ["k"])
    V = Steps(nc, "r_dve", ["v", "rest"])
    stored = [nc.alloc_semaphore(f"r_stored{s}") for s in range(2)]
    lam_p = nc.alloc_semaphore("lambda_products")
    lam_e = nc.alloc_semaphore("lambda_exps")
    WSCALE = SCALE * 8 ** -0.5
    n_of = lambda t: 128 if t < 8 else TS

    with nc.Block() as block:

        @block.gpsimd
        def _(pool):
            join(m, pool, m.joined)

        @block.tensor
        def _(pe):
            for t in range(9):
                n, c = n_of(t), slice(t * 128, t * 128 + n_of(t))
                if t >= 2:
                    pe.wait_ge(A.sem, A.done(t - 2, "k"))
                    pe.wait_ge(V.sem, V.done(t - 2, "rest"))
                b = 3 * (t % 2)

                def turn(bk, at, tile, k):
                    return nc.tensor.transpose(bank(m, bk)[0:n, at:at + k], p[0:k, tile, c], m.c("ident")[0:k, 0:k])

                for h in range(4):
                    last = turn(b, h * 128, 4 + h, 128)
                last.then_inc(*P.step("k"))
                for h in range(4):
                    last = turn(b + 1, h * 128, 8 + h, 128)
                last.then_inc(*P.step("v"))
                turn(b + 2, 0, 20, 128)
                turn(b + 2, 128, 22, 128)
                turn(b + 2, 256, 21, 64)
                turn(b + 2, 320, 23, 8).then_inc(*P.step("rest"))

        @block.scalar
        def _(act):
            act.wait_ge(lam_p, 2)
            nc.scalar.activation(m.lam[:, 0:2], m.lam[:, 0:2], ACT.Exp).then_inc(lam_e, 1)
            for t in range(9):
                act.wait_ge(P.sem, P.done(t, "k"))
                if t == 0:
                    act.wait_ge(m.joined, 8 + 1)
                if t >= 2:
                    act.wait_ge(stored[t % 2], 16 * 5 * (t // 2))
                nc.scalar.activation(rows[0:n_of(t), t % 2, 0:512], bank(m, 3 * (t % 2))[0:n_of(t), :], ACT.Copy)\
                    .then_inc(*A.step("k"))

        @block.vector
        def _(dve):
            nc.vector.tensor_tensor(m.lam_in[:, 0:4:2, :], m.lam_in[:, 0:4:2, :], m.lam_in[:, 1:4:2, :], ALU.mult)\
                .then_inc(lam_p, 1)
            dve.wait_ge(lam_p, 1)
            nc.vector.tensor_reduce(m.lam[:, 0:2], m.lam_in[:, 0:4:2, :], AX.X, ALU.add).then_inc(lam_p, 1)
            dve.wait_ge(lam_e, 1)
            nc.vector.tensor_tensor(m.lam[:, 2:3], m.lam[:, 0:1], m.lam[:, 1:2], ALU.subtract).then_inc(lam_p, 1)
            dve.wait_ge(lam_p, 3)
            nc.vector.tensor_scalar(m.lam[:, 3:4], m.lam[:, 2:3], LAM_INIT, -1.0, ALU.add, ALU.mult)\
                .then_inc(lam_p, 1)
            for t in range(9):
                n, b = n_of(t), 3 * (t % 2)
                dve.wait_ge(P.sem, P.done(t, "v"))
                nc.vector.tensor_copy(m.vn[0:n, t, :], bank(m, b + 1)[0:n, :]).then_inc(*V.step("v"))
                dve.wait_ge(P.sem, P.done(t, "rest"))
                if t == 0:
                    dve.wait_ge(m.joined, 8 + 1)
                if t >= 2:
                    dve.wait_ge(stored[t % 2], 16 * 5 * (t // 2))
                r = bank(m, b + 2)
                nc.vector.tensor_copy(rows[0:n, t % 2, 512:640], r[0:n, 0:128])
                nc.vector.tensor_copy(m.vd[0:n, t, :], r[0:n, 128:256])
                nc.vector.tensor_copy(rows[0:n, t % 2, 640:704], r[0:n, 256:320])
                nc.vector.tensor_scalar(m.wn[0:n, t, :], r[0:n, 320:328], WSCALE, None, ALU.mult)\
                    .then_inc(*V.step("rest"))

        @block.sync
        def _(sp):
            for t in range(9):
                n = n_of(t)

                def out(name):
                    o = io[name + ("_p" if t < 8 else "_s")][0, 0]
                    if len(o.shape) == 4:
                        o = o.rearrange("s h m d -> s (h m d)")
                    elif len(o.shape) == 3:
                        o = o.rearrange("s h d -> s (h d)")
                    return o[t * 128:t * 128 + n] if t < 8 else o

                sp.wait_ge(A.sem, A.done(t, "k"))
                sp.wait_ge(V.sem, V.done(t, "rest"))
                for name, src in (("c_k", rows[0:n, t % 2, 0:512]), ("c_v", m.vn[0:n, t, :]),
                                  ("d_k", rows[0:n, t % 2, 512:640]), ("d_v", m.vd[0:n, t, :]),
                                  ("d_kidx", rows[0:n, t % 2, 640:704])):
                    sp.dma_start(out(name), src).then_inc(stored[t % 2], 16)
            sp.wait_ge(stored[0], 16 * 5 * 5)
            sp.wait_ge(stored[1], 16 * 5 * 4)


def odd_attention(m):
    nc, io = m.nc, m.io
    w = m.odd_work

    def room(n):
        nonlocal w
        w += n
        assert w <= m.limit, w
        return m.arena[:, w - n:w]

    def narrow(n, dt):
        return room(n // 2).bitcast(dt)

    q = room(256).rearrange("p (h q) -> p h q", h=2)
    q_s = room(128)
    qi = room(1024).rearrange("p (h q) -> p h q", h=8)
    qi_s = room(512).rearrange("p (b q) -> p b q", b=4)
    small = room(128)
    probs = room(LS)
    on = room(1024).rearrange("p (s c) -> p s c", s=2)
    on_d = room(512)
    both = room(128)
    w_s = room(4)
    distP, distS = narrow(TP, F16), narrow(LS, F16)
    slopes = narrow(256, F16).rearrange("p (h c) -> p h c", h=2)
    ident16, corner16 = narrow(128, BF16), narrow(128, BF16)
    penalty = narrow(LS, BF16)
    masks = CONST["strict"][0]
    pt = m.const[:, masks:masks + (NPT + 1) * 128].rearrange("p (t q) -> p t q", t=NPT + 1)
    p = m.p
    spare = p[:, 8:12, :].rearrange("p k t -> p (k t)")
    kt_s = spare[:, 0:LS]
    v_s = spare[:, LS:LS + (NPT + 1) * 128].rearrange("p (t c) -> p t c", t=NPT + 1)
    index = p[:, 22:24, :].rearrange("p k t -> p (k t)")
    cache_rows = m.vn[:, 0:4, :].rearrange("p t c -> p (t c)").rearrange("p (t c) -> p t c", t=NPT)
    relu = probs[:, 0:2048].rearrange("p (s k) -> p s k", s=4)
    low, inv, best, lam_rows = small[:, 0:2], small[:, 8:16], small[:, 16:24], small[:, 24:25]
    total = small[:, 32:48].rearrange("p (s c) -> p s c", s=2)
    top = small[:, 48:50]
    PT_BANK, TURN_BANK, OUT_BANK = 5, 4, 7
    mix = room(128)
    idle = m.om[:, 5:6]

    class Family:

        def __init__(self, name, units):
            self.units, self.rounds = units, 0
            self.V = {h: Steps(nc, f"{name}_dve{h}", ["max", "low"]) for h in units}
            self.N = Steps(nc, f"{name}_norm", ["inv", "lam", "part", "norm"])
            self.Q = {h: Steps(nc, f"{name}_q{h}", ["q"]) for h in units}
            self.E = {h: Steps(nc, f"{name}_exp{h}", ["exp"]) for h in units}
            self.P = {h: Steps(nc, f"{name}_scores{h}", ["scores"]) for h in units}
            self.O = {h: Steps(nc, f"{name}_out{h}", ["out"]) for h in units}

    prompt_family, sample_family = Family("o", (0, 1)), Family("os", (0,))
    turned, moved = nc.alloc_semaphore("probs_turned"), nc.alloc_semaphore("probs_moved")
    topk = nc.alloc_semaphore("topk_steps")
    loaded, fresh = nc.alloc_semaphore("cache_loaded"), nc.alloc_semaphore("cache_fresh")
    index_q, index_made, index_relu, index_read = (
        nc.alloc_semaphore(f"index_{n}") for n in ("queries", "made", "relu", "read"))
    summed, joined = nc.alloc_semaphore("index_summed"), nc.alloc_semaphore("index_joined")
    corner, selected = nc.alloc_semaphore("index_corner"), nc.alloc_semaphore("index_selected")
    rows_made, rows_turned = nc.alloc_semaphore("outputs_turned"), nc.alloc_semaphore("outputs_moved")
    ready = nc.alloc_semaphore("o_ready")
    dist_loaded = nc.alloc_semaphore("dist_loaded")
    free = nc.alloc_semaphore("dist_cast")

    with nc.Block() as block:

        @block.gpsimd
        def _(pool):
            for a in (q.rearrange("p h q -> p (h q)"), q_s, qi.rearrange("p h q -> p (h q)"),
                      qi_s.rearrange("p b q -> p (b q)"), on_d):
                nc.gpsimd.memset(a, 0.0)

        @block.sync
        def _(sp):
            c = io["consts"]
            sp.dma_start(probs[:, 0:TP], c[:, CONST["distP"][0]:CONST["distP"][0] + TP]).then_inc(dist_loaded, 16)
            sp.dma_start(both, c[:, CONST["both"][0]:CONST["both"][0] + 128]).then_inc(dist_loaded, 16)
            sp.dma_start(on[:, 0, 0:128], c[:, CONST["corner"][0]:CONST["corner"][0] + 128]).then_inc(dist_loaded, 16)
            sp.wait_ge(free, 1)
            sp.dma_start(probs, c[:, CONST["distS"][0]:CONST["distS"][0] + LS]).then_inc(dist_loaded, 16)

        @block.vector
        def _(dve):
            dve.wait_ge(dist_loaded, 48)
            nc.vector.tensor_copy(corner16, on[:, 0, 0:128])
            nc.vector.tensor_copy(ident16, m.c("ident"))
            nc.vector.tensor_copy(distP, probs[:, 0:TP]).then_inc(free, 1)
            nc.vector.memset(lam_rows[0:64], 1.0)
            nc.vector.tensor_copy(lam_rows[64:128], m.lam[64:128, 3:4])
            wn = m.wn[0:64, 8, :].rearrange("p (b h) -> p h b", h=2)
            nc.vector.tensor_copy(w_s[0:64], wn[:, 0, :])
            nc.vector.tensor_copy(w_s[64:128], wn[:, 1, :])
            dve.wait_ge(dist_loaded, 64)
            nc.vector.tensor_copy(distS, probs).then_inc(free, 1)

    class Queries:
        pass

    counts = {"turned": 0, "index": 0, "out": 0}

    def count_on(name, n):
        counts[name] += n
        return counts[name] - n

    def extent(t, qt):
        t.qt, t.sample = qt, qt == NQ
        t.n = TS if t.sample else 128
        t.cols = slice(qt * 128, qt * 128 + t.n)
        t.nk = LS if t.sample else (qt + 1) * 128
        t.blocks = [(b, min(512, t.nk - b)) for b in range(0, t.nk, 512)]
        return t

    def queries(qt, kind):
        t = extent(Queries(), qt)
        t.kind = kind
        t.f = sample_family if t.sample else prompt_family
        tiles = -(-t.nk // 128)
        cuts = list(range(0, tiles - 1 if t.sample else tiles, 3 if t.sample else 4)) + [tiles]
        t.groups = list(zip(cuts, cuts[1:]))
        t.penal = kind == "D" and t.nk > TOPK
        t.qtile = 0 if kind == "C" else 12
        t.load = t.sample and kind == "C"
        t.ahead = 4 if t.load else 0
        t.per = len(t.f.units) * len(t.groups) + t.ahead
        assert t.per % 2 == 0
        t.round = t.f.rounds
        t.f.rounds += 4
        t.turned = count_on("turned", 4 * t.per)
        t.number = count_on("out", 1)
        t.selected = qt - 1
        t.topk = None
        return t

    def index_tile(qt):
        t = extent(Queries(), qt)
        heads = 4 if t.sample else 8
        t.pieces = [(s, b, n) for s in range(heads) for b, n in t.blocks]
        t.base = count_on("index", len(t.pieces))
        t.number = qt - 2
        return t

    def flat(ap):
        return ap.rearrange("p a t -> p (a t)")

    def scores(pe, t, i, h):
        r = i + t.round
        if t.sample and isinstance(i, int) and i == 0:
            pe.wait_ge(rows_turned, t.number)
        if t.load:
            turn_cache_tensor(pe, i + 1, i * t.per + t.turned)
        if t.penal:
            pe.wait_ge(selected, t.selected)
        pe.wait_ge(t.f.Q[h].sem, t.f.Q[h].done(r, "q"))
        first = 0 if t.sample else TP - 128 - t.qt * 128
        dist = (distS if t.sample else distP)[:, first:first + t.nk]
        keys = kt_s if t.sample else flat(p[:, ds(i + 4, 1), :]) if t.kind == "C" else p[:, 20, :]
        for b, n in t.blocks:
            out = m.ps[:, h * 1024 + b:h * 1024 + b + n]
            edge = not t.sample and b + n == t.nk
            nc.tensor.matmul(out, q_s if t.sample else q[:, h, :], keys[:, b:b + n], start=True, stop=False)
            last = nc.tensor.matmul(out, slopes[:, h, :], dist[:, b:b + n], start=False,
                                    stop=not (edge or t.penal))
            if t.penal:
                last = nc.tensor.matmul(out, ident16, penalty[:, b:b + n], start=False, stop=not edge)
            if edge:
                last = nc.tensor.matmul(out[:, n - 128:n], ident16, corner16, start=False, stop=True)
        last.then_inc(*t.f.P[h].step("scores"))

    def groups_of(t, h):
        return [(t.ahead + t.f.units.index(h) * len(t.groups) + j, a, z) for j, (a, z) in enumerate(t.groups)]

    def key_rows(t, kt):
        return min(128, t.nk - kt * 128)

    def bank_of(t, local, i):
        return PT_BANK + (t.turned + local) % 2

    def turn_group(pe, t, i, h, local, a, z):
        if t.turned + local >= 2 or not isinstance(i, int):
            pe.wait_ge(moved, i * t.per + (t.turned + local - 1))
        elif i:
            pe.wait_ge(moved, i * t.per + (t.turned + local - 1))
        for kt in range(a, z):
            k = key_rows(t, kt)
            last = nc.tensor.transpose(
                bank(m, bank_of(t, local, i))[0:k, (kt - a) * 128:(kt - a) * 128 + 128],
                probs[:, h * TP + kt * 128:h * TP + kt * 128 + k], m.c("ident"))
        last.then_inc(turned, 1)

    def value_group(pe, t, i, h, local, a, z):
        pe.wait_ge(moved, i * t.per + (t.turned + local + 1))
        at, width = (0, 128) if t.sample else (h * 128, 128) if t.kind == "C" else (h * 64, 64)
        for kt in range(a, z):
            k = key_rows(t, kt)
            if t.sample:
                v = v_s[0:k, kt, :]
            elif t.kind == "C":
                v = m.vn[0:k, kt, ds(i * 128, 128)]
            else:
                v = m.vd[0:k, kt, 64 * h:64 * h + 64]
            last = nc.tensor.matmul(bank(m, OUT_BANK)[:, at:at + width], pt[0:k, h * 8 + kt, :], v,
                                    start=(kt == 0), stop=(kt == t.groups[-1][1] - 1))
        return last

    def unit_tensor(pe, t, i, h, after):
        r = i + t.round
        pe.wait_ge(t.f.E[h].sem, t.f.E[h].done(r, "exp"))
        groups = groups_of(t, h)
        for local, a, z in groups[:2]:
            turn_group(pe, t, i, h, local, a, z)
        if after and h in after[0].f.units and not after[0].load:
            scores(pe, *after, h)
        if h == 0 and not (isinstance(i, int) and r == 0):
            pe.wait_ge(t.f.N.sem, t.f.N.rounds(r))
        for n, g in enumerate(groups):
            last = value_group(pe, t, i, h, *g)
            if n + 2 < len(groups):
                turn_group(pe, t, i, h, *groups[n + 2])
        last.then_inc(*t.f.O[h].step("out"))
        if after and h in after[0].f.units and after[0].load:
            scores(pe, *after, h)

    def take_wait(i, n):
        if not isinstance(i, int):
            nc.scalar.activation(m.om[:, n:n + 1], m.om[:, n:n + 1], ACT.Copy)

    def load_queries(act, t, i, h):
        r = i + t.round
        if not (isinstance(i, int) and r == 0):
            act.wait_ge(t.f.P[h].sem, t.f.P[h].rounds(r))
            take_wait(i, 6 + h)
        src = flat(p[:, ds(i + t.qtile, 1), t.cols])
        if t.sample:
            for half in (slice(0, 64), slice(64, 128)):
                nc.scalar.activation(q_s[half, half], src[half], ACT.Copy, scale=SCALE)
        else:
            half = slice(64 * h, 64 * h + 64)
            nc.scalar.activation(q[half, h, :], src[half], ACT.Copy, scale=SCALE)
        if t.kind == "C":
            last = nc.scalar.activation(slopes[:, h, :], m.c("ident"), ACT.Copy, scale=m.c("slopeC")[:, ds(i, 1)])
        elif t.sample:
            for g, half in enumerate((slice(0, 64), slice(64, 128))):
                last = nc.scalar.activation(slopes[half, h, :], m.c("ident")[half], ACT.Copy,
                                            scale=m.c("slopeD")[half, ds(i + 4 * g, 1)])
        else:
            last = nc.scalar.activation(slopes[:, h, :], m.c("ident"), ACT.Copy,
                                        scale=m.c("slopeD")[:, ds(i + 4 * h, 1)])
        last.then_inc(*t.f.Q[h].step("q"))

    def exponentials(act, t, i, h):
        r = i + t.round
        act.wait_ge(t.f.V[h].sem, t.f.V[h].done(r, "low"))
        take_wait(i, 4 + h)
        nc.scalar.activation(probs[:, h * TP:h * TP + t.nk], m.ps[:, h * 1024:h * 1024 + t.nk], ACT.Exp,
                             bias=low[:, h:h + 1], accum_out=total[:, t.number % 2, ds(i * 2 + h, 1)])\
            .then_inc(*t.f.E[h].step("exp"))

    def move_group(act, t, i, h, local, a, z):
        act.wait_ge(turned, i * t.per + (t.turned + local + 1))
        full = min(z, t.nk // 128)
        src = bank(m, bank_of(t, local, i)).rearrange("p (t q) -> p t q", t=4)
        if full > a:
            last = nc.scalar.activation(pt[:, h * 8 + a:h * 8 + full, :], src[:, 0:full - a, :], ACT.Copy)
        if full < z:
            last = nc.scalar.activation(pt[0:TS, full:z, :], src[0:TS, full - a:z - a, :], ACT.Copy)
        last.then_inc(moved, 1)

    def maximum(dve, t, i, h):
        r = i + t.round
        dve.wait_ge(t.f.P[h].sem, t.f.P[h].done(r, "scores"))
        nc.vector.tensor_reduce(top[:, h:h + 1], m.ps[:, h * 1024:h * 1024 + t.nk], AX.X, ALU.max)\
            .then_inc(*t.f.V[h].step("max"))
        dve.wait_ge(t.f.V[h].sem, t.f.V[h].done(r, "max"))
        nc.vector.tensor_scalar(low[:, h:h + 1], top[:, h:h + 1], -1.0, None, ALU.mult)\
            .then_inc(*t.f.V[h].step("low"))

    def normalise(dve, t, i):
        r = i + t.round
        N, last = t.f.N, t.f.units[-1]
        n = len(t.f.units)
        if not (isinstance(i, int) and r == 0):
            dve.wait_ge(N.sem, N.rounds(r))
        dve.wait_ge(t.f.E[last].sem, t.f.E[last].done(r, "exp"))
        if not isinstance(i, int):
            nc.vector.memset(small[:, 121:122], 0.0)
        nc.vector.reciprocal(inv[:, 0:n], total[:, t.number % 2, ds(i * 2, n)]).then_inc(*N.step("inv"))
        dve.wait_ge(N.sem, N.done(r, "inv"))
        scale = lam_rows if t.sample and t.kind == "C" else m.lam[:, 3:4] if t.kind == "C" else None
        if scale is None:
            nc.vector.memset(small[:, 120:121], 0.0).then_inc(*N.step("lam"))
        else:
            nc.vector.tensor_scalar(inv[:, 2:3], inv[:, n - 1:n], scale, None, ALU.mult).then_inc(*N.step("lam"))
        dve.wait_ge(N.sem, N.done(r, "lam"))
        dve.wait_ge(t.f.O[last].sem, t.f.O[last].done(r, "out"))
        o, dst = bank(m, OUT_BANK), on[:, t.number % 2, :]

        def scaled(out, src, by):
            return nc.vector.tensor_scalar(out, src, by, None, ALU.mult)

        if t.kind == "C" and t.sample:
            nc.vector.memset(small[:, 120:121], 0.0).then_inc(*N.step("part"))
            scaled(dst[:, ds(i * 128, 128)], o[:, 0:128], inv[:, 2:3]).then_inc(*N.step("norm"))
        elif t.kind == "C":
            nc.vector.tensor_scalar(mix, o[:, 0:128], inv[:, 0:1], None, ALU.mult).then_inc(*N.step("part"))
            dve.wait_ge(N.sem, N.done(r, "part"))
            nc.vector.scalar_tensor_tensor(out=dst[:, ds(i * 128, 128)], in0=o[:, 128:256], scalar=inv[:, 2:3],
                                           in1=mix, op0=ALU.mult, op1=ALU.add).then_inc(*N.step("norm"))
        elif t.sample:
            scaled(on_d[0:64, ds(i * 128, 64)], o[0:64, 0:64], inv[0:64, 0:1]).then_inc(*N.step("part"))
            scaled(on_d[64:128, ds(i * 128 + 64, 64)], o[64:128, 64:128], inv[64:128, 0:1]).then_inc(*N.step("norm"))
        else:
            scaled(dst[:, ds(i * 128, 64)], o[:, 0:64], inv[:, 0:1]).then_inc(*N.step("part"))
            scaled(dst[:, ds(i * 128 + 64, 64)], o[:, 64:128], inv[:, 1:2]).then_inc(*N.step("norm"))

    def turn_outputs(pe, t):
        pe.wait_ge(t.f.N.sem, t.f.N.rounds(t.round + 4))
        if t.number:
            pe.wait_ge(rows_turned, t.number)
        src = on_d if t.sample and t.kind == "D" else on[:, t.number % 2, :]
        for a in range(4):
            out = bank(m, TURN_BANK)
            if t.sample:
                last = nc.tensor.matmul(out[:, a * 128:a * 128 + 64], src[:, a * 128:a * 128 + 128], both[:, 0:64],
                                        start=True, stop=True)
            else:
                last = nc.tensor.transpose(out[:, a * 128:a * 128 + 128], src[:, a * 128:a * 128 + 128],
                                           m.c("ident"))
        last.then_inc(rows_made, 1)

    def move_outputs(act, t):
        act.wait_ge(rows_made, t.number + 1)
        src = heads4(bank(m, TURN_BANK))[:, :, 0:t.n]
        nc.scalar.activation(p[:, t.qtile:t.qtile + 4, t.cols], src, ACT.Copy).then_inc(rows_turned, 1)

    def turn_cache_tensor(pe, n, at):
        pe.wait_ge(loaded, n * 32 + 32)
        for j in range(4):
            pe.wait_ge(moved, at + (j - 1))
            for kt in range(4):
                last = nc.tensor.transpose(bank(m, PT_BANK + j % 2)[:, kt * 128:kt * 128 + 128],
                                           cache_rows[:, 4 * j + kt, :], m.c("ident"))
            last.then_inc(turned, 1)
        pe.wait_ge(fresh, n + 1)

    def turn_cache_scalar(act, i, at, kind):
        for j in range(4):
            act.wait_ge(turned, at + (j + 1))
            nc.scalar.activation(kt_s[:, 512 * j:512 * j + 512], bank(m, PT_BANK + j % 2), ACT.Copy)\
                .then_inc(moved, 1)
        if kind == "C":
            new_k, new_v = flat(p[:, ds(i + 4, 1), TP:T]), m.vn[0:TS, 8, ds(i * 128, 128)]
        else:
            new_k, new_v = p[:, 21 if kind == "I" else 20, TP:T], m.vd[0:TS, 8, :]
        if kind != "I":
            nc.scalar.activation(v_s[0:TS, NPT, :], new_v, ACT.Copy)
        nc.scalar.activation(kt_s[:, PAST:LS], new_k, ACT.Copy).then_inc(fresh, 1)

    def index_tensor(pe, t):
        pe.wait_ge(index_q, t.number + 1)
        keys, queries_i = (kt_s, qi_s) if t.sample else (p[:, 21, :], qi)
        for c, (s, b, n) in enumerate(t.pieces):
            if c >= 4:
                pe.wait_ge(index_relu, t.base + c - 3)
            nc.tensor.matmul(bank(m, c % 4)[:, 0:n], queries_i[:, s, :], keys[:, b:b + n],
                             start=True, stop=True).then_inc(index_made, 1)
        pe.wait_ge(index_relu, t.base + len(t.pieces))
        if t.sample:
            pe.wait_ge(rows_turned, 2 * NQ - 1)
            pe.wait_ge(index_read, t.base + len(t.pieces))
            for c, (b, n) in enumerate(t.blocks):
                nc.tensor.matmul(m.ps[:, b:b + n], both, index[:, b:b + n], start=True, stop=True)\
                    .then_inc(summed, 1)
            pe.wait_ge(joined, len(t.blocks))

    def index_scalar(act, t):
        if t.sample:
            for h, half in enumerate((slice(0, 64), slice(64, 128))):
                last = nc.scalar.activation(qi_s[half, :, half], p[half, 16:20, t.cols], ACT.Copy)
        else:
            if t.number:
                act.wait_ge(index_made, t.base)
            nc.scalar.activation(qi[0:64, 0:4, 0:t.n], p[0:64, 16:20, t.cols], ACT.Copy)
            last = nc.scalar.activation(qi[64:128, 4:8, 0:t.n], p[64:128, 16:20, t.cols], ACT.Copy)
        last.then_inc(index_q, 1)
        for c, (s, b, n) in enumerate(t.pieces):
            act.wait_ge(index_made, t.base + c + 1)
            if t.base + c >= 4:
                act.wait_ge(index_read, t.base + c - 3)
            nc.scalar.activation(relu[:, c % 4, 0:n], bank(m, c % 4)[:, 0:n], ACT.Relu).then_inc(index_relu, 1)

    def index_vector(dve, t):
        blocks = len(t.blocks)
        for c, (s, b, n) in enumerate(t.pieces):
            dve.wait_ge(index_relu, t.base + c + 1)
            head = 2 * (s % 4) + s // 4
            wt = w_s[:, s:s + 1] if t.sample else m.wn[:, t.qt, head:head + 1]
            if s == 0:
                nc.vector.tensor_scalar(index[:, b:b + n], relu[:, c % 4, 0:n], wt, None, ALU.mult)\
                    .then_inc(index_read, 1)
            else:
                dve.wait_ge(index_read, t.base + c + 1 - blocks)
                nc.vector.scalar_tensor_tensor(out=index[:, b:b + n], in0=relu[:, c % 4, 0:n], scalar=wt,
                                               in1=index[:, b:b + n], op0=ALU.mult, op1=ALU.add)\
                    .then_inc(index_read, 1)
        dve.wait_ge(index_read, t.base + len(t.pieces))
        if t.sample:
            for c, (b, n) in enumerate(t.blocks):
                dve.wait_ge(summed, c + 1)
                nc.vector.tensor_copy(index[:, b:b + n], m.ps[:, b:b + n]).then_inc(joined, 1)
            dve.wait_ge(joined, blocks)
        else:
            nc.vector.memset(index[0:64, t.nk - 64:t.nk], -FAR).then_inc(corner, 1)
            dve.wait_ge(corner, t.number + 1)

    EACH = TOPK // 8 // 8

    def select(dve, t, done, i, steps):
        for k in steps:
            at = i * (2 * EACH) + (done + 2 * k)
            nc.vector.max(best, index[:, 0:t.nk]).then_inc(topk, 1)
            dve.wait_ge(topk, at + 1)
            if not isinstance(i, int):
                nc.vector.memset(small[:, 122:123], 0.0)
            nc.vector.match_replace(index[:, 0:t.nk], best, index[:, 0:t.nk], TAKEN).then_inc(topk, 1)
            dve.wait_ge(topk, at + 2)
            if not isinstance(i, int):
                nc.vector.memset(small[:, 123:124], 0.0)

    def make_penalty(dve, t):
        nc.vector.tensor_scalar(penalty[:, 0:t.nk], index[:, 0:t.nk], TAKEN / 2, -FAR, ALU.is_gt, ALU.mult)\
            .then_inc(selected, 1)
        dve.wait_ge(selected, t.number + 1)

    runs = [(None, [queries(0, "C"), queries(0, "D"), queries(1, "C")])]
    for qt in range(2, NQ + 1):
        if qt == NQ:
            cache_index = ("I", 0, count_on("turned", 4))
        t = index_tile(qt)
        run = [queries(qt - 1, "D")]
        if qt < NQ:
            run.append(queries(qt, "C"))
            run[1].topk = t
        run[0].topk = t
        runs.append((t, run))
    sample_c = queries(NQ, "C")
    sample_c.topk = runs[-1][0]
    runs.append((None, [sample_c]))
    cache_d = ("D", 5, count_on("turned", 4))
    sample_d = queries(NQ, "D")
    runs.append(("cache", [sample_d]))
    sample_index = runs[-3][0]
    for n, t in enumerate(x for _, run in runs for x in run):
        t.done = 0
    for t, run in runs:
        for x in run:
            if x.topk:
                x.done = (x.topk.number * 8 + (4 if x.kind == "C" else 0)) * 2 * EACH

    def each_round(engine, run, body):
        for n, t in enumerate(run):
            start = 0
            if t.round == 0:
                body(t, 0, (t, 1))
                start = 1
            with engine.Fori(start, 3) as i:
                body(t, i, (t, i + 1))
            body(t, 3, (run[n + 1], 0) if n + 1 < len(run) else None)
            yield t

    with nc.Block() as block:

        @block.tensor
        def _(pe):
            for before, run in runs:
                if before == "cache":
                    turn_cache_tensor(pe, cache_d[1], cache_d[2])
                elif before:
                    if before.sample:
                        turn_cache_tensor(pe, cache_index[1], cache_index[2])
                    index_tensor(pe, before)
                for h in run[0].f.units:
                    scores(pe, run[0], 0, h)

                def body(t, i, after):
                    for h in t.f.units:
                        unit_tensor(pe, t, i, h, after)

                for t in each_round(pe, run, body):
                    turn_outputs(pe, t)

        @block.scalar
        def _(act):
            for before, run in runs:
                if before == "cache":
                    turn_cache_scalar(act, None, cache_d[2], "D")
                elif before:
                    if before.sample:
                        turn_cache_scalar(act, None, cache_index[2], "I")
                    index_scalar(act, before)
                if run[0].load:
                    turn_cache_scalar(act, 0, run[0].turned, "C")
                for h in run[0].f.units:
                    load_queries(act, run[0], 0, h)
                exponentials(act, run[0], 0, 0)

                def body(t, i, after):
                    for h in t.f.units:
                        if after and not after[0].load:
                            load_queries(act, *after, h)
                        for g in groups_of(t, h):
                            move_group(act, t, i, h, *g)
                        if h + 1 in t.f.units:
                            exponentials(act, t, i, h + 1)
                    if after and after[0].load:
                        act.wait_ge(t.f.P[0].sem, t.f.P[0].rounds(t.round + 1) + i)
                        act.wait_ge(t.f.O[0].sem, t.f.O[0].rounds(t.round + 1) + i)
                        turn_cache_scalar(act, after[1], after[1] * after[0].per + after[0].turned, "C")
                        load_queries(act, *after, 0)
                    if after:
                        exponentials(act, *after, 0)

                for t in each_round(act, run, body):
                    move_outputs(act, t)

        @block.vector
        def _(dve):
            for before, run in runs:
                if before and before != "cache":
                    if before.number:
                        make_penalty(dve, runs[before.number][0])
                    index_vector(dve, before)
                elif before == "cache":
                    make_penalty(dve, sample_index)
                maximum(dve, run[0], 0, 0)

                def body(t, i, after):
                    steps = range(EACH if t.topk else 0)
                    early = steps[:EACH // 2] if len(t.f.units) > 1 else steps[:0]
                    for h in t.f.units[1:]:
                        maximum(dve, t, i, h)
                    select(dve, t.topk, t.done, i, early)
                    if after:
                        maximum(dve, *after, 0)
                    normalise(dve, t, i)
                    select(dve, t.topk, t.done, i, steps[len(early):])

                for t in each_round(dve, run, body):
                    pass

        @block.sync
        def _(sp):
            ck = io["cache_c_k"][0, 0].rearrange("(t p) h m d -> p t (h m d)", p=128)
            cv = io["cache_c_v"][0, 0].rearrange("(t p) h e -> p t (h e)", p=128)
            f, g = prompt_family, sample_family
            last_c = [t for _, run in runs for t in run if t.kind == "C" and not t.sample][-1]
            sp.wait_ge(f.O[1].sem, f.O[1].rounds(last_c.round + 4))
            ki = io["cache_d_kidx"][0, 0].rearrange("(t p) d -> p t d", p=128)
            for h in range(2):
                sp.dma_start(cache_rows[:, :, 64 * h:64 * h + 64], ki).then_inc(loaded, 16)
            sp.wait_ge(index_made, sample_index.base + len(sample_index.pieces))
            sp.dma_start(cache_rows, ck[:, :, 0:128]).then_inc(loaded, 16)
            sp.dma_start(v_s[:, 0:NPT, :], cv[:, :, 0:128]).then_inc(loaded, 16)
            with sp.Fori(1, 4) as i:
                sp.wait_ge(g.P[0].sem, i)
                sp.dma_start(cache_rows, ck[:, :, ds(i * 128, 128)]).then_inc(loaded, 16)
                sp.wait_ge(g.O[0].sem, i)
                sp.dma_start(v_s[:, 0:NPT, :], cv[:, :, ds(i * 128, 128)]).then_inc(loaded, 16)
            sp.wait_ge(g.P[0].sem, 4)
            sp.dma_start(cache_rows, io["cache_d_k"][0, 0].rearrange("(t p) g d -> p t (g d)", p=128))\
              .then_inc(loaded, 16)
            sp.wait_ge(g.O[0].sem, 4)
            sp.dma_start(v_s[:, 0:NPT, :], io["cache_d_v"][0, 0].rearrange("(t p) g d -> p t (g d)", p=128))\
              .then_inc(loaded, 16)


def diff_finish(m):
    nc = m.nc
    w = m.odd_work
    sq, rstd = (m.arena[:, w + n * T:w + n * T + T] for n in range(2))
    gain = m.arena[:, w + 2 * T:w + 2 * T + 129]
    ones = gain[:, 1:129]
    P, V, A = Steps(nc, "f_pe", ["sum"]), Steps(nc, "f_dve", ["rstd", "normal"]), Steps(nc, "f_act", ["sq", "std"])
    ready = nc.alloc_semaphore("f_ready")
    with nc.Block() as block:

        @block.tensor
        def _(pe):
            pe.wait_ge(ready, 1)
            for h in range(4):
                pe.wait_ge(A.sem, A.done(h, "sq"))
                for b in range(4):
                    last = nc.tensor.matmul(m.ps[:, b * 512:b * 512 + TB], ones, sq[:, b * TB:(b + 1) * TB],
                                            start=True, stop=True)
                last.then_inc(*P.step("sum"))

        @block.scalar
        def _(act):
            for h in range(4):
                nc.scalar.activation(sq, m.p[:, h, :], ACT.Square).then_inc(*A.step("sq"))
                act.wait_ge(P.sem, P.done(h, "sum"))
                if h:
                    act.wait_ge(V.sem, V.done(h - 1, "normal"))
                nc.scalar.activation(blocks4(rstd), linear_out(m, 0), ACT.Sqrt, bias=m.eps(0)).then_inc(*A.step("std"))

        @block.vector
        def _(dve):
            nc.vector.memset(ones, 1.0 / 128)
            nc.vector.tensor_scalar(gain[:, 0:1], m.col(ROWS["subln"]), 1.0 - LAM_INIT, None, ALU.mult)\
                .then_inc(ready, 1)
            dve.wait_ge(ready, 1)
            for h in range(4):
                dve.wait_ge(A.sem, A.done(h, "std"))
                nc.vector.reciprocal(rstd, rstd).then_inc(*V.step("rstd"))
                dve.wait_ge(V.sem, V.done(h, "rstd"))
                nc.vector.scalar_tensor_tensor(out=m.p[:, h, :], in0=m.p[:, h, :], scalar=gain[:, 0:1], in1=rstd,
                                               op0=ALU.mult, op1=ALU.mult).then_inc(*V.step("normal"))


def store(m):
    nc, io = m.nc, m.io
    rows = m.arena[:, m.work:m.work + 2 * D].rearrange("p (s d) -> p s d", s=2)
    turned, moved = nc.alloc_semaphore("y_turned"), nc.alloc_semaphore("y_moved")
    stored = [nc.alloc_semaphore(f"y_stored{s}") for s in range(2)]
    with nc.Block() as block:

        @block.tensor
        def _(pe):
            for t in range(9):
                n = 128 if t < 8 else TS
                if t >= 2:
                    pe.wait_ge(moved, t - 1)
                for k in range(8):
                    at = (t % 2) * 1024 + k * 128
                    last = nc.tensor.transpose(m.ps[0:n, at:at + 128], m.x[:, k, t * 128:t * 128 + n], m.c("ident"))
                last.then_inc(turned, 1)

        @block.vector
        def _(dve):
            for t in range(9):
                n = 128 if t < 8 else TS
                dve.wait_ge(turned, t + 1)
                if t >= 2:
                    dve.wait_ge(stored[t % 2], 16 * (t // 2))
                nc.vector.tensor_copy(rows[0:n, t % 2, :], m.ps[0:n, (t % 2) * 1024:(t % 2) * 1024 + 1024])\
                    .then_inc(moved, 1)

        @block.sync
        def _(sp):
            for t in range(9):
                sp.wait_ge(moved, t + 1)
                out = io["y_prompt"][0, t * 128:t * 128 + 128] if t < 8 else io["y_sample"][0]
                sp.dma_start(out, rows[0:128 if t < 8 else TS, t % 2, :]).then_inc(stored[t % 2], 16)
            sp.wait_ge(stored[0], 16 * 5)
            sp.wait_ge(stored[1], 16 * 4)


def build(nc, io):
    io["x_kept"] = nc.dram_tensor("x_kept", (128, KD * T), F32, kind="Internal").ap()
    m = Core()
    m.nc, m.io = nc, io
    columns = 53200
    m.arena_at = (nc.sbuf_base + 31) // 32 * 32
    m.arena = nc.alloc_sbuf_tensor("arena", [128, columns], F32)
    m.rounded = {}
    m.ps = nc.alloc_psum_tensor("psum", [128, 4096], F32)
    at = [0]

    def room(n):
        at[0] += n
        return m.arena[:, at[0] - n:at[0]]

    m.nconst = CONST["distP"][0]
    m.const = room(m.nconst)
    m.cols = room(128)
    m.sink = room(8)
    m.lam_in = room(256).rearrange("p (v d) -> p v d", v=4)
    m.lam = room(8)
    m.om = room(8)
    m.c = lambda name: m.const[:, CONST[name][0]:CONST[name][0] + CONST[name][1]]
    m.eps = lambda n: m.c("eps")[:, n:n + 1]
    m.col = lambda n: m.cols[:, n:n + 1]
    m.linears = Ring(m)
    m.joined = nc.alloc_semaphore("x_joined")
    m.mlp_sems = [nc.alloc_semaphore(f"mlp_{n}") for n in ("relu", "added", "squared", "hidden_high", "hidden_split", "scaled")]
    room(-at[0] % 8)
    m.x_at = at[0]
    m.x = room(KD * T).rearrange("p (k t) -> p k t", k=KD)
    after_x = at[0]
    m.limit = columns
    m.work = after_x
    start(m)

    m.p = m.arena[:, after_x:after_x + 21 * T].rearrange("p (k t) -> p k t", k=21)
    m.work = after_x + 21 * T
    m.ring, m.high = m.work, m.arena[:, columns - 8 * T:columns]
    assert m.ring + RING <= columns - 8 * T
    project_even(m)
    window_attention(m)
    m.state = m.arena[:, m.work:m.work + 512]
    m.work += 512
    rwkv_prepare(m)
    rwkv_chunks(m)
    rwkv_finish(m)
    m.ring = m.work
    project_out(m, "out0", io["w_out_even"][0], lambda k: m.p[:, k, :], 0)
    layer_norm(m, "ln0", ROWS["mixg"], ROWS["mixb"])
    m.work = after_x
    mlp(m, 0)
    m.work += 8 * T
    layer_norm(m, "ln1", ROWS["ffng"], ROWS["ffnb"], m.acc)
    m.p = m.arena[:, after_x:after_x + 24 * T].rearrange("p (k t) -> p k t", k=24)
    m.work = after_x + 24 * T
    m.ring = m.work
    assert m.ring + RING <= columns - 8 * T
    project_odd(m)
    turn_rows(m)
    odd_attention(m)
    diff_finish(m)
    m.ring = m.work
    project_out(m, "out1", io["w_out_odd"][0], lambda k: m.p[:, k if k < 4 else 8 + k, :], 4)
    layer_norm(m, "ln2", ROWS["mixg"] + 8, ROWS["mixb"] + 8)
    m.work = after_x
    mlp(m, 1)
    m.work += 8 * T
    layer_norm(m, "ln3", ROWS["ffng"] + 8, ROWS["ffnb"] + 8, m.acc)
    store(m)


_INS = ["x_prompt", "x_sample", "cache_a_k", "cache_a_v", "state_b_shift", "state_b_wkv", "cache_c_k", "cache_c_v",
        "cache_d_k", "cache_d_v", "cache_d_kidx", "w_in_even", "sink_a", "mu_b", "w0_b", "w_up_b", "a0_b", "a_up_b",
        "g_up_b", "k_k_b", "k_a_b", "r_k_b", "lnx_g_b", "lnx_b_b", "w_out_even", "w_in_odd", "lam_q1_c", "lam_k1_c",
        "lam_q2_c", "lam_k2_c", "subln_g_c", "w_out_odd", "ln_mix_g", "ln_mix_b", "ln_ffn_g", "ln_ffn_b",
        "w_ff_up", "w_ff_down"]
_OUTS = [("y_prompt", (1, TP, D)), ("y_sample", (1, TS, D)),
         ("a_k_p", (1, 1, 128, 2, HD)), ("a_v_p", (1, 1, 128, 2, HD)), ("b_shift_p", (1, 1, 1, 1792)),
         ("b_wkv_p", (1, 1, 8, HD, HD)), ("c_k_p", (1, 1, TP, 4, 2, HD)), ("c_v_p", (1, 1, TP, 4, 128)),
         ("d_k_p", (1, 1, TP, 2, HD)), ("d_v_p", (1, 1, TP, 2, HD)), ("d_kidx_p", (1, 1, TP, HD)),
         ("a_k_s", (1, 1, 128, 2, HD)), ("a_v_s", (1, 1, 128, 2, HD)), ("b_shift_s", (1, 1, 1, 1792)),
         ("b_wkv_s", (1, 1, 8, HD, HD)), ("c_k_s", (1, 1, TS, 4, 2, HD)), ("c_v_s", (1, 1, TS, 4, 128)),
         ("d_k_s", (1, 1, TS, 2, HD)), ("d_v_s", (1, 1, TS, 2, HD)), ("d_kidx_s", (1, 1, TS, HD))]


def kernel(**inputs):
    import concourse.bacc as _bacc
    from concourse.bass_utils import run_bass_kernel_spmd as _run

    nc = _bacc.Bacc("TRN2", target_bir_lowering=False, num_devices=1)
    arrays, io = {}, {}
    for name in _INS:
        a = np.ascontiguousarray(inputs[name])
        arrays[f"in_{name}"] = a
        io[name] = nc.dram_tensor(f"in_{name}", a.shape, F32, kind="ExternalInput").ap()
    arrays["in_consts"] = constants()
    io["consts"] = nc.dram_tensor("in_consts", (128, NCONST), F32, kind="ExternalInput").ap()
    for name, shape in _OUTS:
        io[name] = nc.dram_tensor(f"out_{name}", shape, F32, kind="ExternalOutput").ap()
    build(nc, io)
    r = _run(nc, [arrays], core_ids=[0])
    return tuple(r.results[0][f"out_{name}"] for name, _ in _OUTS)
```

```python
import math

import numpy as np
import concourse.bass as bass
from concourse import mybir

F32 = mybir.dt.float32
F32R = mybir.dt.float32r
F16 = mybir.dt.float16
BF16 = mybir.dt.bfloat16
ALU = mybir.AluOpType
ACT = mybir.ActivationFunctionType
AX = mybir.AxisListType

D = 1024
KD = D // 128
TP = 1024
TS = 64
T = TP + TS
TB = T // 4
NQ = TP // 128
PAST = 2048
LS = PAST + TS
NPT = PAST // 128
CH = 64
HD = 64
NCHUNK = TP // CH
FF = 4096
ALPHA = 4 ** 0.25
LN_EPS = 1e-5
GN_EPS = 64e-5
DECAY = math.exp(-0.5)
LAM_INIT = 0.8 - 0.6 * math.exp(-0.3)
TOPK = 256
SCALE = HD ** -0.5
FAR = 1e30
TAKEN = -3e38

ROWS = {}
_at = 0
for _n, _c in (("mu", 14), ("w0", 4), ("a0", 4), ("kk", 4), ("ka", 4), ("rk", 4), ("lnxg", 4), ("lnxb", 4),
               ("mixg", 16), ("mixb", 16), ("ffng", 16), ("ffnb", 16), ("subln", 1), ("shift", 14)):
    ROWS[_n] = _at
    _at += _c
NROWS = _at

CONST = {}
_at = 0
for _n, _c in (("ident", 128), ("mean", 128), ("heads", 128), ("slopeC", 4), ("slopeD", 8), ("eps", 3),
               ("strict", 128), ("upto", 128), ("low1", 128), ("up1", 128), ("low2", 128), ("low4", 128),
               ("low8", 128), ("low16", 128), ("low32", 128), ("reset", T), ("distA", 256),
               ("distP", TP), ("distS", LS), ("corner", 128), ("both", 128)):
    CONST[_n] = (_at, _c)
    _at += _c
NCONST = _at


def constants():
    c = np.zeros((128, NCONST), np.float32)

    def put(name, a):
        o, n = CONST[name]
        c[:, o:o + n] = a

    i = np.arange(128)
    p, q = i[:, None], i[None, :]
    same = (p // 64) == (q // 64)
    put("ident", p == q)
    put("mean", 1.0 / D)
    put("heads", same)
    put("slopeC", -2.0 ** (-8.0 * np.arange(1, 5) / 4)[None, :])
    put("slopeD", -2.0 ** (-8.0 * np.arange(1, 9) / 8)[None, :])
    put("eps", np.array([LN_EPS, 1e-12, GN_EPS])[None, :])
    put("strict", same & (p < q))
    put("upto", same & (p <= q))
    for n in (1, 2, 4, 8, 16, 32):
        low = (p // (2 * n) == q // (2 * n)) & (p // n > q // n)
        put(f"low{n}", low)
        if n == 1:
            put("up1", low.T)
    put("reset", (np.arange(T) % CH != 0)[None, :])
    x = np.arange(256)[None, :]
    dist = np.abs(p + 128 - x).astype(np.float64)
    put("distA", np.where(np.where(p < 64, x < 192, x >= 64), dist, FAR))
    x = np.arange(TP)[None, :]
    dist = np.abs(p + TP - 128 - x).astype(np.float64)
    put("distP", dist)
    put("corner", np.where((p < 64) & (q >= 64), -FAR, 0.0))
    put("both", p % 64 == q % 64)
    x = np.arange(LS)[None, :]
    put("distS", np.abs(p % 64 + PAST - x) - 1024)
    return c


class Steps:

    def __init__(self, nc, name, steps):
        self.sem, self.steps, self.at = nc.alloc_semaphore(name), list(steps), 0

    def step(self, name):
        assert self.steps[self.at % len(self.steps)] == name, (name, self.steps[self.at % len(self.steps)])
        self.at += 1
        return self.sem, 1

    def done(self, t, name):
        return t * len(self.steps) + self.steps.index(name) + 1

    def rounds(self, t):
        return t * len(self.steps)


def ds(start, n):
    return bass.ds(start, n) if not isinstance(start, int) else slice(start, start + n)


def repeat(engine, parts, body):
    for start, end in parts:
        if end - start == 1:
            body(start, start == 0)
        else:
            with engine.Fori(start, end) as i:
                body(i, False)


class Core:
    pass


def blocks4(ap):
    return ap.rearrange("p (b t) -> p b t", b=4)


def bank(m, b):
    return m.ps[:, b * 512:(b + 1) * 512]


def linear_out(m, buf):
    return m.ps[:, buf * 2048:(buf + 1) * 2048].rearrange("p (b t) -> p b t", b=4)[:, :, 0:TB]


def heads4(ap):
    return ap.rearrange("p (h c) -> p h c", h=4)


SLOTS = 4
HIGHS = 2
RING = (SLOTS + HIGHS) * 1024


def rounded(m, ap):
    size = math.prod(ap.shape[1:])
    key = (ap.offset, size)
    if key not in m.rounded:
        m.rounded[key] = m.nc.alloc_sbuf_tensor_at(f"rounded_{ap.offset}_{size}", [128, size], F32R,
                                                   offset=m.arena_at + 4 * ap.offset)
    whole = m.rounded[key][:, 0:size]
    return whole if len(ap.shape) == 2 else whole.rearrange("p (k c) -> p k c", k=ap.shape[1])


class Ring:

    def __init__(self, m):
        nc, self.m = m.nc, m
        self.loaded = [nc.alloc_semaphore(f"weights_loaded{s}") for s in range(SLOTS)]
        self.weights_high = nc.alloc_semaphore("weights_high")
        self.weights_split = nc.alloc_semaphore("weights_split")
        self.used = nc.alloc_semaphore("weights_used")
        self.freed = nc.alloc_semaphore("linear_freed")
        self.x_high, self.x_split = nc.alloc_semaphore("operand_high"), nc.alloc_semaphore("operand_split")
        self.next = (0, 0, 0, 0)

    def begin(self, at, ndma, pieces, tiles):
        self.pieces, self.loads, self.operands, self.tiles = self.next
        self.ndma = ndma
        self.next = (self.pieces + pieces, self.loads + pieces // SLOTS * ndma * 16,
                     self.operands + 8, self.tiles + tiles)
        arena = self.m.arena
        self.low = arena[:, at:at + SLOTS * 1024].rearrange("p (s k c) -> p s k c", s=SLOTS, k=8)
        self.high = arena[:, at + SLOTS * 1024:at + RING].rearrange("p (s k c) -> p s k c", s=HIGHS, k=8)
        return self

    def load(self, sp, at, u, first, pairs):
        if not first or u >= SLOTS:
            sp.wait_ge(self.used, at + (self.pieces + u + 1 - SLOTS))
        for dst, src in pairs(self.low[:, u % SLOTS]):
            sp.dma_start(dst, src).then_inc(self.loaded[u % SLOTS], 16)

    def split(self, dve, at, fills, u, first):
        nc, m = self.m.nc, self.m
        low, high = self.low[:, u % SLOTS], self.high[:, u % HIGHS]
        dve.wait_ge(self.loaded[u % SLOTS], fills * 16 * self.ndma + (self.loads + (u // SLOTS + 1) * 16 * self.ndma))
        if not first or u >= HIGHS:
            dve.wait_ge(self.used, at + (self.pieces + u + 1 - HIGHS))
        nc.vector.tensor_copy(rounded(m, high), low).then_inc(self.weights_high, 1)
        dve.wait_ge(self.weights_high, at + (self.pieces + u + 1))
        nc.vector.tensor_tensor(rounded(m, low), low, rounded(m, high), ALU.subtract).then_inc(self.weights_split, 1)

    def multiply(self, pe, at, u, x_high, x_low, ready=None):
        nc, m = self.m.nc, self.m
        pe.wait_ge(self.weights_split, at + (self.pieces + u + 1))
        low, high = self.low[:, u % SLOTS], self.high[:, u % HIGHS]
        for k in range(8):
            if ready:
                ready(k)
            terms = ((low, x_high), (high, x_low), (high, x_high))
            for n, (w, x) in enumerate(terms):
                for b in range(4):
                    out = (u % 2) * 2048 + b * 512
                    last = nc.tensor.matmul(
                        m.ps[:, out:out + TB], rounded(m, w)[:, k, :], rounded(m, x(k))[:, b * TB:(b + 1) * TB],
                        start=(k == 0 and n == 0), stop=(k == 7 and n == 2), skip_group_check=True)
        last.then_inc(self.used, 1)


def linear(m, name, tiles, loads, ndma, parts, operand, evacuate, on_vector=False, then=None):
    nc = m.nc
    per = 4
    rounds = tiles // per
    ring = m.linears.begin(m.ring, ndma, tiles, tiles)
    high = m.high.rearrange("p (k t) -> p k t", k=8)
    with nc.Block() as block:

        @block.sync
        def _(sp):
            def fill(i, first):
                for u in range(per):
                    ring.load(sp, i * per, u, first, lambda slot: loads(i, u, slot))

            repeat(sp, parts, fill)

        @block.tensor
        def _(pe):
            def multiply(i, first):
                for u in range(per):
                    if not first or u >= 2:
                        pe.wait_ge(ring.freed, i * per + (ring.tiles + u - 1))
                    ready = (lambda k: pe.wait_ge(ring.x_split, ring.operands + k + 1)) if first and u == 0 else None
                    ring.multiply(pe, i * per, u, lambda k: high[:, k, :], operand, ready)

            repeat(pe, [(0, 1), (1, rounds)], multiply)

        def leave(engine, i, u):
            engine.wait_ge(ring.used, i * per + (ring.pieces + u + 1))
            evacuate(engine, i * per + u, linear_out(m, u % 2)).then_inc(ring.freed, 1)
            if then:
                engine.wait_ge(ring.freed, i * per + (ring.tiles + u + 1))
                then(i * per + u)

        @block.scalar
        def _(act):
            for k in range(8):
                nc.scalar.activation(rounded(m, high[:, k, :]), operand(k), ACT.Copy).then_inc(ring.x_high, 1)
            if not on_vector:
                repeat(act, [(0, 1), (1, rounds)], lambda i, first: [leave(act, i, u) for u in range(per)])

        @block.vector
        def _(dve):
            def body(i, first):
                for u in range(per):
                    ring.split(dve, i * per, i, u, first)
                    if first and u == 0:
                        for k in range(8):
                            dve.wait_ge(ring.x_high, ring.operands + k + 1)
                            nc.vector.tensor_tensor(rounded(m, operand(k)), operand(k), rounded(m, high[:, k, :]),
                                                    ALU.subtract)\
                                .then_inc(ring.x_split, 1)
                    if on_vector and not (first and u == 0):
                        if u:
                            leave(dve, i, u - 1)
                        else:
                            leave(dve, i - 1, per - 1)

            repeat(dve, [(0, 1), (1, rounds)], body)
            if on_vector:
                leave(dve, rounds - 1, per - 1)


def sum_tile(m, tile, u):
    nc = m.nc
    if u == 0:
        nc.vector.tensor_copy(m.sum, tile).then_inc(m.tile_summed, 1)
    else:
        nc.vector.wait_ge(m.tile_summed, m.tiles_summed)
        nc.vector.tensor_tensor(m.sum, m.sum, tile, ALU.add).then_inc(m.tile_summed, 1)
    m.tiles_summed += 1


def join(m, pool, joined):
    high = m.high.rearrange("p (k t) -> p k t", k=8)
    for k in range(8):
        m.nc.gpsimd.tensor_tensor(m.x[:, k, :], rounded(m, m.x[:, k, :]), rounded(m, high[:, k, :]), ALU.add)\
            .then_inc(joined, 1)


def weight_view(w):
    return w.rearrange("(k p) c -> p k c", p=128)


def halves(slot, src):
    return [(slot[:, 0:4], src[:, 0:4]), (slot[:, 4:8], src[:, 4:8])]


def grouped_columns(slot, w, base, a):
    return [(slot[:, :, 64 * g:64 * g + 64], w[:, :, base + 256 * g + 64 * a:base + 256 * g + 64 * a + 64])
            for g in range(2)]


def project_even(m):
    w = weight_view(m.io["w_in_even"][0])

    def loads(i, u, slot):
        if isinstance(i, int) and i == 0:
            return grouped_columns(slot, w, 0, u)
        if isinstance(i, int):
            at = (512, 640, 2304, 2432)[u]
            return halves(slot, w[:, :, at:at + 128])
        return halves(slot, w[:, :, ds(i * 512 + (256 + 128 * u), 128)])

    def evacuate(act, tile, out):
        return m.nc.scalar.activation(blocks4(tile_of(m.p, tile)), out, ACT.Copy)

    linear(m, "in0", 20, loads, 2, [(0, 1), (1, 4), (4, 5)], lambda k: m.x[:, k, :], evacuate)


def tile_of(p, tile):
    if isinstance(tile, int):
        return p[:, tile, :]
    return p[:, ds(tile, 1), :].rearrange("p a t -> p (a t)")


def project_odd(m):
    w = weight_view(m.io["w_in_odd"][0])

    def loads(i, u, slot):
        if isinstance(i, int) and i == 3:
            return grouped_columns(slot, w, 1536, u)
        if isinstance(i, int) and i == 5:
            if u == 1:
                return [(slot[:, :, 0:64], w[:, :, 2816:2880]), (slot[:, :, 64:128], w[:, :, 2816:2880])]
            if u == 3:
                return [(slot[:, :, 0:8], w[:, :, 2880:2888]), (slot[:, :, 8:128], w[:, :, 0:120])]
            at = {0: 2048, 2: 2176}[u]
            return halves(slot, w[:, :, at:at + 128])
        if isinstance(i, int) and i == 4:
            return halves(slot, w[:, :, 2304 + 128 * u:2304 + 128 * u + 128])
        return halves(slot, w[:, :, ds(i * 512 + 128 * u, 128)])

    def evacuate(act, tile, out):
        return m.nc.scalar.activation(blocks4(tile_of(m.p, tile)), out, ACT.Copy)

    linear(m, "in1", 24, loads, 2, [(0, 1), (1, 3), (3, 4), (4, 5), (5, 6)], lambda k: m.x[:, k, :],
           evacuate)


def add_residual(m):
    def evacuate(dve, tile, out):
        x = blocks4(tile_of(m.x, tile))
        return m.nc.vector.scalar_tensor_tensor(out=x, in0=x, scalar=ALPHA, in1=out, op0=ALU.mult, op1=ALU.add)
    return evacuate


def project_out(m, name, w, mixed, grouped):
    rows = w.rearrange("(k p) c -> p k c", p=128)
    plain = 4 - grouped
    by_group = w[128 * grouped:128 * grouped + 512, :].rearrange("(g a d) c -> g d a c", g=2, a=4)

    def loads(i, u, slot):
        cols = ds(i * 512 + 128 * u, 128)
        return [(slot[0:64, grouped:grouped + 4], by_group[0][:, :, cols]),
                (slot[64:128, grouped:grouped + 4], by_group[1][:, :, cols]),
                (slot[:, plain:plain + 4], rows[:, plain:plain + 4, cols])]

    m.sum = m.p[:, 8, :]
    linear(m, name, 8, loads, 3, [(0, 1), (1, 2)], mixed, add_residual(m), on_vector=True,
           then=lambda tile: sum_tile(m, m.x[:, tile, :], tile))


def mlp(m, layer):
    nc = m.nc
    QUARTERS = FF // D
    up = weight_view(m.io["w_ff_up"][layer])
    down = m.io["w_ff_down"][layer].rearrange("(r p) c -> p r c", p=128)
    w = m.work
    m.acc, high, hidden, hidden_high = (m.arena[:, w + n * 8 * T:w + (n + 1) * 8 * T]
                                        .rearrange("p (k t) -> p k t", k=8) for n in range(4))
    assert w + 32 * T + RING <= m.limit
    ring = m.linears.begin(w + 32 * T, 2, 64, 0)
    relu, added, squared, hidden_rounded, hidden_split, scaled = m.mlp_sems
    had = layer * FF // 128
    scaled_before = layer * 8
    quarters = [(0, 1), (1, QUARTERS)]
    m.sum = high[:, 0, :]

    with nc.Block() as block:

        @block.sync
        def _(sp):
            def fill(q, first):
                for u in range(8):
                    ring.load(sp, q * 16, u, first,
                              lambda slot: halves(slot, up[:, :, ds(q * D + 128 * u, 128)]))
                for u in range(8):
                    ring.load(sp, q * 16, 8 + u, first,
                              lambda slot: halves(slot, down[:, ds(q * 8, 8), 128 * u:128 * u + 128]))

            repeat(sp, quarters, fill)

        @block.tensor
        def _(pe):
            def multiply(q, first):
                for u in range(8):
                    if u >= 2:
                        pe.wait_ge(relu, q * 8 + (had + u - 1))
                    elif not first:
                        pe.wait_ge(added, q * 8 + (had + u - 1))
                    ready = (lambda k: pe.wait_ge(ring.x_split, ring.operands + k + 1)) if first and u == 0 else None
                    ring.multiply(pe, q * 16, u, lambda k: high[:, k, :], lambda k: m.x[:, k, :], ready)
                for u in range(8):
                    if u >= 2:
                        pe.wait_ge(added, q * 8 + (had + u - 1))
                    else:
                        pe.wait_ge(relu, q * 8 + (had + 7 + u))
                    ready = (lambda k: pe.wait_ge(hidden_split, q * 8 + (had + k + 1))) if u == 0 else None
                    ring.multiply(pe, q * 16, 8 + u, lambda k: hidden_high[:, k, :], lambda k: hidden[:, k, :], ready)

            repeat(pe, quarters, multiply)

        @block.scalar
        def _(act):
            for k in range(8):
                nc.scalar.activation(rounded(m, high[:, k, :]), m.x[:, k, :], ACT.Copy).then_inc(ring.x_high, 1)

            def square(q, first):
                for u in range(8):
                    act.wait_ge(ring.used, q * 16 + (ring.pieces + u + 1))
                    nc.scalar.activation(blocks4(hidden[:, u, :]), linear_out(m, u % 2), ACT.Relu)\
                        .then_inc(relu, 1)
                    act.wait_ge(relu, q * 8 + (had + u + 1))
                    nc.scalar.activation(hidden[:, u, :], hidden[:, u, :], ACT.Square).then_inc(squared, 1)

            repeat(act, quarters, square)

        @block.vector
        def _(dve):
            def split_hidden(q, u):
                dve.wait_ge(squared, q * 8 + (had + u + 1))
                nc.vector.tensor_copy(rounded(m, hidden_high[:, u, :]), hidden[:, u, :]).then_inc(hidden_rounded, 1)
                dve.wait_ge(hidden_rounded, q * 8 + (had + u + 1))
                nc.vector.tensor_tensor(rounded(m, hidden[:, u, :]), hidden[:, u, :],
                                        rounded(m, hidden_high[:, u, :]),
                                        ALU.subtract).then_inc(hidden_split, 1)

            def add(q, u):
                dve.wait_ge(ring.used, q * 16 + (ring.pieces + 9 + u))
                acc = blocks4(m.acc[:, u, :])
                nc.vector.tensor_tensor(acc, acc, linear_out(m, u % 2), ALU.add).then_inc(added, 1)
                if isinstance(q, int) and q == QUARTERS - 1:
                    dve.wait_ge(added, q * 8 + (had + u + 1))
                    sum_tile(m, m.acc[:, u, :], u)

            def body(q, first):
                for u in range(16):
                    ring.split(dve, q * 16, q * 4, u, first)
                    if first and u == 0:
                        for k in range(8):
                            nc.vector.tensor_scalar(m.acc[:, k, :], m.x[:, k, :], ALPHA, None, ALU.mult)\
                                .then_inc(scaled, 1)
                            dve.wait_ge(ring.x_high, ring.operands + k + 1)
                            dve.wait_ge(scaled, scaled_before + k + 1)
                            nc.vector.tensor_tensor(rounded(m, m.x[:, k, :]), m.x[:, k, :], rounded(m, high[:, k, :]),
                                                    ALU.subtract).then_inc(ring.x_split, 1)
                    if 1 <= u <= 8:
                        split_hidden(q, u - 1)
                    elif u:
                        add(q, u - 9)
                    elif not first:
                        add(q - 1, 7)

            repeat(dve, [(0, 1), (1, QUARTERS - 1), (QUARTERS - 1, QUARTERS)], body)
            add(QUARTERS - 1, 7)


def layer_norm(m, name, gain, shift, source=None):
    nc = m.nc
    P = Steps(nc, f"{name}_pe", ["mean"] + [f"v{k}" for k in range(8)])
    V = Steps(nc, f"{name}_dve", [f"c{k}" for k in range(8)] + ["rstd"] + [f"n{k}" for k in range(8)])
    A = Steps(nc, f"{name}_act", [f"s{k}" for k in range(8)] + ["std"] + [f"g{k}" for k in range(8)])
    sq = m.arena[:, m.work:m.work + 2 * T].rearrange("p (s t) -> p s t", s=2)
    rstd = m.arena[:, m.work + 2 * T:m.work + 3 * T]
    source = m.x if source is None else source
    with nc.Block() as block:

        @block.tensor
        def _(pe):
            for b in range(4):
                last = nc.tensor.matmul(m.ps[:, b * 512:b * 512 + TB], m.c("mean"), m.sum[:, b * TB:(b + 1) * TB],
                                        start=True, stop=True)
            last.then_inc(*P.step("mean"))
            for k in range(8):
                pe.wait_ge(A.sem, A.done(0, f"s{k}"))
                for b in range(4):
                    at = 2048 + b * 512
                    last = nc.tensor.matmul(m.ps[:, at:at + TB], m.c("mean"), sq[:, k % 2, b * TB:(b + 1) * TB],
                                            start=(k == 0), stop=(k == 7), skip_group_check=True)
                last.then_inc(*P.step(f"v{k}"))

        @block.vector
        def _(dve):
            dve.wait_ge(P.sem, P.done(0, "mean"))
            for k in range(8):
                nc.vector.tensor_tensor(blocks4(m.x[:, k, :]), blocks4(source[:, k, :]), linear_out(m, 0),
                                        ALU.subtract).then_inc(*V.step(f"c{k}"))
            dve.wait_ge(A.sem, A.done(0, "std"))
            nc.vector.reciprocal(rstd, rstd).then_inc(*V.step("rstd"))
            dve.wait_ge(V.sem, V.done(0, "rstd"))
            for k in range(8):
                nc.vector.tensor_tensor(m.x[:, k, :], m.x[:, k, :], rstd, ALU.mult).then_inc(*V.step(f"n{k}"))

        @block.scalar
        def _(act):
            for k in range(8):
                act.wait_ge(V.sem, V.done(0, f"c{k}"))
                if k >= 2:
                    act.wait_ge(P.sem, P.done(0, f"v{k - 2}"))
                nc.scalar.activation(sq[:, k % 2], m.x[:, k, :], ACT.Square).then_inc(*A.step(f"s{k}"))
            act.wait_ge(P.sem, P.done(0, "v7"))
            nc.scalar.activation(blocks4(rstd), linear_out(m, 1), ACT.Sqrt,
                                 bias=m.eps(0)).then_inc(*A.step("std"))
            for k in range(8):
                act.wait_ge(V.sem, V.done(0, f"n{k}"))
                nc.scalar.activation(m.x[:, k, :], m.x[:, k, :], ACT.Identity, scale=m.col(gain + k),
                                     bias=m.col(shift + k)).then_inc(*A.step(f"g{k}"))


def start(m):
    nc, io = m.nc, m.io
    natural = m.arena[:, m.work:m.work + 9 * D].rearrange("p (t d) -> p t d", t=9)
    rows = m.arena[:, m.work + 9 * D:m.work + 9 * D + 128]
    consts = nc.alloc_semaphore("consts_loaded")
    params = nc.alloc_semaphore("params_loaded")
    prompt = nc.alloc_semaphore("prompt_loaded")
    sample = nc.alloc_semaphore("sample_loaded")
    sinks = m.sinks_loaded = nc.alloc_semaphore("sinks_loaded")
    cleared = nc.alloc_semaphore("rows_cleared")
    turned = nc.alloc_semaphore("turned")
    moved = nc.alloc_semaphore("turned_moved")
    by_rows = [("mu", io["mu_b"], 14), ("w0", io["w0_b"], 4), ("a0", io["a0_b"], 4), ("kk", io["k_k_b"], 4),
               ("ka", io["k_a_b"], 4), ("lnxg", io["lnx_g_b"], 4), ("lnxb", io["lnx_b_b"], 4),
               ("subln", io["subln_g_c"], 1)]
    with nc.Block() as block:

        @block.sync
        def _(sp):
            sp.dma_start(m.const, io["consts"][:, 0:m.nconst]).then_inc(consts, 16)
            sp.dma_start(natural[:, 0:8, :], io["x_prompt"][0].rearrange("(t p) d -> p t d", p=128))\
              .then_inc(prompt, 16)
            sp.dma_start(natural[0:TS, 8, :], io["x_sample"][0]).then_inc(sample, 16)

        @block.scalar
        def _(act):
            act.wait_ge(cleared, 1)
            n = 0
            for name, src, count in by_rows:
                act.dma_start(rows[ROWS[name]:ROWS[name] + count, :],
                              src[0].rearrange("(k p) -> k p", p=128)).then_inc(params, 16)
                n += 1
            act.dma_start(rows[ROWS["rk"]:ROWS["rk"] + 4, :],
                          io["r_k_b"][0].rearrange("(k h) d -> k (h d)", h=2)).then_inc(params, 16)
            act.dma_start(rows[ROWS["shift"]:ROWS["shift"] + 14, :],
                          io["state_b_shift"][0, 0, 0].rearrange("(k p) -> k p", p=128)).then_inc(params, 16)
            for name, src in (("mixg", "ln_mix_g"), ("mixb", "ln_mix_b"), ("ffng", "ln_ffn_g"), ("ffnb", "ln_ffn_b")):
                act.dma_start(rows[ROWS[name]:ROWS[name] + 16, :],
                              io[src].rearrange("l (k p) -> (l k) p", p=128)).then_inc(params, 16)
            act.dma_start(m.sink, io["sink_a"].partition_broadcast(128).rearrange("p a h -> p (a h)"))\
               .then_inc(sinks, 16)
            for v, name in enumerate(("lam_q1_c", "lam_k1_c", "lam_q2_c", "lam_k2_c")):
                act.dma_start(m.lam_in[:, v, :], io[name].partition_broadcast(128).rearrange("p a h -> p (a h)"))\
                   .then_inc(sinks, 16)
            act.wait_ge(sinks, 16 * 5)

        @block.vector
        def _(dve):
            nc.vector.memset(m.om, 0.0)
            nc.vector.memset(rows, 0.0).then_inc(cleared, 1)
            for t in range(9):
                n = 128 if t < 8 else TS
                dve.wait_ge(turned, t + 1)
                nc.vector.tensor_copy(m.x[:, :, t * 128:t * 128 + n],
                                      m.ps[:, (t % 2) * 1024:(t % 2) * 1024 + 1024]
                                      .rearrange("p (k t) -> p k t", k=8)[:, :, 0:n]).then_inc(moved, 1)
            dve.wait_ge(turned, 10)
            nc.vector.tensor_copy(m.cols, bank(m, 4)[:, 0:128]).then_inc(moved, 1)

        @block.tensor
        def _(pe):
            pe.wait_ge(consts, 16)
            pe.wait_ge(prompt, 16)
            for t in range(9):
                n = 128 if t < 8 else TS
                if t == 8:
                    pe.wait_ge(sample, 16)
                if t >= 2:
                    pe.wait_ge(moved, t - 1)
                for k in range(8):
                    at = (t % 2) * 1024 + k * 128
                    last = nc.tensor.transpose(m.ps[:, at:at + n], natural[0:n, t, k * 128:(k + 1) * 128],
                                               m.c("ident")[0:n, 0:n])
                last.then_inc(turned, 1)
            pe.wait_ge(params, 16 * 14)
            nc.tensor.transpose(bank(m, 4)[:, 0:128], rows, m.c("ident")).then_inc(turned, 1)


def window_attention(m):
    nc, io = m.nc, m.io
    w = m.work
    vn = m.arena[:, w:w + 1280].rearrange("p (t c) -> p t c", t=10)
    kcache = m.arena[:, w + 1280:w + 1408]
    kct = m.arena[:, w + 1408:w + 1536]
    out_rows = m.arena[:, w + 1536:w + 2048].rearrange("p (a c) -> p a c", a=4)
    w += 2048
    qz = m.arena[:, w:w + 1024].rearrange("p (h q) -> p h q", h=8)
    logits = m.arena[:, w + 1024:w + 3072].rearrange("p (h k) -> p h k", h=8)
    pt = m.arena[:, w + 3072:w + 5120].rearrange("p (h j q) -> p h j q", h=8, j=2)
    on = m.arena[:, w + 5120:w + 5632]
    st = m.arena[:, w + 5632:w + 5696]
    top, low, total, sink_e, inv = (st[:, 8 * n:8 * n + 8] for n in range(5))
    q, kT, vT = m.p[:, 0:4, :], m.p[:, 16, :], m.p[:, 17, :]

    cached = nc.alloc_semaphore("a_cache_loaded")
    stored = nc.alloc_semaphore("a_stored")
    pre = Steps(nc, "a_pre_pe", [f"v{t}" for t in range(9)] + ["kc", "k7", "k8"])
    prev = Steps(nc, "a_pre_dve", [f"v{t}" for t in range(9)] + ["kc", "k7", "k8"])
    with nc.Block() as block:

        @block.sync
        def _(sp):
            sp.dma_start(kcache, io["cache_a_k"][0, 0].rearrange("s g d -> s (g d)")).then_inc(cached, 16)
            sp.dma_start(vn[:, 9, :], io["cache_a_v"][0, 0].rearrange("s g d -> s (g d)")).then_inc(cached, 16)
            rows = lambda o: o[0, 0].rearrange("s g d -> s (g d)")
            sp.dma_start(rows(io["a_k_s"])[0:64], io["cache_a_k"][0, 0, 64:128].rearrange("s g d -> s (g d)"))\
              .then_inc(stored, 16)
            sp.dma_start(rows(io["a_v_s"])[0:64], io["cache_a_v"][0, 0, 64:128].rearrange("s g d -> s (g d)"))\
              .then_inc(stored, 16)
            sp.wait_ge(prev.sem, prev.done(0, "k8"))
            sp.dma_start(rows(io["a_v_p"]), vn[:, 7, :]).then_inc(stored, 16)
            sp.dma_start(rows(io["a_v_s"])[64:128], vn[0:64, 8, :]).then_inc(stored, 16)
            sp.dma_start(rows(io["a_k_p"]), out_rows[:, 0, :]).then_inc(stored, 16)
            sp.dma_start(rows(io["a_k_s"])[64:128], out_rows[0:64, 1, :]).then_inc(stored, 16)
            sp.wait_ge(stored, 16 * 6)

        @block.gpsimd
        def _(pool):
            nc.gpsimd.memset(qz, 0.0)
            join(m, pool, m.joined)

        @block.tensor
        def _(pe):
            def turn(bk, src, n, name):
                nc.tensor.transpose(bank(m, bk)[0:n, 0:128], src, m.c("ident")).then_inc(*pre.step(name))

            for t in range(9):
                n = 128 if t < 8 else TS
                if t >= 4:
                    pe.wait_ge(prev.sem, prev.done(0, f"v{t - 4}"))
                turn(t % 4, vT[:, t * 128:t * 128 + n], n, f"v{t}")
            pe.wait_ge(cached, 32)
            turn(4, kcache, 128, "kc")
            turn(5, kT[:, TP - 128:TP], 128, "k7")
            turn(6, kT[:, TP:T], TS, "k8")

        @block.vector
        def _(dve):
            for t in range(9):
                n = 128 if t < 8 else TS
                dve.wait_ge(pre.sem, pre.done(0, f"v{t}"))
                nc.vector.tensor_copy(vn[0:n, t, :], bank(m, t % 4)[0:n, 0:128]).then_inc(*prev.step(f"v{t}"))
            for name, bk, dst in (("kc", 4, kct), ("k7", 5, out_rows[:, 0, :]), ("k8", 6, out_rows[0:64, 1, :])):
                dve.wait_ge(pre.sem, pre.done(0, name))
                n = dst.shape[0]
                nc.vector.tensor_copy(dst, bank(m, bk)[0:n, 0:128]).then_inc(*prev.step(name))

    names = ("a_scores", "a_probs_turned", "a_out", "a_rows_turned", "a_q", "a_probs_moved", "a_rows_moved")
    PS, PT, PO, PU, AQ, AM, AU = (Steps(nc, n, [n]) for n in names)
    VP = Steps(nc, "a_logits", [f"logits{h}" for h in range(4)] + ["max", "top", "low"])
    VN = Steps(nc, "a_norm", ["sum", "inv", "norm"])
    AE = Steps(nc, "a_exps", [f"exp{h}" for h in range(4)] + ["sink"])
    kept = nc.alloc_semaphore("x_kept")

    def one(steps):
        return steps.step(steps.steps[0])

    def ended(engine, steps, unit):
        engine.wait_ge(steps.sem, steps.done(unit, steps.steps[0]))

    def kind(t):
        return "first" if isinstance(t, int) and t == 0 else "sample" if isinstance(t, int) and t == NQ else "middle"

    def keys(t):
        return {"first": (128, 256), "sample": (0, 192), "middle": (0, 256)}[kind(t)]

    def tiles(t):
        return (1,) if kind(t) == "first" else (0, 1)

    def rows_of(t, j):
        return TS if kind(t) == "sample" and j == 1 else 128

    with nc.Block() as block:

        @block.sync
        def _(sp):
            sp.dma_start(io["x_kept"], m.arena[:, m.x_at:m.x_at + 8 * T]).then_inc(kept, 16)
            sp.wait_ge(kept, 16)

        def rounds(engine, body):
            body(0, 1)
            with engine.Fori(1, NQ - 1) as t:
                body(t, t + 1)
            body(NQ - 1, NQ)
            body(NQ, None)

        def waits(t):
            return not (isinstance(t, int) and t == 0)

        @block.scalar
        def _(act):
            def take_wait(t, place):
                if not isinstance(t, int):
                    idle = m.om[:, 5 + place:6 + place]
                    nc.scalar.activation(idle, idle, ACT.Copy)

            def load(t, g):
                n = TS if kind(t) == "sample" else 128
                if waits(t):
                    ended(act, PS, t * 2 + (g - 2))
                take_wait(t, g)
                half = slice(64 * g, 64 * g + 64)
                nc.scalar.activation(qz[half, 4 * g:4 * g + 4, 0:n], q[half, :, ds(t * 128, n)], ACT.Copy,
                                     scale=SCALE).then_inc(*one(AQ))

            def exponentials(t, g):
                a, z = keys(t)
                act.wait_ge(VP.sem, VP.done(t * 2 + g, "low"))
                for h in range(4 * g, 4 * g + 4):
                    e = logits[:, h, a:z]
                    nc.scalar.activation(e, e, ACT.Exp, bias=low[:, h:h + 1], accum_out=total[:, h:h + 1])\
                        .then_inc(*AE.step(f"exp{h % 4}"))
                nc.scalar.activation(sink_e[:, 4 * g:4 * g + 4], top[:, 4 * g:4 * g + 4], ACT.Exp)\
                    .then_inc(*AE.step("sink"))

            def move(t, g):
                ended(act, PT, t * 2 + g)
                src = m.ps[:, 2048:3072].rearrange("p (h j q) -> p h j q", h=4, j=2)
                dst = pt[:, 4 * g:4 * g + 4]
                if kind(t) == "middle":
                    last = nc.scalar.activation(dst, src, ACT.Copy)
                else:
                    for j in tiles(t):
                        k = rows_of(t, j)
                        last = nc.scalar.activation(dst[0:k, :, j, :], src[0:k, :, j, :], ACT.Copy)
                last.then_inc(*one(AM))

            def move_rows(t):
                n = TS if kind(t) == "sample" else 128
                ended(act, PU, t)
                take_wait(t, 2)
                src = m.ps[:, 3072:4096].rearrange("p (b a q) -> p b a q", b=2, a=4)[:, :, 2:4, 0:n]
                dst = q.rearrange("p (b a) t -> p b a t", b=2)
                for b in range(2):
                    last = nc.scalar.activation(dst[:, b, :, ds(t * 128, n)], src[:, b], ACT.Copy)
                last.then_inc(*one(AU))

            def body(t, after):
                if after is not None:
                    load(after, 0)
                move(t, 0)
                if waits(t):
                    move_rows(t - 1)
                exponentials(t, 1)
                if after is not None:
                    load(after, 1)
                move(t, 1)
                if after is not None:
                    exponentials(after, 0)

            load(0, 0)
            load(0, 1)
            exponentials(0, 0)
            rounds(act, body)
            move_rows(NQ)

        @block.vector
        def _(dve):
            def prepare(t, g):
                a, z = keys(t)
                u, mine = t * 2 + g, slice(4 * g, 4 * g + 4)
                ended(dve, PS, u)
                for h in range(4 * g, 4 * g + 4):
                    at = h * 256
                    nc.vector.scalar_tensor_tensor(
                        out=logits[:, h, a:z], in0=m.c("distA")[:, a:z], scalar=-2.0 ** (-(h + 1)),
                        in1=m.ps[:, at + a:at + z], op0=ALU.mult, op1=ALU.add)\
                        .then_inc(*VP.step(f"logits{h % 4}"))
                dve.wait_ge(VP.sem, VP.done(u, "logits3"))
                nc.vector.tensor_reduce(top[:, mine], logits[:, mine, a:z], AX.X, ALU.max).then_inc(*VP.step("max"))
                dve.wait_ge(VP.sem, VP.done(u, "max"))
                nc.vector.tensor_tensor(low[:, mine], top[:, mine], m.sink[:, mine], ALU.max)\
                    .then_inc(*VP.step("top"))
                dve.wait_ge(VP.sem, VP.done(u, "top"))
                nc.vector.tensor_tensor(top[:, mine], m.sink[:, mine], low[:, mine], ALU.subtract)
                nc.vector.tensor_scalar(low[:, mine], low[:, mine], -1.0, None, ALU.mult).then_inc(*VP.step("low"))

            def normalise(t, g):
                u, mine = t * 2 + g, slice(4 * g, 4 * g + 4)
                dve.wait_ge(AE.sem, AE.done(u, "sink"))
                nc.vector.tensor_tensor(inv[:, mine], total[:, mine], sink_e[:, mine], ALU.add)\
                    .then_inc(*VN.step("sum"))
                dve.wait_ge(VN.sem, VN.done(u, "sum"))
                nc.vector.reciprocal(inv[:, mine], inv[:, mine]).then_inc(*VN.step("inv"))
                dve.wait_ge(VN.sem, VN.done(u, "inv"))
                ended(dve, PO, u)
                nc.vector.tensor_tensor(
                    on.rearrange("p (a g d) -> p g a d", a=4, g=2)[:, g],
                    bank(m, 6 + g)[:, 0:256].rearrange("p (a d) -> p a d", a=4),
                    inv[:, mine].unsqueeze(2).to_broadcast([128, 4, 64]), ALU.mult).then_inc(*VN.step("norm"))

            def body(t, after):
                prepare(t, 1)
                normalise(t, 0)
                if after is not None:
                    prepare(after, 0)
                normalise(t, 1)

            prepare(0, 0)
            rounds(dve, body)

        @block.tensor
        def _(pe):
            def scores(t, g):
                ended(pe, AQ, t * 2 + g)
                for h in range(4 * g, 4 * g + 4):
                    at = h * 256
                    if kind(t) == "sample":
                        nc.tensor.matmul(m.ps[:, at:at + 128], qz[:, h, :], kct, start=True, stop=True)
                        last = nc.tensor.matmul(m.ps[:, at + 128:at + 192], qz[:, h, :], kT[:, TP:T],
                                                start=True, stop=True)
                    elif kind(t) == "first":
                        last = nc.tensor.matmul(m.ps[:, at + 128:at + 256], qz[:, h, :], kT[:, 0:128],
                                                start=True, stop=True)
                    else:
                        last = nc.tensor.matmul(m.ps[:, at:at + 256], qz[:, h, :], kT[:, ds(t * 128 - 128, 256)],
                                                start=True, stop=True)
                last.then_inc(*one(PS))

            def turn_probs(t, g):
                if g or waits(t):
                    ended(pe, AM, t * 2 + (g - 1))
                pe.wait_ge(AE.sem, AE.done(t * 2 + g, "exp3"))
                for h in range(4):
                    for j in tiles(t):
                        k = rows_of(t, j)
                        at = 2048 + h * 256 + j * 128
                        last = nc.tensor.transpose(m.ps[0:k, at:at + 128], logits[:, 4 * g + h, j * 128:j * 128 + k],
                                                   m.c("ident"))
                last.then_inc(*one(PT))

            def values(t, g):
                ended(pe, AM, t * 2 + g)
                if waits(t):
                    pe.wait_ge(VN.sem, VN.done(t * 2 + (g - 2), "norm"))
                    if g == 0:
                        ended(pe, AU, t - 1)
                for h in range(4):
                    for j in tiles(t):
                        k = rows_of(t, j)
                        if kind(t) != "middle":
                            v = vn[0:k, (9, 8)[j] if kind(t) == "sample" else 0, 64 * g:64 * g + 64]
                        else:
                            v = vn[:, ds(t + (j - 1), 1), 64 * g:64 * g + 64].rearrange("p a d -> p (a d)")
                        last = nc.tensor.matmul(bank(m, 6 + g)[:, h * 64:h * 64 + 64], pt[0:k, 4 * g + h, j, :], v,
                                                start=(j == tiles(t)[0]), stop=(j == 1))
                last.then_inc(*one(PO))

            def turn_rows(t):
                pe.wait_ge(VN.sem, VN.done(t * 2 + 1, "norm"))
                for a in range(4):
                    at = 256 + (a % 2) * 128
                    last = nc.tensor.transpose(bank(m, 6 + a // 2)[:, at:at + 128], on[:, a * 128:a * 128 + 128],
                                               m.c("ident"))
                last.then_inc(*one(PU))

            def body(t, after):
                turn_probs(t, 0)
                if waits(t):
                    turn_rows(t - 1)
                if after is not None:
                    scores(after, 0)
                values(t, 0)
                turn_probs(t, 1)
                if after is not None:
                    scores(after, 1)
                values(t, 1)

            scores(0, 0)
            scores(0, 1)
            rounds(pe, body)
            turn_rows(NQ)


def rwkv_prepare(m):
    nc, io = m.nc, m.io
    w = m.work
    m.kk = m.arena[:, w:w + 4 * T].rearrange("p (h t) -> p h t", h=4)
    m.a = m.arena[:, w + 4 * T:w + 8 * T].rearrange("p (h t) -> p h t", h=4)
    m.pc = m.arena[:, w + 8 * T:w + 8 * T + 68].rearrange("p (h c) -> p h c", h=4)
    m.g_up = m.arena[:, w + 8 * T + 68:w + 8 * T + 580]
    w += 8 * T + 580
    m.chunk_at = w
    diff = m.arena[:, w:w + 2 * T].rearrange("p (s t) -> p s t", s=2)
    edge = m.arena[:, w + 2 * T:w + 2 * T + 28].rearrange("p (k e) -> p k e", e=2)
    lastc = m.arena[:, w + 2 * T + 28:w + 2 * T + 56]
    lastr = m.arena[:, w + 2 * T + 64:w + 2 * T + 192]
    wa_up = m.arena[:, w + 2 * T + 192:w + 2 * T + 704]
    w += 2 * T + 704
    sg, cum, before, tmp = (m.arena[:, w + n * T:w + n * T + T] for n in range(4))
    assert w + 4 * T <= m.limit, w + 4 * T
    p = m.p
    r, k, v = p[:, 4:8, :], p[:, 8:12, :], p[:, 12:16, :]
    spots = [(0, 12, 4), (12, 14, 18)]

    loaded = nc.alloc_semaphore("b_weights_loaded")
    stored = nc.alloc_semaphore("b_shift_stored")
    S = Steps(nc, "b_shift_dve", ["edge"] + [f"t{j}" for j in range(3 * 14)] + ["last"])
    S2 = nc.alloc_semaphore("b_shift_turned")
    with nc.Block() as block:

        @block.sync
        def _(sp):
            sp.dma_start(wa_up[0:64], io["w_up_b"][0]).then_inc(loaded, 16)
            sp.dma_start(wa_up[64:128], io["a_up_b"][0]).then_inc(loaded, 16)
            sp.dma_start(m.g_up, io["g_up_b"][0]).then_inc(loaded, 16)
            sp.wait_ge(S.sem, S.done(0, "last"))
            for n, out in enumerate(("b_shift_p", "b_shift_s")):
                sp.dma_start(io[out][0, 0, 0].rearrange("(k p) -> k p", p=128), lastr[14 * n:14 * n + 14, :])\
                    .then_inc(stored, 16)
            sp.wait_ge(stored, 32)

        @block.vector
        def _(dve):
            for a, b, at in spots:
                nc.vector.tensor_copy(lastc[:, a:b], p[:, at:at + b - a, TP - 1])
                nc.vector.tensor_copy(lastc[:, 14 + a:14 + b], p[:, at:at + b - a, T - 1])
            for a, b, at in spots:
                nc.vector.tensor_scalar(edge[:, a:b, 0], p[:, at:at + b - a, 0], -1.0, None, ALU.mult)
                last = nc.vector.tensor_tensor(edge[:, a:b, 1], m.cols[:, ROWS["shift"] + a:ROWS["shift"] + b],
                                               p[:, at:at + b - a, TP], ALU.subtract)
            last.then_inc(*S.step("edge"))
            dve.wait_ge(S.sem, S.done(0, "edge"))
            for j in range(14):
                x = p[:, 4 + j if j < 12 else 6 + j, :]
                d = diff[:, j % 2]
                nc.vector.tensor_tensor(d[:, 1:T], x[:, 0:T - 1], x[:, 1:T], ALU.subtract)\
                    .then_inc(*S.step(f"t{3 * j}"))
                dve.wait_ge(S.sem, S.done(0, f"t{3 * j}"))
                nc.vector.tensor_copy(d[:, 0:T:TP], edge[:, j, :]).then_inc(*S.step(f"t{3 * j + 1}"))
                dve.wait_ge(S.sem, S.done(0, f"t{3 * j + 1}"))
                nc.vector.scalar_tensor_tensor(out=x, in0=d, scalar=m.col(ROWS["mu"] + j), in1=x,
                                               op0=ALU.mult, op1=ALU.add).then_inc(*S.step(f"t{3 * j + 2}"))
            dve.wait_ge(S2, 1)
            nc.vector.tensor_copy(lastr[0:28, :], bank(m, 0)[0:28, 0:128]).then_inc(*S.step("last"))

        @block.tensor
        def _(pe):
            pe.wait_ge(S.sem, S.done(0, "edge"))
            nc.tensor.transpose(bank(m, 0)[0:28, 0:128], lastc, m.c("ident")).then_inc(S2, 1)

    bonus = [16, 17, 20, 18]
    m.bonus = bonus
    m.y = r
    P = Steps(nc, "b_pe", ["w", "a", "norm", "bonus"])
    V = Steps(nc, "b_dve", ["kk", "kk2", "cum", "before", "ak", "k", "rk", "rkk", "rnorm", "kkn", "bon", "b",
                            "A", "K", "B", "pc"])
    A = Steps(nc, "b_act", ["sg", "a", "norm", "e1", "e2", "e3"])
    om = m.om
    pre = nc.alloc_semaphore("b_one_minus_ka")
    gates = nc.alloc_semaphore("b_gates")
    e1, e2, e3 = diff[:, 0], diff[:, 1], sg

    with nc.Block() as block:

        @block.tensor
        def _(pe):
            pe.wait_ge(loaded, 48)
            for h in range(4):
                cols = slice(128 * h, 128 * h + 128)

                def product(base, lhsT, src, name):
                    for b in range(4):
                        at = base + 512 * b
                        last = nc.tensor.matmul(m.ps[:, at:at + TB], lhsT, src[:, b * TB:(b + 1) * TB],
                                                start=True, stop=True)
                    last.then_inc(*P.step(name))

                if h:
                    pe.wait_ge(A.sem, A.done(h - 1, "norm"))
                pe.wait_ge(gates, 1)
                product(0, wa_up[0:64, cols], p[0:64, 18, :], "w")
                if h:
                    pe.wait_ge(V.sem, V.done(h - 1, "bon"))
                product(2048, wa_up[64:128, cols], p[64:128, 18, :], "a")
                pe.wait_ge(A.sem, A.done(h, "a"))
                pe.wait_ge(V.sem, V.done(h, "kk2"))
                product(0, m.c("heads"), tmp, "norm")
                pe.wait_ge(V.sem, V.done(h, "rkk"))
                product(2048, m.c("heads"), before, "bonus")

        @block.scalar
        def _(act):
            for h in range(4):
                if h == 0:
                    nc.scalar.activation(p[0:64, 18, :], p[0:64, 18, :], ACT.Tanh).then_inc(gates, 1)
                    nc.scalar.activation(p[:, 19, :], p[:, 19, :], ACT.Sigmoid).then_inc(gates, 1)
                act.wait_ge(P.sem, P.done(h, "w"))
                if h:
                    act.wait_ge(V.sem, V.done(h - 1, "B"))
                nc.scalar.activation(blocks4(sg), linear_out(m, 0), ACT.Sigmoid, bias=m.col(ROWS["w0"] + h))\
                    .then_inc(*A.step("sg"))
                act.wait_ge(P.sem, P.done(h, "a"))
                nc.scalar.activation(blocks4(m.a[:, h]), linear_out(m, 1), ACT.Sigmoid,
                                     bias=m.col(ROWS["a0"] + h)).then_inc(*A.step("a"))
                act.wait_ge(P.sem, P.done(h, "norm"))
                nc.scalar.activation(blocks4(tmp), linear_out(m, 0), ACT.Sqrt, bias=m.eps(1))\
                    .then_inc(*A.step("norm"))
                act.wait_ge(V.sem, V.done(h, "k"))
                nc.scalar.activation(e1, cum, ACT.Exp, scale=-DECAY).then_inc(*A.step("e1"))
                nc.scalar.activation(e2, e2, ACT.Exp, scale=-DECAY).then_inc(*A.step("e2"))
                nc.scalar.activation(e3, cum, ACT.Exp, scale=DECAY).then_inc(*A.step("e3"))

        @block.vector
        def _(dve):
            dve.wait_ge(S.sem, S.done(0, "last"))
            nc.vector.tensor_scalar(om[:, 0:4], m.cols[:, ROWS["ka"]:ROWS["ka"] + 4], -1.0, 1.0,
                                    ALU.mult, ALU.add).then_inc(pre, 1)
            dve.wait_ge(pre, 1)
            tt, stt = nc.vector.tensor_tensor, nc.vector.scalar_tensor_tensor

            for h in range(4):
                kk, a = m.kk[:, h], m.a[:, h]

                def after(name, t=h):
                    dve.wait_ge(V.sem, V.done(t, name))

                nc.vector.tensor_scalar(kk, k[:, h], m.col(ROWS["kk"] + h), None, ALU.mult).then_inc(*V.step("kk"))
                after("kk")
                tt(tmp, kk, kk, ALU.mult).then_inc(*V.step("kk2"))
                dve.wait_ge(A.sem, A.done(h, "a"))
                nc.vector.tensor_tensor_scan(cum, m.c("reset"), sg, 0.0, ALU.mult, ALU.add)\
                    .then_inc(*V.step("cum"))
                after("cum")
                tt(e2, cum, sg, ALU.subtract).then_inc(*V.step("before"))
                nc.vector.tensor_scalar(e1, a, m.col(ROWS["ka"] + h), om[:, h:h + 1], ALU.mult, ALU.add)\
                    .then_inc(*V.step("ak"))
                after("ak")
                tt(k[:, h], k[:, h], e1, ALU.mult).then_inc(*V.step("k"))
                nc.vector.tensor_scalar(before, r[:, h], m.col(ROWS["rk"] + h), None, ALU.mult)\
                    .then_inc(*V.step("rk"))
                after("rk")
                tt(before, before, k[:, h], ALU.mult).then_inc(*V.step("rkk"))
                dve.wait_ge(A.sem, A.done(h, "norm"))
                nc.vector.reciprocal(tmp, tmp).then_inc(*V.step("rnorm"))
                after("rnorm")
                stt(out=kk, in0=kk, scalar=-1.0, in1=tmp, op0=ALU.mult, op1=ALU.mult).then_inc(*V.step("kkn"))
                dve.wait_ge(P.sem, P.done(h, "bonus"))
                tt(blocks4(p[:, bonus[h], :]), linear_out(m, 1), blocks4(v[:, h]), ALU.mult)\
                    .then_inc(*V.step("bon"))
                after("kkn")
                stt(out=a, in0=a, scalar=-1.0, in1=kk, op0=ALU.mult, op1=ALU.mult).then_inc(*V.step("b"))
                dve.wait_ge(A.sem, A.done(h, "e3"))
                after("b")
                tt(r[:, h], r[:, h], e1, ALU.mult)
                tt(kk, kk, e2, ALU.mult).then_inc(*V.step("A"))
                tt(k[:, h], k[:, h], e3, ALU.mult).then_inc(*V.step("K"))
                tt(a, a, e3, ALU.mult).then_inc(*V.step("B"))
                nc.vector.tensor_copy(m.pc[:, h, :], e1[:, CH - 1:T:CH]).then_inc(*V.step("pc"))
                after("pc")


def rwkv_chunks(m):
    nc, io = m.nc, m.io
    room = {"spare": (m.chunk_at, m.limit), "x": (m.x_at, m.x_at + 8 * T)}
    handed = ("R", "A", "XT1", "LkT", "MbT", "MkT", "Vn", "Bn", "Kn")
    names = [f"{n}{i}" for n in handed for i in range(2)]
    names += ["B", "K", "V", "X0", "X1", "Xt0", "Xt1", "LT", "T1", "U", "SA", "Sn", "state_in", "state_out"]
    at = {n: lo for n, (lo, _) in room.items()}
    slot = {"S": m.state}
    for name in names:
        where = "x" if at["x"] + 512 <= room["x"][1] else "spare"
        slot[name] = m.arena[:, at[where]:at[where] + 512]
        at[where] += 512
        assert at[where] <= room[where][1]
    S = slot["S"]
    block4 = {n: heads4(a) for n, a in slot.items()}
    p = m.p
    src = {"R": p[:, 4:8, :], "A": m.kk, "B": m.a, "K": p[:, 8:12, :], "V": p[:, 12:16, :]}
    LEVELS = (2, 4, 8, 16, 32)
    pairs = (("L", "A", "B"), ("LT", "B", "A"), ("LkT", "K", "A"), ("MbT", "B", "R"), ("MkT", "K", "R"))
    free_steps = ["L", "LT", "LkT", "MbT", "MkT", "T2", "Vn", "X2", "XT2", "T4", "Bn", "X4", "XT4", "T8", "Kn",
                  "X8", "XT8", "T16", "X16", "XT16", "T32", "XT32"]
    banks = {n: i % 6 for i, n in enumerate(free_steps)}
    banks.update(U=6, SA=7, S=6, Y=7)
    by_scalar = ("Vn", "Bn", "Kn")
    FP, SP = Steps(nc, "w_free_pe", free_steps), Steps(nc, "w_state_pe", ["U", "SA", "S", "Y"])
    FV = Steps(nc, "w_free_dve", ["L", "X1", "LT", "XT1m", "XT1", "LkT", "MbT", "T2", "MkT",
                                  "X2", "XT2"]
               + sum([[f"T{n}"] + ([f"X{n}"] if n < 32 else []) + [f"XT{n}"] for n in LEVELS[1:]], []))
    SV = Steps(nc, "w_state_dve", ["Sadd", "S"])
    FA = Steps(nc, "w_free_act", ["Vn", "Bn", "Kn"])
    CV, CA = Steps(nc, "w_copies_dve", ["R", "A"]), Steps(nc, "w_copies_act", ["B", "K", "V"])
    SA = Steps(nc, "w_state_act", ["U", "SA", "Y"])
    st_load = nc.alloc_semaphore("w_state_loaded")
    st_turn = nc.alloc_semaphore("w_state_turned")
    st_move = nc.alloc_semaphore("w_state_moved")
    cleared = nc.alloc_semaphore("w_cleared")
    stored = nc.alloc_semaphore("w_stored")
    state_in, state_out = slot["state_in"], slot["state_out"]

    def mask(name):
        return m.c(name).unsqueeze(1).to_broadcast([128, 4, 128])

    def halves_copy(op, out, name, t):
        cols = ds(t * CH, CH)
        op(out[0:64, :, 0:64], src[name][0:64, :, cols])
        return op(out[64:128, :, 64:128], src[name][64:128, :, cols])

    def psum(name):
        return heads4(bank(m, banks[name]))


    def copies_vector(dve, t, odd, first):
        if not first:
            dve.wait_ge(SP.sem, SP.done(t - 2, "Y"))
        halves_copy(nc.vector.tensor_copy, block4[f"R{odd}"], "R", t).then_inc(*CV.step("R"))
        halves_copy(nc.vector.tensor_copy, block4[f"A{odd}"], "A", t).then_inc(*CV.step("A"))

    def copies_scalar(act, t):
        def copy(out, in_):
            return nc.scalar.activation(out, in_, ACT.Copy)

        for name in ("B", "K", "V"):
            halves_copy(copy, block4[name], name, t).then_inc(*CA.step(name))

    def chunk_vector(dve, t, odd, free, state, following):
        tt = nc.vector.tensor_tensor
        mine = {n: block4[f"{n}{odd}"] for n in handed}

        def after(name):
            dve.wait_ge(FV.sem, FV.done(t, name))

        def product(name):
            dve.wait_ge(FP.sem, FP.done(t, name))
            return psum(name)

        def masked(name, out, by):
            tt(out, product(name), mask(by), ALU.mult).then_inc(*FV.step(name))

        def state_sum():
            if state:
                dve.wait_ge(SP.sem, SP.done(t - 1, "S"))
                tt(block4["Sn"], psum("S"), block4["S"], ALU.add).then_inc(*SV.step("Sadd"))

        def state_decay():
            if state:
                dve.wait_ge(SP.sem, SP.done(t - 1, "Y"))
                dve.wait_ge(SV.sem, SV.done(t - 1, "Sadd"))
                tt(block4["S"], block4["Sn"], m.pc[:, :, ds(t - 1, 1)].to_broadcast([128, 4, 128]), ALU.mult)\
                    .then_inc(*SV.step("S"))

        if not free:
            state_sum()
            state_decay()
            return
        masked("L", block4["T1"], "low1")
        after("L")
        tt(block4["X0"], block4["T1"], mask("ident"), ALU.add).then_inc(*FV.step("X1"))
        masked("LT", block4["LT"], "strict")
        after("LT")
        tt(block4["T1"], block4["LT"], mask("up1"), ALU.mult).then_inc(*FV.step("XT1m"))
        after("XT1m")
        tt(block4["Xt0"], block4["T1"], mask("ident"), ALU.add).then_inc(*FV.step("XT1"))
        masked("LkT", mine["LkT"], "strict")
        masked("MbT", mine["MbT"], "upto")
        masked("T2", block4["T1"], "low2")
        masked("MkT", mine["MkT"], "upto")
        for i, n in enumerate(LEVELS):
            old, new = i % 2, 1 - i % 2
            if i:
                masked(f"T{n}", block4["T1"], f"low{n}")
            if n == 16:
                state_sum()
            if n < 32:
                tt(block4[f"X{new}"], product(f"X{n}"), block4[f"X{old}"], ALU.add).then_inc(*FV.step(f"X{n}"))
            out = mine["XT1"] if n == 32 else block4[f"Xt{new}"]
            tt(out, product(f"XT{n}"), block4[f"Xt{old}"], ALU.add).then_inc(*FV.step(f"XT{n}"))
            if n == 16:
                state_decay()
                if following:
                    copies_vector(dve, t + 1, 1 - odd, not state)

    def chunk_scalar(act, t, odd, free, state, following):
        def copy(out, in_):
            return nc.scalar.activation(out, in_, ACT.Copy)

        def turned(name):
            if free:
                act.wait_ge(FP.sem, FP.done(t, name))
                copy(slot[f"{name}{odd}"], bank(m, banks[name])).then_inc(*FA.step(name))

        def through(name):
            if state:
                act.wait_ge(SP.sem, SP.done(t - 1, name))
                copy(slot[name], bank(m, banks[name])).then_inc(*SA.step(name))

        turned("Vn")
        through("U")
        turned("Bn")
        through("SA")
        turned("Kn")
        if following:
            copies_scalar(act, t + 1)
        if state:
            act.wait_ge(SP.sem, SP.done(t - 1, "Y"))
            y = psum("Y")
            cols = ds((t - 1) * CH, CH)
            copy(m.y[0:64, :, cols], y[0:64, :, 0:64])
            copy(m.y[64:128, :, cols], y[64:128, :, 64:128]).then_inc(*SA.step("Y"))

    def chunk_tensor(pe, t, odd, free, state, following):
        def product(steps, name, *terms):
            for h in range(4):
                out = bank(m, banks[name])[:, h * 128:h * 128 + 128]
                for i, (lhsT, rhs) in enumerate(terms):
                    last = nc.tensor.matmul(out, block4[lhsT][:, h, :], block4[rhs][:, h, :], start=(i == 0),
                                            stop=(i == len(terms) - 1))
            last.then_inc(*steps.step(name))

        def turn(name, src_name):
            room_of(name)
            for h in range(4):
                last = nc.tensor.transpose(bank(m, banks[name])[:, h * 128:h * 128 + 128], block4[src_name][:, h, :],
                                           m.c("ident"))
            last.then_inc(*FP.step(name))

        def room_of(name):
            i = free_steps.index(name) - 6
            if i < 0:
                return
            if free_steps[i] in by_scalar:
                pe.wait_ge(FA.sem, FA.done(t, free_steps[i]))
            else:
                pe.wait_ge(FV.sem, FV.done(t, free_steps[i]))

        other = 1 - odd

        def through(name):
            if not state:
                return
            if name == "U":
                pe.wait_ge(FV.sem, FV.done(t - 1, "XT32"))
                if not (isinstance(t, int) and t == 1):
                    pe.wait_ge(SV.sem, SV.done(t - 2, "S"))
                    pe.wait_ge(SA.sem, SA.done(t - 2, "Y"))
                product(SP, "U", (f"A{other}", "S"), (f"LkT{other}", f"Vn{other}"))
            elif name == "SA":
                pe.wait_ge(SA.sem, SA.done(t - 1, "U"))
                product(SP, "SA", (f"XT1{other}", "U"))
            elif name == "S":
                pe.wait_ge(SA.sem, SA.done(t - 1, "SA"))
                product(SP, "S", (f"Bn{other}", "SA"), (f"Kn{other}", f"Vn{other}"))
            else:
                product(SP, "Y", ("S", f"R{other}"), ("SA", f"MbT{other}"), (f"Vn{other}", f"MkT{other}"))

        if not free:
            for name in ("U", "SA", "S", "Y"):
                through(name)
            return
        pe.wait_ge(CV.sem, CV.done(t, "A"))
        pe.wait_ge(CA.sem, CA.done(t, "V"))
        for name, lhsT, rhs in pairs:
            if name == "MbT" and state:
                pe.wait_ge(FV.sem, FV.done(t - 1, "XT32"))
            left, right = (n if n in "BK" else f"{n}{odd}" for n in (lhsT, rhs))
            product(FP, name, (left, right))
        between = {2: ("Vn", "V", "U"), 4: ("Bn", "B", "SA"), 8: ("Kn", "K", "S"), 16: (None, None, None),
                   32: (None, None, None)}
        for i, n in enumerate(LEVELS):
            old = i % 2
            if i == 0:
                pe.wait_ge(FV.sem, FV.done(t, "XT1"))
            else:
                pe.wait_ge(FV.sem, FV.done(t, f"XT{LEVELS[i - 1]}"))
            room_of(f"T{n}")
            product(FP, f"T{n}", ("LT", f"X{old}"))
            turned, source, passed = between[n]
            if turned:
                turn(turned, source)
            if n == 16:
                through("Y")
            pe.wait_ge(FV.sem, FV.done(t, f"T{n}"))
            if n < 32:
                room_of(f"X{n}")
                product(FP, f"X{n}", (f"Xt{old}", "T1"))
            room_of(f"XT{n}")
            product(FP, f"XT{n}", ("T1", f"Xt{old}"))
            if passed:
                through(passed)

    def over_chunks(engine, body, before, between):
        before(engine)
        body(engine, 0, 0, True, False, True)
        with engine.Fori(0, NCHUNK // 2 - 1) as i:
            body(engine, i * 2 + 1, 1, True, True, True)
            body(engine, i * 2 + 2, 0, True, True, True)
        body(engine, NCHUNK - 1, 1, True, True, True)
        body(engine, NCHUNK, 0, True, True, False)
        between(engine)
        body(engine, NCHUNK + 1, 1, False, True, False)

    heads_out = io["b_wkv_p"][0, 0], io["b_wkv_s"][0, 0]

    with nc.Block() as block:

        @block.gpsimd
        def _(pool):
            for n in ("R0", "A0", "B", "K", "V", "S", "R1", "A1", "state_in"):
                nc.gpsimd.memset(slot[n], 0.0).then_inc(cleared, 1)

        @block.vector
        def _(dve):
            def before(engine):
                dve.wait_ge(cleared, 8)
                copies_vector(dve, 0, 0, True)

            def save(n):
                dve.wait_ge(st_turn, 2 * n + 1)
                nc.vector.tensor_copy(state_out, bank(m, 0)).then_inc(st_move, 1)

            def between(engine):
                save(0)
                dve.wait_ge(st_turn, 2)
                nc.vector.tensor_copy(S, bank(m, 1)).then_inc(st_move, 1)

            over_chunks(dve, chunk_vector, before, between)
            dve.wait_ge(stored, 32 * 4)
            save(1)

        @block.scalar
        def _(act):
            def before(engine):
                act.wait_ge(cleared, 5)
                copies_scalar(act, 0)

            over_chunks(act, chunk_scalar, before, lambda engine: None)

        @block.tensor
        def _(pe):
            def save(t):
                pe.wait_ge(SV.sem, SV.done(t, "S"))
                for h in range(4):
                    last = nc.tensor.transpose(bank(m, 0)[:, h * 128:h * 128 + 128], block4["S"][:, h, :],
                                               m.c("ident"))
                last.then_inc(st_turn, 1)

            def between(engine):
                pe.wait_ge(FV.sem, FV.done(NCHUNK, "XT32"))
                save(NCHUNK - 1)
                pe.wait_ge(st_load, 32 * 4)
                for h in range(4):
                    last = nc.tensor.transpose(bank(m, 1)[:, h * 128:h * 128 + 128],
                                               heads4(state_in)[:, h, :], m.c("ident"))
                last.then_inc(st_turn, 1)
                pe.wait_ge(st_move, 2)

            over_chunks(pe, chunk_tensor, lambda engine: None, between)
            save(NCHUNK)

        @block.sync
        def _(sp):
            sp.wait_ge(cleared, 9)
            for h in range(8):
                o = 64 * (h % 2)
                sp.dma_start(heads4(state_in)[o:o + 64, h // 2, o:o + 64], io["state_b_wkv"][0, 0, h])\
                  .then_inc(st_load, 16)
            for n in range(2):
                sp.wait_ge(st_move, 2 * n + 1)
                for h in range(8):
                    o = 64 * (h % 2)
                    sp.dma_start(heads_out[n][h], heads4(state_out)[o:o + 64, h // 2, o:o + 64])\
                      .then_inc(stored, 16)
            sp.wait_ge(stored, 32 * 8)


def rwkv_finish(m):
    nc = m.nc
    w = m.chunk_at
    sq, std = (m.arena[:, w + n * 2 * T:w + (n + 1) * 2 * T].rearrange("p (s t) -> p s t", s=2) for n in range(2))
    PM, PG, PV = (Steps(nc, f"e_{n}_made", [n]) for n in ("mean", "gate", "var"))
    VC, VN, VB = Steps(nc, "e_centred", ["centred"]), Steps(nc, "e_normal", ["rstd", "normal"]), \
        Steps(nc, "e_gated", ["bonus", "gated"])
    AS, AD, AF = (Steps(nc, f"e_act_{n}", [n]) for n in ("square", "std", "affine"))
    y = m.y
    back = nc.alloc_semaphore("x_back")
    with nc.Block() as block:

        @block.sync
        def _(sp):
            sp.dma_start(m.arena[:, m.x_at:m.x_at + 8 * T], m.io["x_kept"]).then_inc(back, 16)
            sp.wait_ge(back, 16)

        def sums(half, lhsT, src, steps):
            for b in range(4):
                at = 2048 * half + 512 * b
                last = nc.tensor.matmul(m.ps[:, at:at + TB], lhsT, src[:, b * TB:(b + 1) * TB], start=True, stop=True)
            last.then_inc(*steps.step(steps.steps[0]))

        @block.tensor
        def _(pe):
            for h in range(4):
                if h >= 2:
                    pe.wait_ge(VC.sem, VC.done(h - 2, "centred"))
                sums(h % 2, m.c("heads"), y[:, h], PM)
            pe.wait_ge(VC.sem, VC.done(3, "centred"))
            for h in range(4):
                pe.wait_ge(AS.sem, AS.done(h, "square"))
                if h:
                    pe.wait_ge(AD.sem, AD.done(h - 1, "std"))
                sums(0, m.c("heads"), sq[:, h % 2], PV)
                if h:
                    pe.wait_ge(VB.sem, VB.done(h - 1, "gated"))
                sums(1, m.g_up[:, h * 128:h * 128 + 128], m.p[:, 19, :], PG)

        @block.vector
        def _(dve):
            for h in range(4):
                dve.wait_ge(PM.sem, PM.done(h, "mean"))
                nc.vector.scalar_tensor_tensor(out=blocks4(y[:, h]), in0=linear_out(m, h % 2), scalar=-1.0 / HD,
                                               in1=blocks4(y[:, h]), op0=ALU.mult, op1=ALU.add)\
                    .then_inc(*VC.step("centred"))

            def normalise(h):
                dve.wait_ge(AD.sem, AD.done(h, "std"))
                nc.vector.reciprocal(std[:, h % 2], std[:, h % 2]).then_inc(*VN.step("rstd"))
                dve.wait_ge(VN.sem, VN.done(h, "rstd"))
                nc.vector.tensor_tensor(y[:, h], y[:, h], std[:, h % 2], ALU.mult).then_inc(*VN.step("normal"))

            def gate(h):
                dve.wait_ge(AF.sem, AF.done(h, "affine"))
                nc.vector.tensor_tensor(y[:, h], y[:, h], m.p[:, m.bonus[h], :], ALU.add).then_inc(*VB.step("bonus"))
                dve.wait_ge(PG.sem, PG.done(h, "gate"))
                dve.wait_ge(VB.sem, VB.done(h, "bonus"))
                nc.vector.tensor_tensor(blocks4(y[:, h]), blocks4(y[:, h]), linear_out(m, 1), ALU.mult)\
                    .then_inc(*VB.step("gated"))

            normalise(0)
            for h in range(1, 4):
                normalise(h)
                gate(h - 1)
            gate(3)

        @block.scalar
        def _(act):
            def square(h):
                act.wait_ge(VC.sem, VC.done(h, "centred"))
                if h >= 2:
                    act.wait_ge(PV.sem, PV.done(h - 2, "var"))
                nc.scalar.activation(sq[:, h % 2], y[:, h], ACT.Square).then_inc(*AS.step("square"))

            def deviation(h):
                act.wait_ge(PV.sem, PV.done(h, "var"))
                if h >= 2:
                    act.wait_ge(VN.sem, VN.done(h - 2, "normal"))
                nc.scalar.activation(blocks4(std[:, h % 2]), linear_out(m, 0), ACT.Sqrt, bias=m.eps(2),
                                     scale=1.0 / HD).then_inc(*AD.step("std"))

            def affine(h):
                act.wait_ge(VN.sem, VN.done(h, "normal"))
                nc.scalar.activation(y[:, h], y[:, h], ACT.Identity, scale=m.col(ROWS["lnxg"] + h),
                                     bias=m.col(ROWS["lnxb"] + h)).then_inc(*AF.step("affine"))

            square(0)
            square(1)
            for h in range(4):
                deviation(h)
                if h + 2 < 4:
                    square(h + 2)
                if h:
                    affine(h - 1)
            affine(3)


def turn_rows(m):
    nc, io = m.nc, m.io
    w = m.work
    m.vn = m.arena[:, w:w + 9 * 512].rearrange("p (t c) -> p t c", t=9)
    w += 9 * 512
    m.vd = m.arena[:, w:w + 9 * 128].rearrange("p (t c) -> p t c", t=9)
    w += 9 * 128
    m.wn = m.arena[:, w:w + 72].rearrange("p (t h) -> p t h", t=9)
    w += 72
    m.odd_work = w
    rows = m.arena[:, w:w + 2 * 704].rearrange("p (s c) -> p s c", s=2)
    p = m.p
    P = Steps(nc, "r_pe", ["k", "v", "rest"])
    A = Steps(nc, "r_act", ["k"])
    V = Steps(nc, "r_dve", ["v", "rest"])
    stored = [nc.alloc_semaphore(f"r_stored{s}") for s in range(2)]
    lam_p = nc.alloc_semaphore("lambda_products")
    lam_e = nc.alloc_semaphore("lambda_exps")
    WSCALE = SCALE * 8 ** -0.5
    n_of = lambda t: 128 if t < 8 else TS

    with nc.Block() as block:

        @block.gpsimd
        def _(pool):
            join(m, pool, m.joined)

        @block.tensor
        def _(pe):
            for t in range(9):
                n, c = n_of(t), slice(t * 128, t * 128 + n_of(t))
                if t >= 2:
                    pe.wait_ge(A.sem, A.done(t - 2, "k"))
                    pe.wait_ge(V.sem, V.done(t - 2, "rest"))
                b = 3 * (t % 2)

                def turn(bk, at, tile, k):
                    return nc.tensor.transpose(bank(m, bk)[0:n, at:at + k], p[0:k, tile, c], m.c("ident")[0:k, 0:k])

                for h in range(4):
                    last = turn(b, h * 128, 4 + h, 128)
                last.then_inc(*P.step("k"))
                for h in range(4):
                    last = turn(b + 1, h * 128, 8 + h, 128)
                last.then_inc(*P.step("v"))
                turn(b + 2, 0, 20, 128)
                turn(b + 2, 128, 22, 128)
                turn(b + 2, 256, 21, 64)
                turn(b + 2, 320, 23, 8).then_inc(*P.step("rest"))

        @block.scalar
        def _(act):
            act.wait_ge(lam_p, 2)
            nc.scalar.activation(m.lam[:, 0:2], m.lam[:, 0:2], ACT.Exp).then_inc(lam_e, 1)
            for t in range(9):
                act.wait_ge(P.sem, P.done(t, "k"))
                if t == 0:
                    act.wait_ge(m.joined, 8 + 1)
                if t >= 2:
                    act.wait_ge(stored[t % 2], 16 * 5 * (t // 2))
                nc.scalar.activation(rows[0:n_of(t), t % 2, 0:512], bank(m, 3 * (t % 2))[0:n_of(t), :], ACT.Copy)\
                    .then_inc(*A.step("k"))

        @block.vector
        def _(dve):
            nc.vector.tensor_tensor(m.lam_in[:, 0:4:2, :], m.lam_in[:, 0:4:2, :], m.lam_in[:, 1:4:2, :], ALU.mult)\
                .then_inc(lam_p, 1)
            dve.wait_ge(lam_p, 1)
            nc.vector.tensor_reduce(m.lam[:, 0:2], m.lam_in[:, 0:4:2, :], AX.X, ALU.add).then_inc(lam_p, 1)
            dve.wait_ge(lam_e, 1)
            nc.vector.tensor_tensor(m.lam[:, 2:3], m.lam[:, 0:1], m.lam[:, 1:2], ALU.subtract).then_inc(lam_p, 1)
            dve.wait_ge(lam_p, 3)
            nc.vector.tensor_scalar(m.lam[:, 3:4], m.lam[:, 2:3], LAM_INIT, -1.0, ALU.add, ALU.mult)\
                .then_inc(lam_p, 1)
            for t in range(9):
                n, b = n_of(t), 3 * (t % 2)
                dve.wait_ge(P.sem, P.done(t, "v"))
                nc.vector.tensor_copy(m.vn[0:n, t, :], bank(m, b + 1)[0:n, :]).then_inc(*V.step("v"))
                dve.wait_ge(P.sem, P.done(t, "rest"))
                if t == 0:
                    dve.wait_ge(m.joined, 8 + 1)
                if t >= 2:
                    dve.wait_ge(stored[t % 2], 16 * 5 * (t // 2))
                r = bank(m, b + 2)
                nc.vector.tensor_copy(rows[0:n, t % 2, 512:640], r[0:n, 0:128])
                nc.vector.tensor_copy(m.vd[0:n, t, :], r[0:n, 128:256])
                nc.vector.tensor_copy(rows[0:n, t % 2, 640:704], r[0:n, 256:320])
                nc.vector.tensor_scalar(m.wn[0:n, t, :], r[0:n, 320:328], WSCALE, None, ALU.mult)\
                    .then_inc(*V.step("rest"))

        @block.sync
        def _(sp):
            for t in range(9):
                n = n_of(t)

                def out(name):
                    o = io[name + ("_p" if t < 8 else "_s")][0, 0]
                    if len(o.shape) == 4:
                        o = o.rearrange("s h m d -> s (h m d)")
                    elif len(o.shape) == 3:
                        o = o.rearrange("s h d -> s (h d)")
                    return o[t * 128:t * 128 + n] if t < 8 else o

                sp.wait_ge(A.sem, A.done(t, "k"))
                sp.wait_ge(V.sem, V.done(t, "rest"))
                for name, src in (("c_k", rows[0:n, t % 2, 0:512]), ("c_v", m.vn[0:n, t, :]),
                                  ("d_k", rows[0:n, t % 2, 512:640]), ("d_v", m.vd[0:n, t, :]),
                                  ("d_kidx", rows[0:n, t % 2, 640:704])):
                    sp.dma_start(out(name), src).then_inc(stored[t % 2], 16)
            sp.wait_ge(stored[0], 16 * 5 * 5)
            sp.wait_ge(stored[1], 16 * 5 * 4)


def odd_attention(m):
    nc, io = m.nc, m.io
    w = m.odd_work

    def room(n):
        nonlocal w
        w += n
        assert w <= m.limit, w
        return m.arena[:, w - n:w]

    def narrow(n, dt):
        return room(n // 2).bitcast(dt)

    q = room(256).rearrange("p (h q) -> p h q", h=2)
    q_s = room(128)
    qi = room(1024).rearrange("p (h q) -> p h q", h=8)
    qi_s = room(512).rearrange("p (b q) -> p b q", b=4)
    small = room(128)
    probs = room(LS)
    on = room(1024).rearrange("p (s c) -> p s c", s=2)
    on_d = room(512)
    both = room(128)
    w_s = room(4)
    distP, distS = narrow(TP, F16), narrow(LS, F16)
    slopes = narrow(256, F16).rearrange("p (h c) -> p h c", h=2)
    ident16, corner16 = narrow(128, BF16), narrow(128, BF16)
    penalty = narrow(LS, BF16)
    masks = CONST["strict"][0]
    pt = m.const[:, masks:masks + (NPT + 1) * 128].rearrange("p (t q) -> p t q", t=NPT + 1)
    p = m.p
    spare = p[:, 8:12, :].rearrange("p k t -> p (k t)")
    kt_s = spare[:, 0:LS]
    v_s = spare[:, LS:LS + (NPT + 1) * 128].rearrange("p (t c) -> p t c", t=NPT + 1)
    index = p[:, 22:24, :].rearrange("p k t -> p (k t)")
    cache_rows = m.vn[:, 0:4, :].rearrange("p t c -> p (t c)").rearrange("p (t c) -> p t c", t=NPT)
    relu = probs[:, 0:2048].rearrange("p (s k) -> p s k", s=4)
    low, inv, best, lam_rows = small[:, 0:2], small[:, 8:16], small[:, 16:24], small[:, 24:25]
    total = small[:, 32:48].rearrange("p (s c) -> p s c", s=2)
    top = small[:, 48:50]
    PT_BANK, TURN_BANK, OUT_BANK = 5, 4, 7
    mix = room(128)
    idle = m.om[:, 5:6]

    class Family:

        def __init__(self, name, units):
            self.units, self.rounds = units, 0
            self.V = {h: Steps(nc, f"{name}_dve{h}", ["max", "low"]) for h in units}
            self.N = Steps(nc, f"{name}_norm", ["inv", "lam", "part", "norm"])
            self.Q = {h: Steps(nc, f"{name}_q{h}", ["q"]) for h in units}
            self.E = {h: Steps(nc, f"{name}_exp{h}", ["exp"]) for h in units}
            self.P = {h: Steps(nc, f"{name}_scores{h}", ["scores"]) for h in units}
            self.O = {h: Steps(nc, f"{name}_out{h}", ["out"]) for h in units}

    prompt_family, sample_family = Family("o", (0, 1)), Family("os", (0,))
    turned, moved = nc.alloc_semaphore("probs_turned"), nc.alloc_semaphore("probs_moved")
    topk = nc.alloc_semaphore("topk_steps")
    loaded, fresh = nc.alloc_semaphore("cache_loaded"), nc.alloc_semaphore("cache_fresh")
    index_q, index_made, index_relu, index_read = (
        nc.alloc_semaphore(f"index_{n}") for n in ("queries", "made", "relu", "read"))
    summed, joined = nc.alloc_semaphore("index_summed"), nc.alloc_semaphore("index_joined")
    corner, selected = nc.alloc_semaphore("index_corner"), nc.alloc_semaphore("index_selected")
    rows_made, rows_turned = nc.alloc_semaphore("outputs_turned"), nc.alloc_semaphore("outputs_moved")
    ready = nc.alloc_semaphore("o_ready")
    dist_loaded = nc.alloc_semaphore("dist_loaded")
    free = nc.alloc_semaphore("dist_cast")

    with nc.Block() as block:

        @block.gpsimd
        def _(pool):
            for a in (q.rearrange("p h q -> p (h q)"), q_s, qi.rearrange("p h q -> p (h q)"),
                      qi_s.rearrange("p b q -> p (b q)"), on_d):
                nc.gpsimd.memset(a, 0.0)

        @block.sync
        def _(sp):
            c = io["consts"]
            sp.dma_start(probs[:, 0:TP], c[:, CONST["distP"][0]:CONST["distP"][0] + TP]).then_inc(dist_loaded, 16)
            sp.dma_start(both, c[:, CONST["both"][0]:CONST["both"][0] + 128]).then_inc(dist_loaded, 16)
            sp.dma_start(on[:, 0, 0:128], c[:, CONST["corner"][0]:CONST["corner"][0] + 128]).then_inc(dist_loaded, 16)
            sp.wait_ge(free, 1)
            sp.dma_start(probs, c[:, CONST["distS"][0]:CONST["distS"][0] + LS]).then_inc(dist_loaded, 16)

        @block.vector
        def _(dve):
            dve.wait_ge(dist_loaded, 48)
            nc.vector.tensor_copy(corner16, on[:, 0, 0:128])
            nc.vector.tensor_copy(ident16, m.c("ident"))
            nc.vector.tensor_copy(distP, probs[:, 0:TP]).then_inc(free, 1)
            nc.vector.memset(lam_rows[0:64], 1.0)
            nc.vector.tensor_copy(lam_rows[64:128], m.lam[64:128, 3:4])
            wn = m.wn[0:64, 8, :].rearrange("p (b h) -> p h b", h=2)
            nc.vector.tensor_copy(w_s[0:64], wn[:, 0, :])
            nc.vector.tensor_copy(w_s[64:128], wn[:, 1, :])
            dve.wait_ge(dist_loaded, 64)
            nc.vector.tensor_copy(distS, probs).then_inc(free, 1)

    class Queries:
        pass

    counts = {"turned": 0, "index": 0, "out": 0}

    def count_on(name, n):
        counts[name] += n
        return counts[name] - n

    def extent(t, qt):
        t.qt, t.sample = qt, qt == NQ
        t.n = TS if t.sample else 128
        t.cols = slice(qt * 128, qt * 128 + t.n)
        t.nk = LS if t.sample else (qt + 1) * 128
        t.blocks = [(b, min(512, t.nk - b)) for b in range(0, t.nk, 512)]
        return t

    def queries(qt, kind):
        t = extent(Queries(), qt)
        t.kind = kind
        t.f = sample_family if t.sample else prompt_family
        tiles = -(-t.nk // 128)
        cuts = list(range(0, tiles - 1 if t.sample else tiles, 3 if t.sample else 4)) + [tiles]
        t.groups = list(zip(cuts, cuts[1:]))
        t.penal = kind == "D" and t.nk > TOPK
        t.qtile = 0 if kind == "C" else 12
        t.load = t.sample and kind == "C"
        t.ahead = 4 if t.load else 0
        t.per = len(t.f.units) * len(t.groups) + t.ahead
        assert t.per % 2 == 0
        t.round = t.f.rounds
        t.f.rounds += 4
        t.turned = count_on("turned", 4 * t.per)
        t.number = count_on("out", 1)
        t.selected = qt - 1
        t.topk = None
        return t

    def index_tile(qt):
        t = extent(Queries(), qt)
        heads = 4 if t.sample else 8
        t.pieces = [(s, b, n) for s in range(heads) for b, n in t.blocks]
        t.base = count_on("index", len(t.pieces))
        t.number = qt - 2
        return t

    def flat(ap):
        return ap.rearrange("p a t -> p (a t)")

    def scores(pe, t, i, h):
        r = i + t.round
        if t.sample and isinstance(i, int) and i == 0:
            pe.wait_ge(rows_turned, t.number)
        if t.load:
            turn_cache_tensor(pe, i + 1, i * t.per + t.turned)
        if t.penal:
            pe.wait_ge(selected, t.selected)
        pe.wait_ge(t.f.Q[h].sem, t.f.Q[h].done(r, "q"))
        first = 0 if t.sample else TP - 128 - t.qt * 128
        dist = (distS if t.sample else distP)[:, first:first + t.nk]
        keys = kt_s if t.sample else flat(p[:, ds(i + 4, 1), :]) if t.kind == "C" else p[:, 20, :]
        for b, n in t.blocks:
            out = m.ps[:, h * 1024 + b:h * 1024 + b + n]
            edge = not t.sample and b + n == t.nk
            nc.tensor.matmul(out, q_s if t.sample else q[:, h, :], keys[:, b:b + n], start=True, stop=False)
            last = nc.tensor.matmul(out, slopes[:, h, :], dist[:, b:b + n], start=False,
                                    stop=not (edge or t.penal))
            if t.penal:
                last = nc.tensor.matmul(out, ident16, penalty[:, b:b + n], start=False, stop=not edge)
            if edge:
                last = nc.tensor.matmul(out[:, n - 128:n], ident16, corner16, start=False, stop=True)
        last.then_inc(*t.f.P[h].step("scores"))

    def groups_of(t, h):
        return [(t.ahead + t.f.units.index(h) * len(t.groups) + j, a, z) for j, (a, z) in enumerate(t.groups)]

    def key_rows(t, kt):
        return min(128, t.nk - kt * 128)

    def bank_of(t, local, i):
        return PT_BANK + (t.turned + local) % 2

    def turn_group(pe, t, i, h, local, a, z):
        if t.turned + local >= 2 or not isinstance(i, int):
            pe.wait_ge(moved, i * t.per + (t.turned + local - 1))
        elif i:
            pe.wait_ge(moved, i * t.per + (t.turned + local - 1))
        for kt in range(a, z):
            k = key_rows(t, kt)
            last = nc.tensor.transpose(
                bank(m, bank_of(t, local, i))[0:k, (kt - a) * 128:(kt - a) * 128 + 128],
                probs[:, h * TP + kt * 128:h * TP + kt * 128 + k], m.c("ident"))
        last.then_inc(turned, 1)

    def value_group(pe, t, i, h, local, a, z):
        pe.wait_ge(moved, i * t.per + (t.turned + local + 1))
        at, width = (0, 128) if t.sample else (h * 128, 128) if t.kind == "C" else (h * 64, 64)
        for kt in range(a, z):
            k = key_rows(t, kt)
            if t.sample:
                v = v_s[0:k, kt, :]
            elif t.kind == "C":
                v = m.vn[0:k, kt, ds(i * 128, 128)]
            else:
                v = m.vd[0:k, kt, 64 * h:64 * h + 64]
            last = nc.tensor.matmul(bank(m, OUT_BANK)[:, at:at + width], pt[0:k, h * 8 + kt, :], v,
                                    start=(kt == 0), stop=(kt == t.groups[-1][1] - 1))
        return last

    def unit_tensor(pe, t, i, h, after):
        r = i + t.round
        pe.wait_ge(t.f.E[h].sem, t.f.E[h].done(r, "exp"))
        groups = groups_of(t, h)
        for local, a, z in groups[:2]:
            turn_group(pe, t, i, h, local, a, z)
        if after and h in after[0].f.units and not after[0].load:
            scores(pe, *after, h)
        if h == 0 and not (isinstance(i, int) and r == 0):
            pe.wait_ge(t.f.N.sem, t.f.N.rounds(r))
        for n, g in enumerate(groups):
            last = value_group(pe, t, i, h, *g)
            if n + 2 < len(groups):
                turn_group(pe, t, i, h, *groups[n + 2])
        last.then_inc(*t.f.O[h].step("out"))
        if after and h in after[0].f.units and after[0].load:
            scores(pe, *after, h)

    def take_wait(i, n):
        if not isinstance(i, int):
            nc.scalar.activation(m.om[:, n:n + 1], m.om[:, n:n + 1], ACT.Copy)

    def load_queries(act, t, i, h):
        r = i + t.round
        if not (isinstance(i, int) and r == 0):
            act.wait_ge(t.f.P[h].sem, t.f.P[h].rounds(r))
            take_wait(i, 6 + h)
        src = flat(p[:, ds(i + t.qtile, 1), t.cols])
        if t.sample:
            for half in (slice(0, 64), slice(64, 128)):
                nc.scalar.activation(q_s[half, half], src[half], ACT.Copy, scale=SCALE)
        else:
            half = slice(64 * h, 64 * h + 64)
            nc.scalar.activation(q[half, h, :], src[half], ACT.Copy, scale=SCALE)
        if t.kind == "C":
            last = nc.scalar.activation(slopes[:, h, :], m.c("ident"), ACT.Copy, scale=m.c("slopeC")[:, ds(i, 1)])
        elif t.sample:
            for g, half in enumerate((slice(0, 64), slice(64, 128))):
                last = nc.scalar.activation(slopes[half, h, :], m.c("ident")[half], ACT.Copy,
                                            scale=m.c("slopeD")[half, ds(i + 4 * g, 1)])
        else:
            last = nc.scalar.activation(slopes[:, h, :], m.c("ident"), ACT.Copy,
                                        scale=m.c("slopeD")[:, ds(i + 4 * h, 1)])
        last.then_inc(*t.f.Q[h].step("q"))

    def exponentials(act, t, i, h):
        r = i + t.round
        act.wait_ge(t.f.V[h].sem, t.f.V[h].done(r, "low"))
        take_wait(i, 4 + h)
        nc.scalar.activation(probs[:, h * TP:h * TP + t.nk], m.ps[:, h * 1024:h * 1024 + t.nk], ACT.Exp,
                             bias=low[:, h:h + 1], accum_out=total[:, t.number % 2, ds(i * 2 + h, 1)])\
            .then_inc(*t.f.E[h].step("exp"))

    def move_group(act, t, i, h, local, a, z):
        act.wait_ge(turned, i * t.per + (t.turned + local + 1))
        full = min(z, t.nk // 128)
        src = bank(m, bank_of(t, local, i)).rearrange("p (t q) -> p t q", t=4)
        if full > a:
            last = nc.scalar.activation(pt[:, h * 8 + a:h * 8 + full, :], src[:, 0:full - a, :], ACT.Copy)
        if full < z:
            last = nc.scalar.activation(pt[0:TS, full:z, :], src[0:TS, full - a:z - a, :], ACT.Copy)
        last.then_inc(moved, 1)

    def maximum(dve, t, i, h):
        r = i + t.round
        dve.wait_ge(t.f.P[h].sem, t.f.P[h].done(r, "scores"))
        nc.vector.tensor_reduce(top[:, h:h + 1], m.ps[:, h * 1024:h * 1024 + t.nk], AX.X, ALU.max)\
            .then_inc(*t.f.V[h].step("max"))
        dve.wait_ge(t.f.V[h].sem, t.f.V[h].done(r, "max"))
        nc.vector.tensor_scalar(low[:, h:h + 1], top[:, h:h + 1], -1.0, None, ALU.mult)\
            .then_inc(*t.f.V[h].step("low"))

    def normalise(dve, t, i):
        r = i + t.round
        N, last = t.f.N, t.f.units[-1]
        n = len(t.f.units)
        if not (isinstance(i, int) and r == 0):
            dve.wait_ge(N.sem, N.rounds(r))
        dve.wait_ge(t.f.E[last].sem, t.f.E[last].done(r, "exp"))
        if not isinstance(i, int):
            nc.vector.memset(small[:, 121:122], 0.0)
        nc.vector.reciprocal(inv[:, 0:n], total[:, t.number % 2, ds(i * 2, n)]).then_inc(*N.step("inv"))
        dve.wait_ge(N.sem, N.done(r, "inv"))
        scale = lam_rows if t.sample and t.kind == "C" else m.lam[:, 3:4] if t.kind == "C" else None
        if scale is None:
            nc.vector.memset(small[:, 120:121], 0.0).then_inc(*N.step("lam"))
        else:
            nc.vector.tensor_scalar(inv[:, 2:3], inv[:, n - 1:n], scale, None, ALU.mult).then_inc(*N.step("lam"))
        dve.wait_ge(N.sem, N.done(r, "lam"))
        dve.wait_ge(t.f.O[last].sem, t.f.O[last].done(r, "out"))
        o, dst = bank(m, OUT_BANK), on[:, t.number % 2, :]

        def scaled(out, src, by):
            return nc.vector.tensor_scalar(out, src, by, None, ALU.mult)

        if t.kind == "C" and t.sample:
            nc.vector.memset(small[:, 120:121], 0.0).then_inc(*N.step("part"))
            scaled(dst[:, ds(i * 128, 128)], o[:, 0:128], inv[:, 2:3]).then_inc(*N.step("norm"))
        elif t.kind == "C":
            nc.vector.tensor_scalar(mix, o[:, 0:128], inv[:, 0:1], None, ALU.mult).then_inc(*N.step("part"))
            dve.wait_ge(N.sem, N.done(r, "part"))
            nc.vector.scalar_tensor_tensor(out=dst[:, ds(i * 128, 128)], in0=o[:, 128:256], scalar=inv[:, 2:3],
                                           in1=mix, op0=ALU.mult, op1=ALU.add).then_inc(*N.step("norm"))
        elif t.sample:
            scaled(on_d[0:64, ds(i * 128, 64)], o[0:64, 0:64], inv[0:64, 0:1]).then_inc(*N.step("part"))
            scaled(on_d[64:128, ds(i * 128 + 64, 64)], o[64:128, 64:128], inv[64:128, 0:1]).then_inc(*N.step("norm"))
        else:
            scaled(dst[:, ds(i * 128, 64)], o[:, 0:64], inv[:, 0:1]).then_inc(*N.step("part"))
            scaled(dst[:, ds(i * 128 + 64, 64)], o[:, 64:128], inv[:, 1:2]).then_inc(*N.step("norm"))

    def turn_outputs(pe, t):
        pe.wait_ge(t.f.N.sem, t.f.N.rounds(t.round + 4))
        if t.number:
            pe.wait_ge(rows_turned, t.number)
        src = on_d if t.sample and t.kind == "D" else on[:, t.number % 2, :]
        for a in range(4):
            out = bank(m, TURN_BANK)
            if t.sample:
                last = nc.tensor.matmul(out[:, a * 128:a * 128 + 64], src[:, a * 128:a * 128 + 128], both[:, 0:64],
                                        start=True, stop=True)
            else:
                last = nc.tensor.transpose(out[:, a * 128:a * 128 + 128], src[:, a * 128:a * 128 + 128],
                                           m.c("ident"))
        last.then_inc(rows_made, 1)

    def move_outputs(act, t):
        act.wait_ge(rows_made, t.number + 1)
        src = heads4(bank(m, TURN_BANK))[:, :, 0:t.n]
        nc.scalar.activation(p[:, t.qtile:t.qtile + 4, t.cols], src, ACT.Copy).then_inc(rows_turned, 1)

    def turn_cache_tensor(pe, n, at):
        pe.wait_ge(loaded, n * 32 + 32)
        for j in range(4):
            pe.wait_ge(moved, at + (j - 1))
            for kt in range(4):
                last = nc.tensor.transpose(bank(m, PT_BANK + j % 2)[:, kt * 128:kt * 128 + 128],
                                           cache_rows[:, 4 * j + kt, :], m.c("ident"))
            last.then_inc(turned, 1)
        pe.wait_ge(fresh, n + 1)

    def turn_cache_scalar(act, i, at, kind):
        for j in range(4):
            act.wait_ge(turned, at + (j + 1))
            nc.scalar.activation(kt_s[:, 512 * j:512 * j + 512], bank(m, PT_BANK + j % 2), ACT.Copy)\
                .then_inc(moved, 1)
        if kind == "C":
            new_k, new_v = flat(p[:, ds(i + 4, 1), TP:T]), m.vn[0:TS, 8, ds(i * 128, 128)]
        else:
            new_k, new_v = p[:, 21 if kind == "I" else 20, TP:T], m.vd[0:TS, 8, :]
        if kind != "I":
            nc.scalar.activation(v_s[0:TS, NPT, :], new_v, ACT.Copy)
        nc.scalar.activation(kt_s[:, PAST:LS], new_k, ACT.Copy).then_inc(fresh, 1)

    def index_tensor(pe, t):
        pe.wait_ge(index_q, t.number + 1)
        keys, queries_i = (kt_s, qi_s) if t.sample else (p[:, 21, :], qi)
        for c, (s, b, n) in enumerate(t.pieces):
            if c >= 4:
                pe.wait_ge(index_relu, t.base + c - 3)
            nc.tensor.matmul(bank(m, c % 4)[:, 0:n], queries_i[:, s, :], keys[:, b:b + n],
                             start=True, stop=True).then_inc(index_made, 1)
        pe.wait_ge(index_relu, t.base + len(t.pieces))
        if t.sample:
            pe.wait_ge(rows_turned, 2 * NQ - 1)
            pe.wait_ge(index_read, t.base + len(t.pieces))
            for c, (b, n) in enumerate(t.blocks):
                nc.tensor.matmul(m.ps[:, b:b + n], both, index[:, b:b + n], start=True, stop=True)\
                    .then_inc(summed, 1)
            pe.wait_ge(joined, len(t.blocks))

    def index_scalar(act, t):
        if t.sample:
            for h, half in enumerate((slice(0, 64), slice(64, 128))):
                last = nc.scalar.activation(qi_s[half, :, half], p[half, 16:20, t.cols], ACT.Copy)
        else:
            if t.number:
                act.wait_ge(index_made, t.base)
            nc.scalar.activation(qi[0:64, 0:4, 0:t.n], p[0:64, 16:20, t.cols], ACT.Copy)
            last = nc.scalar.activation(qi[64:128, 4:8, 0:t.n], p[64:128, 16:20, t.cols], ACT.Copy)
        last.then_inc(index_q, 1)
        for c, (s, b, n) in enumerate(t.pieces):
            act.wait_ge(index_made, t.base + c + 1)
            if t.base + c >= 4:
                act.wait_ge(index_read, t.base + c - 3)
            nc.scalar.activation(relu[:, c % 4, 0:n], bank(m, c % 4)[:, 0:n], ACT.Relu).then_inc(index_relu, 1)

    def index_vector(dve, t):
        blocks = len(t.blocks)
        for c, (s, b, n) in enumerate(t.pieces):
            dve.wait_ge(index_relu, t.base + c + 1)
            head = 2 * (s % 4) + s // 4
            wt = w_s[:, s:s + 1] if t.sample else m.wn[:, t.qt, head:head + 1]
            if s == 0:
                nc.vector.tensor_scalar(index[:, b:b + n], relu[:, c % 4, 0:n], wt, None, ALU.mult)\
                    .then_inc(index_read, 1)
            else:
                dve.wait_ge(index_read, t.base + c + 1 - blocks)
                nc.vector.scalar_tensor_tensor(out=index[:, b:b + n], in0=relu[:, c % 4, 0:n], scalar=wt,
                                               in1=index[:, b:b + n], op0=ALU.mult, op1=ALU.add)\
                    .then_inc(index_read, 1)
        dve.wait_ge(index_read, t.base + len(t.pieces))
        if t.sample:
            for c, (b, n) in enumerate(t.blocks):
                dve.wait_ge(summed, c + 1)
                nc.vector.tensor_copy(index[:, b:b + n], m.ps[:, b:b + n]).then_inc(joined, 1)
            dve.wait_ge(joined, blocks)
        else:
            nc.vector.memset(index[0:64, t.nk - 64:t.nk], -FAR).then_inc(corner, 1)
            dve.wait_ge(corner, t.number + 1)

    EACH = TOPK // 8 // 8

    def select(dve, t, done, i, steps):
        for k in steps:
            at = i * (2 * EACH) + (done + 2 * k)
            nc.vector.max(best, index[:, 0:t.nk]).then_inc(topk, 1)
            dve.wait_ge(topk, at + 1)
            if not isinstance(i, int):
                nc.vector.memset(small[:, 122:123], 0.0)
            nc.vector.match_replace(index[:, 0:t.nk], best, index[:, 0:t.nk], TAKEN).then_inc(topk, 1)
            dve.wait_ge(topk, at + 2)
            if not isinstance(i, int):
                nc.vector.memset(small[:, 123:124], 0.0)

    def make_penalty(dve, t):
        nc.vector.tensor_scalar(penalty[:, 0:t.nk], index[:, 0:t.nk], TAKEN / 2, -FAR, ALU.is_gt, ALU.mult)\
            .then_inc(selected, 1)
        dve.wait_ge(selected, t.number + 1)

    runs = [(None, [queries(0, "C"), queries(0, "D"), queries(1, "C")])]
    for qt in range(2, NQ + 1):
        if qt == NQ:
            cache_index = ("I", 0, count_on("turned", 4))
        t = index_tile(qt)
        run = [queries(qt - 1, "D")]
        if qt < NQ:
            run.append(queries(qt, "C"))
            run[1].topk = t
        run[0].topk = t
        runs.append((t, run))
    sample_c = queries(NQ, "C")
    sample_c.topk = runs[-1][0]
    runs.append((None, [sample_c]))
    cache_d = ("D", 5, count_on("turned", 4))
    sample_d = queries(NQ, "D")
    runs.append(("cache", [sample_d]))
    sample_index = runs[-3][0]
    for n, t in enumerate(x for _, run in runs for x in run):
        t.done = 0
    for t, run in runs:
        for x in run:
            if x.topk:
                x.done = (x.topk.number * 8 + (4 if x.kind == "C" else 0)) * 2 * EACH

    def each_round(engine, run, body):
        for n, t in enumerate(run):
            start = 0
            if t.round == 0:
                body(t, 0, (t, 1))
                start = 1
            with engine.Fori(start, 3) as i:
                body(t, i, (t, i + 1))
            body(t, 3, (run[n + 1], 0) if n + 1 < len(run) else None)
            yield t

    with nc.Block() as block:

        @block.tensor
        def _(pe):
            for before, run in runs:
                if before == "cache":
                    turn_cache_tensor(pe, cache_d[1], cache_d[2])
                elif before:
                    if before.sample:
                        turn_cache_tensor(pe, cache_index[1], cache_index[2])
                    index_tensor(pe, before)
                for h in run[0].f.units:
                    scores(pe, run[0], 0, h)

                def body(t, i, after):
                    for h in t.f.units:
                        unit_tensor(pe, t, i, h, after)

                for t in each_round(pe, run, body):
                    turn_outputs(pe, t)

        @block.scalar
        def _(act):
            for before, run in runs:
                if before == "cache":
                    turn_cache_scalar(act, None, cache_d[2], "D")
                elif before:
                    if before.sample:
                        turn_cache_scalar(act, None, cache_index[2], "I")
                    index_scalar(act, before)
                if run[0].load:
                    turn_cache_scalar(act, 0, run[0].turned, "C")
                for h in run[0].f.units:
                    load_queries(act, run[0], 0, h)
                exponentials(act, run[0], 0, 0)

                def body(t, i, after):
                    for h in t.f.units:
                        if after and not after[0].load:
                            load_queries(act, *after, h)
                        for g in groups_of(t, h):
                            move_group(act, t, i, h, *g)
                        if h + 1 in t.f.units:
                            exponentials(act, t, i, h + 1)
                    if after and after[0].load:
                        act.wait_ge(t.f.P[0].sem, t.f.P[0].rounds(t.round + 1) + i)
                        act.wait_ge(t.f.O[0].sem, t.f.O[0].rounds(t.round + 1) + i)
                        turn_cache_scalar(act, after[1], after[1] * after[0].per + after[0].turned, "C")
                        load_queries(act, *after, 0)
                    if after:
                        exponentials(act, *after, 0)

                for t in each_round(act, run, body):
                    move_outputs(act, t)

        @block.vector
        def _(dve):
            for before, run in runs:
                if before and before != "cache":
                    if before.number:
                        make_penalty(dve, runs[before.number][0])
                    index_vector(dve, before)
                elif before == "cache":
                    make_penalty(dve, sample_index)
                maximum(dve, run[0], 0, 0)

                def body(t, i, after):
                    steps = range(EACH if t.topk else 0)
                    early = steps[:-1] if len(t.f.units) > 1 else steps[:0]
                    for h in t.f.units[1:]:
                        maximum(dve, t, i, h)
                    select(dve, t.topk, t.done, i, early)
                    if after:
                        maximum(dve, *after, 0)
                    normalise(dve, t, i)
                    select(dve, t.topk, t.done, i, steps[len(early):])

                for t in each_round(dve, run, body):
                    pass

        @block.sync
        def _(sp):
            ck = io["cache_c_k"][0, 0].rearrange("(t p) h m d -> p t (h m d)", p=128)
            cv = io["cache_c_v"][0, 0].rearrange("(t p) h e -> p t (h e)", p=128)
            f, g = prompt_family, sample_family
            last_c = [t for _, run in runs for t in run if t.kind == "C" and not t.sample][-1]
            sp.wait_ge(f.O[1].sem, f.O[1].rounds(last_c.round + 4))
            ki = io["cache_d_kidx"][0, 0].rearrange("(t p) d -> p t d", p=128)
            for h in range(2):
                sp.dma_start(cache_rows[:, :, 64 * h:64 * h + 64], ki).then_inc(loaded, 16)
            sp.wait_ge(index_made, sample_index.base + len(sample_index.pieces))
            sp.dma_start(cache_rows, ck[:, :, 0:128]).then_inc(loaded, 16)
            sp.dma_start(v_s[:, 0:NPT, :], cv[:, :, 0:128]).then_inc(loaded, 16)
            with sp.Fori(1, 4) as i:
                sp.wait_ge(g.P[0].sem, i)
                sp.dma_start(cache_rows, ck[:, :, ds(i * 128, 128)]).then_inc(loaded, 16)
                sp.wait_ge(g.O[0].sem, i)
                sp.dma_start(v_s[:, 0:NPT, :], cv[:, :, ds(i * 128, 128)]).then_inc(loaded, 16)
            sp.wait_ge(g.P[0].sem, 4)
            sp.dma_start(cache_rows, io["cache_d_k"][0, 0].rearrange("(t p) g d -> p t (g d)", p=128))\
              .then_inc(loaded, 16)
            sp.wait_ge(g.O[0].sem, 4)
            sp.dma_start(v_s[:, 0:NPT, :], io["cache_d_v"][0, 0].rearrange("(t p) g d -> p t (g d)", p=128))\
              .then_inc(loaded, 16)


def diff_finish(m):
    nc = m.nc
    w = m.odd_work
    sq, rstd = (m.arena[:, w + n * T:w + n * T + T] for n in range(2))
    gain = m.arena[:, w + 2 * T:w + 2 * T + 129]
    ones = gain[:, 1:129]
    P, V, A = Steps(nc, "f_pe", ["sum"]), Steps(nc, "f_dve", ["rstd", "normal"]), Steps(nc, "f_act", ["sq", "std"])
    ready = nc.alloc_semaphore("f_ready")
    with nc.Block() as block:

        @block.tensor
        def _(pe):
            pe.wait_ge(ready, 1)
            for h in range(4):
                pe.wait_ge(A.sem, A.done(h, "sq"))
                for b in range(4):
                    last = nc.tensor.matmul(m.ps[:, b * 512:b * 512 + TB], ones, sq[:, b * TB:(b + 1) * TB],
                                            start=True, stop=True)
                last.then_inc(*P.step("sum"))

        @block.scalar
        def _(act):
            for h in range(4):
                nc.scalar.activation(sq, m.p[:, h, :], ACT.Square).then_inc(*A.step("sq"))
                act.wait_ge(P.sem, P.done(h, "sum"))
                if h:
                    act.wait_ge(V.sem, V.done(h - 1, "normal"))
                nc.scalar.activation(blocks4(rstd), linear_out(m, 0), ACT.Sqrt, bias=m.eps(0)).then_inc(*A.step("std"))

        @block.vector
        def _(dve):
            nc.vector.memset(ones, 1.0 / 128)
            nc.vector.tensor_scalar(gain[:, 0:1], m.col(ROWS["subln"]), 1.0 - LAM_INIT, None, ALU.mult)\
                .then_inc(ready, 1)
            dve.wait_ge(ready, 1)
            for h in range(4):
                dve.wait_ge(A.sem, A.done(h, "std"))
                nc.vector.reciprocal(rstd, rstd).then_inc(*V.step("rstd"))
                dve.wait_ge(V.sem, V.done(h, "rstd"))
                nc.vector.scalar_tensor_tensor(out=m.p[:, h, :], in0=m.p[:, h, :], scalar=gain[:, 0:1], in1=rstd,
                                               op0=ALU.mult, op1=ALU.mult).then_inc(*V.step("normal"))


def store(m):
    nc, io = m.nc, m.io
    rows = m.arena[:, m.work:m.work + 2 * D].rearrange("p (s d) -> p s d", s=2)
    turned, moved = nc.alloc_semaphore("y_turned"), nc.alloc_semaphore("y_moved")
    stored = [nc.alloc_semaphore(f"y_stored{s}") for s in range(2)]
    with nc.Block() as block:

        @block.tensor
        def _(pe):
            for t in range(9):
                n = 128 if t < 8 else TS
                if t >= 2:
                    pe.wait_ge(moved, t - 1)
                for k in range(8):
                    at = (t % 2) * 1024 + k * 128
                    last = nc.tensor.transpose(m.ps[0:n, at:at + 128], m.x[:, k, t * 128:t * 128 + n], m.c("ident"))
                last.then_inc(turned, 1)

        @block.vector
        def _(dve):
            for t in range(9):
                n = 128 if t < 8 else TS
                dve.wait_ge(turned, t + 1)
                if t >= 2:
                    dve.wait_ge(stored[t % 2], 16 * (t // 2))
                nc.vector.tensor_copy(rows[0:n, t % 2, :], m.ps[0:n, (t % 2) * 1024:(t % 2) * 1024 + 1024])\
                    .then_inc(moved, 1)

        @block.sync
        def _(sp):
            for t in range(9):
                sp.wait_ge(moved, t + 1)
                out = io["y_prompt"][0, t * 128:t * 128 + 128] if t < 8 else io["y_sample"][0]
                sp.dma_start(out, rows[0:128 if t < 8 else TS, t % 2, :]).then_inc(stored[t % 2], 16)
            sp.wait_ge(stored[0], 16 * 5)
            sp.wait_ge(stored[1], 16 * 4)


def build(nc, io):
    io["x_kept"] = nc.dram_tensor("x_kept", (128, KD * T), F32, kind="Internal").ap()
    m = Core()
    m.nc, m.io = nc, io
    columns = 53200
    m.arena_at = (nc.sbuf_base + 31) // 32 * 32
    m.arena = nc.alloc_sbuf_tensor("arena", [128, columns], F32)
    m.rounded = {}
    m.ps = nc.alloc_psum_tensor("psum", [128, 4096], F32)
    at = [0]

    def room(n):
        at[0] += n
        return m.arena[:, at[0] - n:at[0]]

    m.nconst = CONST["distP"][0]
    m.const = room(m.nconst)
    m.cols = room(128)
    m.sink = room(8)
    m.lam_in = room(256).rearrange("p (v d) -> p v d", v=4)
    m.lam = room(8)
    m.om = room(8)
    m.c = lambda name: m.const[:, CONST[name][0]:CONST[name][0] + CONST[name][1]]
    m.eps = lambda n: m.c("eps")[:, n:n + 1]
    m.col = lambda n: m.cols[:, n:n + 1]
    m.linears = Ring(m)
    m.joined = nc.alloc_semaphore("x_joined")
    m.tile_summed, m.tiles_summed = nc.alloc_semaphore("tile_summed"), 0
    m.mlp_sems = [nc.alloc_semaphore(f"mlp_{n}")
                  for n in ("relu", "added", "squared", "hidden_high", "hidden_split", "scaled")]
    room(-at[0] % 8)
    m.x_at = at[0]
    m.x = room(KD * T).rearrange("p (k t) -> p k t", k=KD)
    after_x = at[0]
    m.limit = columns
    m.work = after_x
    start(m)

    m.p = m.arena[:, after_x:after_x + 21 * T].rearrange("p (k t) -> p k t", k=21)
    m.work = after_x + 21 * T
    m.ring, m.high = m.work, m.arena[:, columns - 8 * T:columns]
    assert m.ring + RING <= columns - 8 * T
    project_even(m)
    window_attention(m)
    m.state = m.arena[:, m.work:m.work + 512]
    m.work += 512
    rwkv_prepare(m)
    rwkv_chunks(m)
    rwkv_finish(m)
    m.ring = m.work
    project_out(m, "out0", io["w_out_even"][0], lambda k: m.p[:, k, :], 0)
    layer_norm(m, "ln0", ROWS["mixg"], ROWS["mixb"])
    m.work = after_x
    mlp(m, 0)
    m.work += 8 * T
    layer_norm(m, "ln1", ROWS["ffng"], ROWS["ffnb"], m.acc)
    m.p = m.arena[:, after_x:after_x + 24 * T].rearrange("p (k t) -> p k t", k=24)
    m.work = after_x + 24 * T
    m.ring = m.work
    assert m.ring + RING <= columns - 8 * T
    project_odd(m)
    turn_rows(m)
    odd_attention(m)
    diff_finish(m)
    m.ring = m.work
    project_out(m, "out1", io["w_out_odd"][0], lambda k: m.p[:, k if k < 4 else 8 + k, :], 4)
    layer_norm(m, "ln2", ROWS["mixg"] + 8, ROWS["mixb"] + 8)
    m.work = after_x
    mlp(m, 1)
    m.work += 8 * T
    layer_norm(m, "ln3", ROWS["ffng"] + 8, ROWS["ffnb"] + 8, m.acc)
    store(m)


_INS = ["x_prompt", "x_sample", "cache_a_k", "cache_a_v", "state_b_shift", "state_b_wkv", "cache_c_k", "cache_c_v",
        "cache_d_k", "cache_d_v", "cache_d_kidx", "w_in_even", "sink_a", "mu_b", "w0_b", "w_up_b", "a0_b", "a_up_b",
        "g_up_b", "k_k_b", "k_a_b", "r_k_b", "lnx_g_b", "lnx_b_b", "w_out_even", "w_in_odd", "lam_q1_c", "lam_k1_c",
        "lam_q2_c", "lam_k2_c", "subln_g_c", "w_out_odd", "ln_mix_g", "ln_mix_b", "ln_ffn_g", "ln_ffn_b",
        "w_ff_up", "w_ff_down"]
_OUTS = [("y_prompt", (1, TP, D)), ("y_sample", (1, TS, D)),
         ("a_k_p", (1, 1, 128, 2, HD)), ("a_v_p", (1, 1, 128, 2, HD)), ("b_shift_p", (1, 1, 1, 1792)),
         ("b_wkv_p", (1, 1, 8, HD, HD)), ("c_k_p", (1, 1, TP, 4, 2, HD)), ("c_v_p", (1, 1, TP, 4, 128)),
         ("d_k_p", (1, 1, TP, 2, HD)), ("d_v_p", (1, 1, TP, 2, HD)), ("d_kidx_p", (1, 1, TP, HD)),
         ("a_k_s", (1, 1, 128, 2, HD)), ("a_v_s", (1, 1, 128, 2, HD)), ("b_shift_s", (1, 1, 1, 1792)),
         ("b_wkv_s", (1, 1, 8, HD, HD)), ("c_k_s", (1, 1, TS, 4, 2, HD)), ("c_v_s", (1, 1, TS, 4, 128)),
         ("d_k_s", (1, 1, TS, 2, HD)), ("d_v_s", (1, 1, TS, 2, HD)), ("d_kidx_s", (1, 1, TS, HD))]


def kernel(**inputs):
    import concourse.bacc as _bacc
    from concourse.bass_utils import run_bass_kernel_spmd as _run

    nc = _bacc.Bacc("TRN2", target_bir_lowering=False, num_devices=1)
    arrays, io = {}, {}
    for name in _INS:
        a = np.ascontiguousarray(inputs[name])
        arrays[f"in_{name}"] = a
        io[name] = nc.dram_tensor(f"in_{name}", a.shape, F32, kind="ExternalInput").ap()
    arrays["in_consts"] = constants()
    io["consts"] = nc.dram_tensor("in_consts", (128, NCONST), F32, kind="ExternalInput").ap()
    for name, shape in _OUTS:
        io[name] = nc.dram_tensor(f"out_{name}", shape, F32, kind="ExternalOutput").ap()
    build(nc, io)
    r = _run(nc, [arrays], core_ids=[0])
    return tuple(r.results[0][f"out_{name}"] for name, _ in _OUTS)
```
